# Optimizing a Trainium2 kernel written in Bass

```python
import jax, jax.numpy as jnp
from jax import lax
import numpy as np

D_MODEL = 2048
BATCH = 1
SEQ = 256
DEPTH = 1

CHUNK = 64
HEAD_DIM = 128
N_HEADS_A = 8
N_HEADS_B = 8
WIDTH_A = N_HEADS_A * HEAD_DIM
WIDTH_B = N_HEADS_B * HEAD_DIM
MIX_WIDTH = WIDTH_A + WIDTH_B
LEFT_CHUNKS = 8
BAND = (LEFT_CHUNKS + 1) * CHUNK
MAX_REL = 128
IDX_HEADS = 16
IDX_DIM = 64
TOPK_MAX = 256
Q_BLOCK = 128
ROPE_THETA = 500000.0
ROPE_FRACTION = 4
PEER_HEADS = 8
PEER_KEYS = 128
PEER_EXPERTS = PEER_KEYS * PEER_KEYS
PEER_QDIM = 256
PEER_TOPK = 16
PEER_BLOCK = 128
PLE_DIM = 256
IN_PROJ_WIDTH = 3 * WIDTH_A + 3 * WIDTH_B + IDX_HEADS * IDX_DIM + IDX_DIM + IDX_HEADS
EPS = 1e-6

kernel_name = "hybrid_chunk_relpos_dsa_peer_block"

def rms_norm(x, g):
    xf = x.astype(jnp.float32)
    y = xf * lax.rsqrt(jnp.mean(xf * xf, axis=-1, keepdims=True) + EPS)
    return (y * g.astype(jnp.float32)).astype(x.dtype)

def partial_rope(x, pos):
    rot = x.shape[-1] // ROPE_FRACTION
    half = rot // 2
    inv_freq = 1.0 / (ROPE_THETA ** (jnp.arange(half, dtype=jnp.float32) / half))
    ang = pos.astype(jnp.float32)[..., None] * inv_freq
    cos = jnp.cos(ang)[:, :, None, :]
    sin = jnp.sin(ang)[:, :, None, :]
    x1 = x[..., :half].astype(jnp.float32)
    x2 = x[..., half:rot].astype(jnp.float32)
    r1 = (x1 * cos - x2 * sin).astype(x.dtype)
    r2 = (x2 * cos + x1 * sin).astype(x.dtype)
    return jnp.concatenate([r1, r2, x[..., rot:]], axis=-1)

def split_offsets():
    sizes = (WIDTH_A, WIDTH_A, WIDTH_A, WIDTH_B, WIDTH_B, WIDTH_B,
             IDX_HEADS * IDX_DIM, IDX_DIM, IDX_HEADS)
    offs = []
    acc = 0
    for s in sizes[:-1]:
        acc += s
        offs.append(acc)
    return offs

def chunked_relpos_attention(q, k, v, rel_bias):
    B, S, H, d = q.shape
    nc = S // CHUNK
    qc = q.reshape(B, nc, CHUNK, H, d)
    pad = ((0, 0), (LEFT_CHUNKS * CHUNK, 0), (0, 0), (0, 0))
    kp = jnp.pad(k, pad).reshape(B, nc + LEFT_CHUNKS, CHUNK, H, d)
    vp = jnp.pad(v, pad).reshape(B, nc + LEFT_CHUNKS, CHUNK, H, d)
    band_idx = jnp.arange(nc)[:, None] + jnp.arange(LEFT_CHUNKS + 1)[None, :]
    kb = kp[:, band_idx].reshape(B, nc, BAND, H, d)
    vb = vp[:, band_idx].reshape(B, nc, BAND, H, d)
    s = jnp.einsum('bcqhd,bckhd->bhcqk', qc, kb, preferred_element_type=jnp.float32) * (d ** -0.5)
    dist = jnp.arange(CHUNK)[:, None] + LEFT_CHUNKS * CHUNK - jnp.arange(BAND)[None, :]
    dist = jnp.clip(dist, -MAX_REL, MAX_REL) + MAX_REL
    bias = rel_bias[:, dist].astype(jnp.float32)
    key_chunk = jnp.arange(nc)[:, None] - LEFT_CHUNKS + jnp.arange(LEFT_CHUNKS + 1)[None, :]
    valid = jnp.repeat(key_chunk >= 0, CHUNK, axis=1)
    s = s + bias[None, :, None]
    s = jnp.where(valid[None, None, :, None, :], s, -jnp.inf)
    pr = jax.nn.softmax(s, axis=-1)
    o = jnp.einsum('bhcqk,bckhd->bcqhd', pr.astype(vb.dtype), vb)
    return o.reshape(B, S, H * d)

def dsa_attention(q, k, v, q_idx, k_idx, w_idx):
    B, S, H, d = q.shape
    topk = min(TOPK_MAX, S // 4)
    nb = S // Q_BLOCK
    key_chunk = jnp.arange(S) // CHUNK

    def to_blocks(a):
        return a.reshape((B, nb, Q_BLOCK) + a.shape[2:]).swapaxes(0, 1)

    def block_fn(args):
        qb, qib, wb, start = args
        q_chunk = (start + jnp.arange(Q_BLOCK)) // CHUNK
        logits = jnp.einsum('bqhi,bsi->bqhs', qib, k_idx,
                            preferred_element_type=jnp.float32) * (IDX_DIM ** -0.5)
        score = jnp.einsum('bqh,bqhs->bqs', wb.astype(jnp.float32) * (IDX_HEADS ** -0.5),
                           jax.nn.relu(logits))
        admissible = key_chunk[None, :] <= q_chunk[:, None]
        score = jnp.where(admissible[None], score, -jnp.inf)
        _, sel = lax.top_k(score, topk)
        sel_ok = key_chunk[sel] <= q_chunk[None, :, None]
        ks = jax.vmap(lambda kk, ii: kk[ii])(k, sel)
        vs = jax.vmap(lambda vv, ii: vv[ii])(v, sel)
        att = jnp.einsum('bqhd,bqkhd->bqhk', qb, ks, preferred_element_type=jnp.float32) * (d ** -0.5)
        att = jnp.where(sel_ok[:, :, None, :], att, -jnp.inf)
        pr = jax.nn.softmax(att, axis=-1)
        return jnp.einsum('bqhk,bqkhd->bqhd', pr.astype(vs.dtype), vs)

    starts = jnp.arange(nb, dtype=jnp.int32) * Q_BLOCK
    out = lax.map(block_fn, (to_blocks(q), to_blocks(q_idx), to_blocks(w_idx), starts))
    return out.swapaxes(0, 1).reshape(B, S, H * d)

def peer_ffn(x, w_query, sub_keys, expert_u, expert_v):
    B, S, D = x.shape
    nb = S // PEER_BLOCK
    half = PEER_QDIM // 2
    xb = x.reshape(B, nb, PEER_BLOCK, D).swapaxes(0, 1)

    def block_fn(xt):
        qv = (xt @ w_query).reshape(B, PEER_BLOCK, PEER_HEADS, 2, half)
        s1 = jnp.einsum('bthd,nd->bthn', qv[..., 0, :], sub_keys[0], preferred_element_type=jnp.float32)
        s2 = jnp.einsum('bthd,nd->bthn', qv[..., 1, :], sub_keys[1], preferred_element_type=jnp.float32)
        v1, i1 = lax.top_k(s1, PEER_TOPK)
        v2, i2 = lax.top_k(s2, PEER_TOPK)
        cand = (v1[..., :, None] + v2[..., None, :]).reshape(B, PEER_BLOCK, PEER_HEADS, PEER_TOPK * PEER_TOPK)
        sc, ci = lax.top_k(cand, PEER_TOPK)
        e1 = jnp.take_along_axis(i1, ci // PEER_TOPK, axis=-1)
        e2 = jnp.take_along_axis(i2, ci % PEER_TOPK, axis=-1)
        expert = e1 * PEER_KEYS + e2
        g = jax.nn.softmax(sc, axis=-1)
        u_sel = expert_u[expert]
        v_sel = expert_v[expert]
        act = jax.nn.gelu(jnp.einsum('btd,bthkd->bthk', xt, u_sel, preferred_element_type=jnp.float32))
        coef = (g * act).astype(xt.dtype)
        return jnp.einsum('bthk,bthkd->btd', coef, v_sel)

    out = lax.map(block_fn, xb)
    return out.swapaxes(0, 1).reshape(B, S, D)

def setup_inputs(seed: int = 0) -> dict:
    key = jax.random.key(seed)
    ks = jax.random.split(key, 20)
    f32 = jnp.float32

    def nrm(k, shape, scale):
        return jax.random.normal(k, shape, f32) * scale

    def gain(k, shape):
        return 1.0 + 0.01 * jax.random.normal(k, shape, f32)

    x = jax.random.normal(ks[0], (BATCH, SEQ, D_MODEL), f32)
    p = jax.random.normal(ks[1], (DEPTH, BATCH, SEQ, PLE_DIM), f32)
    offset = jax.random.randint(ks[2], (BATCH, 1), 0, 1024, dtype=jnp.int32)
    positions = offset + jnp.arange(SEQ, dtype=jnp.int32)[None, :]
    return {
        "x": x,
        "p": p,
        "positions": positions,
        "norm_mix": gain(ks[3], (DEPTH, D_MODEL)),
        "w_in": nrm(ks[4], (DEPTH, D_MODEL, IN_PROJ_WIDTH), D_MODEL ** -0.5),
        "qk_norm_a": gain(ks[5], (DEPTH, 2, HEAD_DIM)),
        "qk_norm_b": gain(ks[6], (DEPTH, 2, HEAD_DIM)),
        "rel_bias": nrm(ks[7], (DEPTH, N_HEADS_A, 2 * MAX_REL + 1), 0.1),
        "w_out": nrm(ks[8], (DEPTH, MIX_WIDTH, D_MODEL), MIX_WIDTH ** -0.5),
        "norm_ffn": gain(ks[9], (DEPTH, D_MODEL)),
        "peer_query": nrm(ks[10], (DEPTH, D_MODEL, PEER_HEADS * PEER_QDIM), D_MODEL ** -0.5),
        "peer_sub_keys": nrm(ks[11], (DEPTH, 2, PEER_KEYS, PEER_QDIM // 2), (PEER_QDIM // 2) ** -0.5),
        "peer_u": nrm(ks[12], (DEPTH, PEER_EXPERTS, D_MODEL), D_MODEL ** -0.5),
        "peer_v": nrm(ks[13], (DEPTH, PEER_EXPERTS, D_MODEL), PEER_HEADS ** -0.5),
        "norm_ple": gain(ks[14], (DEPTH, D_MODEL)),
        "ple_gate": nrm(ks[15], (DEPTH, D_MODEL, D_MODEL), D_MODEL ** -0.5),
        "ple_proj": nrm(ks[16], (DEPTH, PLE_DIM, D_MODEL), PLE_DIM ** -0.5),
    }

def reference(x, p, positions, norm_mix, w_in, qk_norm_a, qk_norm_b, rel_bias, w_out,
              norm_ffn, peer_query, peer_sub_keys, peer_u, peer_v, norm_ple, ple_gate, ple_proj):
    B, S, _ = x.shape
    offs = split_offsets()
    h = x
    for i in range(DEPTH):
        hn = rms_norm(h, norm_mix[i])
        proj = hn @ w_in[i]
        qa, ka, va, qb, kb, vb, qi, ki, wi = jnp.split(proj, offs, axis=-1)
        qa = rms_norm(qa.reshape(B, S, N_HEADS_A, HEAD_DIM), qk_norm_a[i, 0])
        ka = rms_norm(ka.reshape(B, S, N_HEADS_A, HEAD_DIM), qk_norm_a[i, 1])
        va = va.reshape(B, S, N_HEADS_A, HEAD_DIM)
        out_a = chunked_relpos_attention(qa, ka, va, rel_bias[i])
        qb = partial_rope(rms_norm(qb.reshape(B, S, N_HEADS_B, HEAD_DIM), qk_norm_b[i, 0]), positions)
        kb = partial_rope(rms_norm(kb.reshape(B, S, N_HEADS_B, HEAD_DIM), qk_norm_b[i, 1]), positions)
        vb = vb.reshape(B, S, N_HEADS_B, HEAD_DIM)
        qi = partial_rope(qi.reshape(B, S, IDX_HEADS, IDX_DIM), positions)
        ki = partial_rope(ki[:, :, None, :], positions)[:, :, 0, :]
        out_b = dsa_attention(qb, kb, vb, qi, ki, wi)
        h = h + jnp.concatenate([out_a, out_b], axis=-1) @ w_out[i]
        h = h + peer_ffn(rms_norm(h, norm_ffn[i]), peer_query[i], peer_sub_keys[i], peer_u[i], peer_v[i])
        gate = jax.nn.sigmoid(rms_norm(h, norm_ple[i]) @ ple_gate[i])
        h = h + gate * (p[i] @ ple_proj[i])
    return h


_drawn_inputs = setup_inputs


def setup_inputs(seed=0):
    import zlib

    import numpy as np

    out = dict(_drawn_inputs(seed))
    spreads = {}
    factors = {'qk_norm_a': 8.0,
     'qk_norm_b': 7.147,
     'rel_bias': 3.004,
     'norm_ffn': 3.433,
     'norm_ple': 8.0}
    for name, (base, spread) in spreads.items():
        noise = np.random.default_rng([zlib.crc32(name.encode()), seed]).standard_normal(out[name].shape)
        drawn = base * np.exp(spread * noise) if base else spread * noise
        out[name] = __import__('jax').numpy.asarray(drawn.astype(out[name].dtype))
    for name, factor in factors.items():
        out[name] = (out[name] * factor).astype(out[name].dtype)
    return out
```

```python
from contextlib import ExitStack

import numpy as np

import concourse.bass as bass
from concourse import mybir

F32 = mybir.dt.float32
F32R = mybir.dt.float32r
U32 = mybir.dt.uint32
I32 = mybir.dt.int32
ALU = mybir.AluOpType
ACT = mybir.ActivationFunctionType
AX = mybir.AxisListType

P = 128
T = 256
TT = T // P
D = 2048
KC = D // P
HD = 128
HALF = 1024
ROUND = 8
RAW, HI, LO = 4, 4, 2
NH = 16
IH, IDIM = 16, 64
CH = 64
TOPK = 64
PH, PN, PK = 8, 128, 16
NE1 = 128
EPS = 1e-6
THETA = 500000.0
SCALE = float(HD) ** -0.5
NEG = -1.0e30
TAKEN = -3.0e38
SMALL = 144

N_SMALL, N_PLAIN, N_QK = 8, 48, 64
N_OUT, N_QUERY, N_U, N_V, N_PROJ, N_GATE = 32, 32, 256, 256, 8, 32
B_SMALL = 0
B_PLAIN = B_SMALL + N_SMALL
B_QK = B_PLAIN + N_PLAIN
B_OUT = B_QK + N_QK
B_QUERY = B_OUT + N_OUT
B_U = B_QUERY + N_QUERY
B_V = B_U + N_U
B_PROJ = B_V + N_V
B_GATE = B_PROJ + N_PROJ
N_ALL = B_GATE + N_GATE


AHEAD = HI - 1
TAIL_ORDER = [0, 1, 2, 3] + list(range(6, 16)) + [4, 5]


class Tally:

    def __init__(self, eng, sem):
        self.eng, self.sem = eng, sem
        self.total, self.i, self.per, self.k = 0, None, 0, 0

    def enter(self, i, per):
        self.i, self.per, self.k = i, per, 0

    def leave(self, n):
        assert self.k == self.per, (self.k, self.per)
        self.total += n * self.per
        self.i = None

    def mark(self, ins):
        ins.then_inc(self.sem, 1)
        if self.i is None:
            self.total += 1
            return self.total
        self.k += 1
        return self.i * self.per + (self.total + self.k)

    def now(self):
        return self.total if self.i is None else self.i * self.per + (self.total + self.k)

    def seq(self, ins):
        self.eng.wait_ge(self.sem, self.mark(ins))


def layer_kernel(nc, xT, pT, pos, norms, head_gains, bias_a, subkeys,
                 w_small, w_plain, w_qk, w_out, w_query, w_u, w_v, w_proj, w_gate, out):
    ctx = ExitStack()
    with ctx:
        def sb(name, shape, dt=F32):
            return ctx.enter_context(nc.sbuf_tensor(name, shape, dt))

        def sem(name):
            return ctx.enter_context(nc.semaphore(name))

        big = sb("big", [P, NE1 * T])
        X1 = sb("x_hi", [P, KC, T], F32R)
        X2 = sb("x_lo", [P, KC, T], F32R)
        WR = sb("w_raw", [P, RAW, HALF])
        WL = sb("w_lo", [P, LO, HALF], F32R)
        OHA = WR[:, 2, :].rearrange("p (s n) -> p s n", n=P)
        OHB = WR[:, 3, :].rearrange("p (s n) -> p s n", n=P)
        IOTA = sb("iota_row", [P, P])
        WH = sb("w_hi", [P, HI, HALF], F32R)
        IDENT = sb("ident", [P, P])
        ONES = sb("ones", [P, P])
        RSTDB = sb("rstd_bcast", [P, T])
        TMP = sb("tmp", [P, 2, T])
        E1T = sb("e1_t", [P, T])
        E2T = sb("e2_t", [P, T])
        GT = sb("g_t", [P, T])
        GAIN = sb("gain", [P, 3, KC])
        MISC = sb("misc", [P, 24])
        RSTD1 = MISC[:, 0:2]
        SSC = MISC[:, 2:4]
        VAR = MISC[:, 4:6]
        RSC = MISC[:, 6:8]
        MHALF = MISC[:, 8:24]

        def view(off, *shape, dt=None):
            n = int(np.prod(shape))
            v = big[:, off:off + n]
            if dt is not None:
                v = v.bitcast(dt)
            if len(shape) == 2:
                v = v.rearrange("p (a b) -> p a b", b=shape[1])
            elif len(shape) == 3:
                v = v.rearrange("p (a b c) -> p a b c", b=shape[1], c=shape[2])
            return v

        XT = view(24576, KC, T)
        SQ0 = view(28672, 4, HALF)
        O_QI, O_VB, O_VA, O_QK, O_KI = 0, 2048, 4096, 6144, 14336
        QI = view(O_QI, TT, IH, IDIM)
        V_ = {8: view(O_VB, TT, HALF), 0: view(O_VA, TT, HALF)}
        KI = view(O_KI, TT, SMALL)
        POSI = view(14624, TT, dt=I32)
        POSF = view(14626, TT)
        ANG = view(14628, TT, 16)
        ANGK = view(14660, TT, 16)
        ANGA = view(14692, TT, 16)
        COS = view(14724, TT, 16)
        SIN = view(14756, TT, 16)
        COS8 = view(14788, TT, 8)
        SIN8 = view(14804, TT, 8)
        HG = view(15104, 4, HD)
        SS = view(15616, 4, TT, 8)
        RS = view(15680, 4, TT * 8)
        O_ROPE = 24576
        BIAS = view(15872, 8, 384)
        MASKB = view(18944, 384)
        SCORE = view(19328, 384)
        QIT = view(19712, 2, T)
        KIT = view(20224, T)
        RELU = view(20480, 2, 384)
        QKT = view(21248, 2, 512)
        S_ = view(22272, 2, 384)
        PR_ = view(23040, 2, 384)
        PT_ = view(23808, 2, 384)
        SMX = ctx.enter_context(nc.sbuf_tensor("softmax_small", [P, 2, 4], F32))
        T8 = ctx.enter_context(nc.sbuf_tensor("top8", [P, 8], F32))
        HT = view(0, KC, T)
        SQ = view(4096, T)
        SQACC = view(4352, T)
        QT = view(16384, 4, T)
        SALL = view(17408, TT, 2 * PH, PN)
        SUBK = view(21504, 2, PN)
        SC = view(21760, 2, PN)
        SC2 = view(22016, 2, PN)
        V16 = view(22272, 2, PK)
        I16U = view(22304, 2, PK, dt=U32)
        I16F = view(22336, 2, PK)
        IJU = view(22368, 2, PK, dt=U32)
        IJF = view(22400, 2, PK)
        C16 = view(22432, PK)
        CIU = view(22448, PK, dt=U32)
        CAND = view(22528, PK, PK)
        CAND2 = view(22784, PK * PK)
        OH = view(23040, PK, PK)
        TOK = view(23552, 3, TT * PH * PK)
        IOTA16 = view(24320, PK)
        GSUM = view(24336, TT * PH)
        SQ4 = view(10240, KC, T)
        PROJ = view(4608, KC, T)
        PTIN = view(9728, 2, T)

        ps = [ctx.enter_context(nc.psum_tensor(f"bank{b}", [P, 512], F32)) for b in range(8)]
        h_scratch = nc.dram_tensor("h_scratch", (P, KC, T), F32, kind="Internal").ap()

        raw_ready = [sem(f"raw_ready{s}") for s in range(RAW)]
        hi_ready = sem("hi_ready")
        lo_ready = sem("lo_ready")
        pe_done = sem("pe_done")
        x_loaded = [sem(f"x_loaded{q}") for q in range(4)]
        pos_loaded = sem("pos_loaded")
        norms_loaded = sem("norms_loaded")
        hg_loaded = sem("head_gains_loaded")
        bias_loaded = sem("bias_loaded")
        consts = sem("consts")
        x1_ready = sem("x1_ready")
        x2_ready = sem("x2_ready")
        sq_ready = sem("sq_ready")
        sqsum_ready = sem("sqsum_ready")
        ss_mm = sem("ss_mm")
        ssc_ready = sem("ssc_ready")
        rstd_ready = sem("rstd_ready")
        diag_ready = sem("diag_ready")
        bc_mm = sem("bc_mm")
        rstdb_ready = sem("rstdb_ready")
        xblk_evac = sem("xblk_evac")
        angles_ready = sem("angles_ready")
        trig_ready = sem("trig_ready")
        qi_roped = sem("qi_roped")
        qk_normed = sem("qk_normed")
        it_mm, it_ready = sem("it_mm"), sem("it_ready")
        lg_mm, relu_ready, acc_done = sem("lg_mm"), sem("relu_ready"), sem("acc_done")
        qk_tr, qkt_ready = sem("qk_tr"), sem("qkt_ready")
        s_mm, s_ready, exp_ready, p_ready = sem("s_mm"), sem("s_ready"), sem("exp_ready"), sem("p_ready")
        pt_tr, pt_ready, o_mm, o1_ready, o2_ready = (sem(n) for n in ("pt_tr", "pt_ready", "o_mm", "o1_ready", "o2_ready"))
        ht_loaded = sem("ht_loaded")
        h_ready = sem("h_ready")
        q_ready = sem("q_ready")
        sq_done = sem("sq_done")
        h_stored = sem("h_stored")
        subk_loaded = sem("subk_loaded")
        sk_mm, sall_ready = sem("sk_mm"), sem("sall_ready")
        tmp_ready, act_ready = sem("tmp_ready"), sem("act_ready")
        graw_ready, gexp_ready, tok_ready = sem("graw_ready"), sem("gexp_ready"), sem("tok_ready")
        tok_mm, tokt_ready = sem("tok_mm"), sem("tokt_ready")
        iota_ready = sem("iota_ready")
        oh_ready, g_mm, g_done = sem("oh_ready"), sem("g_mm"), sem("g_done")
        c1_ready, c2_ready = sem("c1_ready"), sem("c2_ready")
        ht_back = sem("ht_back")
        p_loaded = sem("p_loaded")
        p1_ready, p2_ready = sem("p1_ready"), sem("p2_ready")
        h3_ready = sem("h3_ready")
        sq4_ready = sem("sq4_ready")
        proj_evac = sem("proj_evac")
        gtmp_ready, sig_ready, hout_ready = sem("gtmp_ready"), sem("sig_ready"), sem("hout_ready")
        out_stored = sem("out_stored")
        act_own, dve_own, pool_own = sem("act_own"), sem("dve_own"), sem("pool_own")

        block = ctx.enter_context(nc.Block())

        def at(i):
            return big[:, bass.ds(i * T, T)]

        @block.sync
        def _(sp):
            def load(slot, src, width):
                sp.dma_start(WR[:, slot % RAW, 0:width], src).then_inc(raw_ready[slot % RAW], 16)

            def stream(base, w, n, first=0):
                def tile(i, s):
                    sp.wait_ge(lo_ready, i * ROUND + (base + s + 1 - RAW))
                    load(s, w[bass.ds(i * ROUND + s, 1), :, :].rearrange("a p n -> p (a n)"), HALF)

                for s in range(first, ROUND if first else 0):
                    tile(0, s)
                with sp.Fori(1 if first else 0, n // ROUND) as i:
                    for s in range(ROUND):
                        tile(i, s)

            sp.dma_start(GAIN[:, :, :], norms).then_inc(norms_loaded, 16)
            sp.dma_start(XT[:, 0:4, :], xT[:, 0:4, :]).then_inc(x_loaded[0], 16)
            for s in range(2):
                load(s, w_small[s], 2 * SMALL)
            for q in range(1, 4):
                sp.dma_start(XT[:, 4 * q:4 * q + 4, :], xT[:, 4 * q:4 * q + 4, :]).then_inc(x_loaded[q], 16)
            for s in range(2, ROUND):
                if s >= RAW:
                    sp.wait_ge(lo_ready, s + 1 - RAW)
                load(s, w_small[s], 2 * SMALL)
            sp.dma_start(POSI, pos).then_inc(pos_loaded, 16)
            sp.dma_start(HG, head_gains).then_inc(hg_loaded, 16)
            sp.dma_start(BIAS, bias_a).then_inc(bias_loaded, 16)
            stream(B_PLAIN, w_plain, N_PLAIN)
            stream(B_QK, w_qk, N_QK)
            for s in range(RAW):
                sp.wait_ge(lo_ready, B_OUT + s + 1 - RAW)
                load(s, w_out[s], HALF)
            sp.wait_ge(o_mm, NH)
            sp.dma_start(HT, xT).then_inc(ht_loaded, 16)
            sp.dma_start(SUBK, subkeys).then_inc(subk_loaded, 16)
            stream(B_OUT, w_out, N_OUT, RAW)
            for s in range(RAW):
                sp.wait_ge(lo_ready, B_QUERY + s + 1 - RAW)
                load(s, w_query[s], HALF)
            sp.wait_ge(h_ready, KC)
            sp.dma_start(h_scratch, HT).then_inc(h_stored, 16)
            stream(B_QUERY, w_query, N_QUERY, RAW)
            stream(B_U, w_u, N_U)
            with sp.Fori(0, N_V // ROUND) as i:
                for s in range(ROUND):
                    sp.wait_ge(lo_ready, i * ROUND + (B_V + s + 1 - RAW))
                    if s == 2:
                        sp.wait_ge(g_done, 64)
                    load(s, w_v[bass.ds(i * (ROUND // 2) + s // 2, 1), :, (s % 2) * HALF:(s % 2 + 1) * HALF]
                         .rearrange("a p n -> p (a n)"), HALF)
            sp.wait_ge(c2_ready, NE1)
            sp.wait_ge(h_stored, 16)
            sp.dma_start(HT, h_scratch).then_inc(ht_back, 16)
            sp.dma_start(PTIN, pT).then_inc(p_loaded, 16)
            for s in range(ROUND):
                sp.wait_ge(lo_ready, B_PROJ + s + 1 - RAW)
                load(s, w_proj[s], 512)
            stream(B_GATE, w_gate, N_GATE)
            for q in range(4):
                sp.wait_ge(hout_ready, 4 * (q + 1))
                sp.dma_start(out[:, 4 * q:4 * q + 4, :], HT[:, 4 * q:4 * q + 4, :]).then_inc(out_stored, 16)
            sp.wait_ge(out_stored, 64)

        @block.gpsimd
        def _(pool):
            own = Tally(pool, pool_own)
            nc.gpsimd.memset(ONES[:, :], 1.0).then_inc(consts, 1)
            own.seq(nc.gpsimd.memset(IDENT[:, :], 0.0))
            nc.gpsimd.affine_select(out=IDENT[:, :], in_=IDENT[:, :], compare_op=ALU.not_equal, fill=1.0, base=0,
                                    pattern=[[-1, P]], channel_multiplier=1).then_inc(consts, 1)
            nc.gpsimd.iota(IOTA[:, :], pattern=[[1, P]], base=0, channel_multiplier=0,
                           allow_small_or_imprecise_dtypes=True).then_inc(iota_ready, 1)
            own.seq(nc.gpsimd.memset(MHALF, -0.5))

            def inv_rms(which):
                pool.wait_ge(ssc_ready, which)
                own.seq(nc.gpsimd.tensor_scalar(VAR, SSC, 1.0 / D, EPS, ALU.mult, ALU.add))
                nc.gpsimd.tensor_tensor(RSTD1 if which == 1 else RSC, VAR, MHALF[:, 0:2], ALU.pow).then_inc(rstd_ready, 1)

            inv_rms(1)

            def rope(t, heads, half, cos, sin, last_inc):
                x1, x2 = t[:, :, :, 0:half], t[:, :, :, half:2 * half]

                def tmp(j):
                    return view(O_ROPE + 256 * j, TT, heads, half)

                def bc(c):
                    return c.unsqueeze(2).broadcast_to([P, TT, heads, half])

                a, b, c, d = (tmp(j) for j in range(4))
                nc.gpsimd.tensor_tensor(a, x1, bc(cos), ALU.mult)
                nc.gpsimd.tensor_tensor(b, x2, bc(sin), ALU.mult)
                nc.gpsimd.tensor_tensor(c, x2, bc(cos), ALU.mult)
                own.seq(nc.gpsimd.tensor_tensor(d, x1, bc(sin), ALU.mult))
                own.mark(nc.gpsimd.tensor_tensor(x1, a, b, ALU.subtract))
                own.seq(nc.gpsimd.tensor_tensor(x2, c, d, ALU.add))
                if last_inc is not None:
                    pool.nop().then_inc(last_inc, 1)

            pool.wait_ge(x2_ready, KC)
            pool.wait_ge(sqsum_ready, 1)
            pool.wait_ge(trig_ready, 3)
            pool.wait_ge(xblk_evac, 1)
            rope(KI[:, :, 0:2 * IDIM].rearrange("p t (h d) -> p t h d", d=IDIM), 2, 8, COS8, SIN8, None)
            pool.wait_ge(xblk_evac, 3)
            rope(QI, IH, 8, COS8, SIN8, qi_roped)
            pool.wait_ge(hg_loaded, 16)
            for g in range(4):
                pool.wait_ge(xblk_evac, 7 + 2 * (g + 1))
                own.seq(nc.gpsimd.tensor_scalar(RS[:, g, :], SS[:, g, :, :].rearrange("p a b -> p (a b)"),
                                                1.0 / HD, EPS, ALU.mult, ALU.add))
                own.seq(nc.gpsimd.tensor_tensor(RS[:, g, :], RS[:, g, :], MHALF, ALU.pow))
                q3 = big[:, O_QK + 2048 * g:O_QK + 2048 * (g + 1)].rearrange("p (h d) -> p h d", d=HD)
                own.seq(nc.gpsimd.tensor_tensor(q3, q3, RS[:, g, :].unsqueeze(2).broadcast_to([P, TT * 8, HD]), ALU.mult))
                ins = nc.gpsimd.tensor_tensor(q3, q3, HG[:, g, :].unsqueeze(1).broadcast_to([P, TT * 8, HD]), ALU.mult)
                if g < 2:
                    own.seq(ins)
                    rope(big[:, O_QK + 2048 * g:O_QK + 2048 * (g + 1)].rearrange("p (t h d) -> p t h d", t=TT, d=HD),
                         8, 16, COS, SIN, qk_normed)
                else:
                    ins.then_inc(qk_normed, 1)

            pool.wait_ge(o_mm, NH)
            own.seq(nc.gpsimd.memset(SQACC, 0.0))
            with pool.Fori(0, KC) as i:
                own.enter(i, 2)
                pool.wait_ge(h_ready, i + 1)
                h = at(i)
                own.seq(nc.gpsimd.tensor_tensor(SQ, h, h, ALU.mult))
                own.seq(nc.gpsimd.tensor_tensor(SQACC, SQACC, SQ, ALU.add))
                own.leave(KC)
            pool.nop().then_inc(sq_done, 1)
            inv_rms(2)
            inv_rms(3)

        @block.scalar
        def _(act):
            own = Tally(act, act_own)

            def hi(s, n, width):
                act.wait_ge(raw_ready[s % RAW], wave(n, s % RAW))
                if not (isinstance(n, int) and n < HI):
                    act.wait_ge(pe_done, n + (1 - HI))
                nc.scalar.activation(WH[:, s % HI, 0:width], WR[:, s % RAW, 0:width], ACT.Copy).then_inc(hi_ready, 1)

            def wave(n, s):
                return 16 * (n // RAW + 1) if isinstance(n, int) else (n - s) * (16 // RAW) + 16

            act.wait_ge(norms_loaded, 16)
            for j in range(8):
                for k in (2 * j, 2 * j + 1):
                    if k % 4 == 0:
                        act.wait_ge(x_loaded[k // 4], 16)
                    nc.scalar.activation(X1[:, k, :], XT[:, k, :], ACT.Copy, scale=GAIN[:, 0, k:k + 1]).then_inc(x1_ready, 1)
                hi(j, j, 2 * SMALL)
            hi(0, B_PLAIN, HALF)
            hi(1, B_PLAIN + 1, HALF)
            for q in range(4):
                nc.scalar.activation(SQ0[:, q, :], XT[:, 4 * q:4 * q + 4, :].rearrange("p a b -> p (a b)"),
                                     ACT.Square).then_inc(sq_ready, 1)
            act.wait_ge(angles_ready, 1)
            own.mark(nc.scalar.activation(SIN, ANG, ACT.Sin))
            own.mark(nc.scalar.activation(COS, ANGA, ACT.Sin))
            act.wait_ge(act_own, own.total)
            nc.scalar.activation(COS8, COS[:, :, 0:16:2], ACT.Copy).then_inc(trig_ready, 1)
            nc.scalar.activation(SIN8, SIN[:, :, 0:16:2], ACT.Copy).then_inc(trig_ready, 1)
            act.nop().then_inc(trig_ready, 1)
            hi(2, B_PLAIN + 2, HALF)
            act.wait_ge(rstd_ready, 1)
            act.wait_ge(pe_done, B_PLAIN)
            for tt in range(TT):
                ins = nc.scalar.activation(KI[:, tt, :], ps[2 + tt][:, 0:SMALL], ACT.Copy, scale=RSTD1[:, tt:tt + 1])
            ins.then_inc(xblk_evac, 1)

            def evac_block(n_end, bank, dst, squares=None):
                act.wait_ge(pe_done, n_end)
                if squares is not None:
                    act.wait_ge(act_own, own.now())
                for tt in range(TT):
                    if squares is not None:
                        for hh in range(4):
                            own.mark(nc.scalar.activation(SQJ[:, 4 * tt + hh, :], ps[bank + tt][:, hh * HD:(hh + 1) * HD], ACT.Square,
                                                 scale=RSTD1[:, tt:tt + 1], accum_out=squares(tt, hh)))
                    ins = nc.scalar.activation(dst(tt), ps[bank + tt][:, :], ACT.Copy, scale=RSTD1[:, tt:tt + 1])
                ins.then_inc(xblk_evac, 1)

            SQJ = view(28672, 8, HD)
            with act.Fori(0, 3) as i:
                for u in range(AHEAD, 16 + AHEAD):
                    hi(u % ROUND, i * 16 + (B_PLAIN + u), HALF)
                    if u % 8 == AHEAD - 1:
                        b = u // 8 - 1
                        evac_block(i * 16 + (B_PLAIN + 8 * (b + 1)), 2 * b,
                                   lambda tt: big[:, bass.ds(i * 2048 + (tt * 1024 + b * 512), 512)])
            with act.Fori(0, 4) as i:
                own.enter(i, 16)
                for u in range(AHEAD, 16 + AHEAD):
                    hi(u % ROUND, i * 16 + (B_QK + u), HALF)
                    if u % 8 == AHEAD - 1:
                        b = u // 8 - 1
                        evac_block(i * 16 + (B_QK + 8 * (b + 1)), 2 * b,
                                   lambda tt: big[:, bass.ds(i * 2048 + (O_QK + tt * 1024 + b * 512), 512)],
                                   lambda tt, hh: big[:, bass.ds(i * 16 + (15616 + tt * 8 + b * 4 + hh), 1)])
                own.leave(4)

            act.wait_ge(it_mm, 1)
            nc.scalar.activation(KIT, ps[4][:, 0:T], ACT.Copy).then_inc(it_ready, 1)

            def qi_evac(pr):
                act.wait_ge(it_mm, pr + 2)
                if pr >= 2:
                    act.wait_ge(lg_mm, 2 * (pr - 1))
                nc.scalar.activation(QIT[:, pr % 2, :], ps[5 - pr % 2][:, 0:T], ACT.Copy).then_inc(it_ready, 1)

            qi_evac(0)
            for pr in range(IH // 2):
                if pr + 1 < IH // 2:
                    qi_evac(pr + 1)
                for h in (2 * pr, 2 * pr + 1):
                    act.wait_ge(lg_mm, h + 1)
                    if h >= 2:
                        act.wait_ge(acc_done, h - 1)
                    nc.scalar.activation(RELU[:, h % 2, :], ps[6 + h % 2][:, 0:384], ACT.Relu,
                                         scale=float(IDIM) ** -0.5 * float(IH) ** -0.5).then_inc(relu_ready, 1)

            def qkt(j):
                act.wait_ge(qk_tr, j + 1)
                if j >= 2:
                    act.wait_ge(s_mm, j - 1)
                nc.scalar.activation(QKT[:, j % 2, :], ps[4 * (j % 2)][:, :], ACT.Copy).then_inc(qkt_ready, 1)

            qkt(0)
            qkt(1)
            for j in range(NH):
                s = j % 2
                act.wait_ge(s_ready, j + 1)
                if j >= 2:
                    act.wait_ge(pt_tr, j - 1)
                nc.scalar.activation(PR_[:, s, 0:128], S_[:, s, 0:128], ACT.Exp, bias=SMX[:, s, 0:1],
                                     accum_out=SMX[:, s, 2:3]).then_inc(exp_ready, 1)
                nc.scalar.activation(PR_[:, s, 128:384], S_[:, s, 128:384], ACT.Exp, bias=SMX[:, s, 1:2],
                                     accum_out=SMX[:, s, 3:4]).then_inc(exp_ready, 1)
                if j + 2 < NH:
                    qkt(j + 2)
                act.wait_ge(pt_tr, j + 1)
                nc.scalar.activation(PT_[:, s, :], ps[4 * s + 2][:, 0:384], ACT.Copy).then_inc(pt_ready, 1)
                act.wait_ge(o_mm, j + 1)
                nc.scalar.activation(X1[:, j, :], ps[4 * s + 3][:, 0:T], ACT.Copy).then_inc(o1_ready, 1)

            with act.Fori(0, N_OUT // ROUND) as i:
                for u in range(AHEAD, ROUND + AHEAD):
                    hi(u % ROUND, i * ROUND + (B_OUT + u), HALF)
            act.wait_ge(pe_done, B_QUERY)
            for k in range(KC):
                act.wait_ge(h_ready, k + 1)
                nc.scalar.activation(X1[:, k, :], HT[:, k, :], ACT.Copy, scale=GAIN[:, 1, k:k + 1]).then_inc(x1_ready, 1)

            def s_evac(i, m):
                act.wait_ge(sk_mm, i * 4 + (m + 1))
                nc.scalar.activation(
                    SALL[:, :, bass.ds(i * 4 + m, 1), :].rearrange("p t a n -> p t (a n)"),
                    ps[4 + m][:, 0:T].rearrange("p (t n) -> p t n", t=TT), ACT.Copy).then_inc(sall_ready, 1)

            for u in range(AHEAD, ROUND + AHEAD):
                hi(u % ROUND, B_QUERY + u, HALF)
                if u == 6:
                    act.wait_ge(bc_mm, 1)
                    nc.scalar.activation(RSTDB[:, :], ps[7][:, 0:T], ACT.Copy).then_inc(rstdb_ready, 1)
            for m in range(4):
                s_evac(0, m)
            with act.Fori(1, N_QUERY // ROUND) as i:
                for u in range(AHEAD, ROUND + AHEAD):
                    hi(u % ROUND, i * ROUND + (B_QUERY + u), HALF)
                for m in range(4):
                    s_evac(i, m)

            def gelu_units(i, last=False):
                for u in range(AHEAD, ROUND + AHEAD):
                    if not (last and u == ROUND + 2):
                        hi(u % ROUND, i * ROUND + (B_U + u), HALF)
                    if u % 2 == 0:
                        m = u // 2 - 2
                        act.wait_ge(tmp_ready, i * 4 + (4 + m + 1))
                        nc.scalar.activation(at(i * 4 + m), TMP[:, m % 2, :],
                                             ACT.Gelu_apprx_tanh).then_inc(act_ready, 1)

            act.wait_ge(h_stored, 16)
            act.nop().then_inc(act_ready, 2)
            with act.Fori(0, 16) as i:
                gelu_units(i)
            act.wait_ge(graw_ready, 1)
            nc.scalar.activation(TOK[:, 2, :], TOK[:, 2, :], ACT.Exp).then_inc(gexp_ready, 1)
            for w in range(3):
                act.wait_ge(tok_mm, w + 1)
                nc.scalar.activation((E1T, E2T, GT)[w][:, :], ps[4 + w][:, 0:T], ACT.Copy).then_inc(tokt_ready, 1)
            with act.Fori(16, 31) as i:
                gelu_units(i)
            gelu_units(31, last=True)

            def c1(i, slot):
                nc.scalar.activation(X1[:, slot, :], at(i), ACT.Copy).then_inc(c1_ready, 1)

            act.wait_ge(g_done, 64)
            c1(0, 0)
            c1(1, 1)
            hi(2, B_V + 2, HALF)
            with act.Fori(0, N_V // ROUND - 1) as i:
                for u in range(AHEAD, ROUND + AHEAD):
                    if u % 2 == 0:
                        c1(i * 4 + u // 2, (u // 2) % 4)
                    hi(u % ROUND, i * ROUND + (B_V + u), HALF)
            for u in range(AHEAD, ROUND + AHEAD):
                if u % 2 == 0 and u < ROUND:
                    c1(NE1 - 4 + u // 2, u // 2)
                hi(u % ROUND, B_V + N_V - ROUND + u, HALF if u < ROUND else 512)

            act.wait_ge(p_loaded, 16)
            nc.scalar.activation(X1[:, 4:6, :], PTIN, ACT.Copy).then_inc(p1_ready, 1)
            for u in range(1, ROUND + 1):
                n = u + AHEAD - 1
                hi(n % ROUND, B_PROJ + n, 512 if n < ROUND else HALF)
                act.wait_ge(pe_done, B_PROJ + u)
                for m in (2 * u - 2, 2 * u - 1):
                    nc.scalar.activation(PROJ[:, m, :], ps[m % 4][:, 0:T], ACT.Copy).then_inc(proj_evac, 1)
                for k in TAIL_ORDER[2 * u - 2:2 * u]:
                    act.wait_ge(h3_ready, k + 1)
                    nc.scalar.activation(X1[:, k, :], HT[:, k, :], ACT.Copy, scale=GAIN[:, 2, k:k + 1]).then_inc(x1_ready, 1)
                    nc.scalar.activation(SQ4[:, k, :], HT[:, k, :], ACT.Square).then_inc(sq4_ready, 1)
            for u in range(AHEAD, 6):
                hi(u % ROUND, B_GATE + u, HALF)
            act.wait_ge(bc_mm, 2)
            nc.scalar.activation(RSTDB[:, :], ps[7][:, 0:T], ACT.Copy).then_inc(rstdb_ready, 1)

            def sig(m, s):
                act.wait_ge(gtmp_ready, m + 1)
                nc.scalar.activation(TMP[:, s, :], TMP[:, s, :], ACT.Sigmoid).then_inc(sig_ready, 1)

            for u in range(6, N_GATE):
                hi(u % ROUND, B_GATE + u, HALF)
                if u % 2 == 0:
                    sig(u // 2 - 3, (u // 2 - 3) % 2)
            for m in range(13, 16):
                sig(m, m % 2)

        @block.vector
        def _(dve):
            own = Tally(dve, dve_own)

            def lo(s, n, width):
                dve.wait_ge(hi_ready, n + 1)
                if not (isinstance(n, int) and n < LO):
                    dve.wait_ge(pe_done, n + (1 - LO))
                nc.vector.tensor_tensor(WL[:, s % LO, 0:width], WR[:, s % RAW, 0:width], WH[:, s % HI, 0:width].bitcast(F32),
                                        ALU.subtract).then_inc(lo_ready, 1)

            dve.wait_ge(norms_loaded, 16)
            for j in range(8):
                for k in (2 * j, 2 * j + 1):
                    dve.wait_ge(x1_ready, k + 1)
                    nc.vector.scalar_tensor_tensor(out=X2[:, k, :], in0=XT[:, k, :], scalar=GAIN[:, 0, k:k + 1],
                                                   in1=X1[:, k, :].bitcast(F32), op0=ALU.mult,
                                                   op1=ALU.subtract).then_inc(x2_ready, 1)
                lo(j, j, 2 * SMALL)
            lo(0, B_PLAIN, HALF)
            dve.wait_ge(sq_ready, 4)
            sq = SQ0.rearrange("p a b -> p (a b)")
            for w in (2048, 1024, 512):
                own.seq(nc.vector.tensor_tensor(sq[:, 0:w], sq[:, 0:w], sq[:, w:2 * w], ALU.add))
            nc.vector.tensor_tensor(sq[:, 0:256], sq[:, 0:256], sq[:, 256:512], ALU.add).then_inc(sqsum_ready, 1)

            dve.wait_ge(pos_loaded, 16)
            own.seq(nc.vector.tensor_copy(POSF, POSI))
            freq = np.float32(1.0) / np.power(np.float32(THETA), np.arange(16, dtype=np.float32) / np.float32(16))
            for f in range(16):
                ins = nc.vector.tensor_scalar(ANG[:, :, f], POSF, float(freq[f]), None, ALU.mult)
                own.mark(ins)
            dve.wait_ge(dve_own, own.total)
            MAGIC = float(1.5 * 2 ** 23)
            own.seq(nc.vector.tensor_scalar(ANGK, ANG, float(1 / (2 * np.pi)), MAGIC, ALU.mult, ALU.add))
            own.seq(nc.vector.tensor_scalar(ANGK, ANGK, -MAGIC, None, ALU.add))
            two_pi = 2 * np.pi
            c1 = 6.28125
            c2 = float(np.float32(int((two_pi - c1) * 2 ** 21) / 2 ** 21))
            c3 = float(np.float32(two_pi - c1 - c2))
            for c in (c1, c2, c3):
                own.seq(nc.vector.scalar_tensor_tensor(out=ANG, in0=ANGK, scalar=-c, in1=ANG, op0=ALU.mult, op1=ALU.add))
            lim = float(np.float32(3.1415925))
            own.seq(nc.vector.tensor_scalar(ANG, ANG, lim, -lim, ALU.min, ALU.max))
            own.seq(nc.vector.tensor_scalar(ANGK, ANG, -1.0, None, ALU.mult))
            own.seq(nc.vector.tensor_tensor(ANGA, ANG, ANGK, ALU.max))
            nc.vector.tensor_scalar(ANGA, ANGA, -1.0, float(np.pi / 2), ALU.mult, ALU.add).then_inc(angles_ready, 1)
            dve.wait_ge(ss_mm, 1)
            nc.vector.tensor_copy(SSC, ps[4][:, 0:2]).then_inc(ssc_ready, 1)

            for base, n in ((B_PLAIN, 3), (B_QK, 4)):
                with dve.Fori(0, 2 * n) as i:
                    for u in range(1, ROUND + 1):
                        lo(u % ROUND, i * ROUND + (base + u), HALF)

            dve.wait_ge(bias_loaded, 16)
            own.mark(nc.vector.memset(BIAS[0:CH, :, 64:128], NEG))
            own.mark(nc.vector.memset(BIAS[0:CH, :, 320:384], NEG))
            own.mark(nc.vector.memset(SCORE, 0.0))
            dve.wait_ge(dve_own, own.total)
            for h in range(IH):
                dve.wait_ge(relu_ready, h + 1)
                o1 = nc.vector.scalar_tensor_tensor(out=SCORE[:, 0:128], in0=RELU[:, h % 2, 0:128],
                                                    scalar=KI[:, 0, 128 + h:129 + h], in1=SCORE[:, 0:128],
                                                    op0=ALU.mult, op1=ALU.add)
                own.mark(o1)
                o2 = nc.vector.scalar_tensor_tensor(out=SCORE[:, 128:384], in0=RELU[:, h % 2, 128:384],
                                                    scalar=KI[:, 1, 128 + h:129 + h], in1=SCORE[:, 128:384],
                                                    op0=ALU.mult, op1=ALU.add)
                own.seq(o2)
                dve.nop().then_inc(acc_done, 1)
            own.mark(nc.vector.memset(SCORE[0:CH, 64:128], NEG))
            own.mark(nc.vector.memset(SCORE[0:CH, 320:384], NEG))
            dve.wait_ge(dve_own, own.total)
            for a, b in ((0, 128), (128, 384)):
                for r in range(TOPK // 8):
                    own.seq(nc.vector.max(T8[:, :], SCORE[:, a:b]))
                    own.seq(nc.vector.match_replace(SCORE[:, a:b], T8[:, :], SCORE[:, a:b], TAKEN))
            own.seq(nc.vector.tensor_scalar(MASKB, SCORE, 0.5 * TAKEN, NEG, ALU.is_gt, ALU.mult))

            def scores(j):
                s = j % 2
                dve.wait_ge(s_mm, j + 1)
                if j >= 2:
                    dve.wait_ge(exp_ready, 2 * (j - 1))
                extra = BIAS[:, j, :] if j < 8 else MASKB
                own.seq(nc.vector.scalar_tensor_tensor(out=S_[:, s, :], in0=ps[4 * s + 1][:, 0:384], scalar=SCALE,
                                                       in1=extra, op0=ALU.mult, op1=ALU.add))
                nc.vector.tensor_reduce(SMX[:, s, 0:1], S_[:, s, 0:128], AX.X, ALU.max, negate=True)
                nc.vector.tensor_reduce(SMX[:, s, 1:2], S_[:, s, 128:384], AX.X, ALU.max, negate=True).then_inc(s_ready, 1)

            scores(0)
            scores(1)
            for j in range(NH):
                s = j % 2
                dve.wait_ge(exp_ready, 2 * (j + 1))
                own.seq(nc.vector.reciprocal(SMX[:, s, 2:4], SMX[:, s, 2:4]))
                nc.vector.tensor_scalar(PR_[:, s, 0:128], PR_[:, s, 0:128], SMX[:, s, 2:3], None, ALU.mult)
                nc.vector.tensor_scalar(PR_[:, s, 128:384], PR_[:, s, 128:384], SMX[:, s, 3:4], None,
                                        ALU.mult).then_inc(p_ready, 1)
                if j + 2 < NH:
                    scores(j + 2)
                dve.wait_ge(o1_ready, j + 1)
                nc.vector.tensor_tensor(X2[:, j, :], ps[4 * s + 3][:, 0:T], X1[:, j, :].bitcast(F32),
                                        ALU.subtract).then_inc(o2_ready, 1)

            def x2_part(k, gain, ready):
                dve.wait_ge(x1_ready, ready)
                nc.vector.scalar_tensor_tensor(out=X2[:, k, :], in0=HT[:, k, :], scalar=GAIN[:, gain, k:k + 1],
                                               in1=X1[:, k, :].bitcast(F32), op0=ALU.mult,
                                               op1=ALU.subtract).then_inc(x2_ready, 1)

            dve.wait_ge(ht_loaded, 16)
            with dve.Fori(0, N_OUT // ROUND) as i:
                for u in range(1, ROUND + 1):
                    lo(u % ROUND, i * ROUND + (B_OUT + u), HALF)
                    if u % 2 == 0:
                        m = u // 2 - 1
                        dve.wait_ge(pe_done, i * ROUND + (B_OUT + u))
                        h = at(i * 4 + m)
                        nc.vector.tensor_tensor(h, ps[m][:, 0:T], h, ALU.add).then_inc(h_ready, 1)
            for k in range(KC):
                x2_part(k, 1, KC + k + 1)

            def diagonals(which):
                dve.wait_ge(rstd_ready, which)
                for tt in range(TT):
                    ins = nc.vector.tensor_scalar(TMP[:, 0, tt * P:(tt + 1) * P], IDENT[:, :], RSC[:, tt:tt + 1], None, ALU.mult)
                ins.then_inc(diag_ready, 1)

            def q_evac(i, m):
                dve.wait_ge(pe_done, i * ROUND + (B_QUERY + 2 * m + 2))
                nc.vector.tensor_tensor(QT[:, m, :], ps[m][:, 0:T], RSTDB[:, :], ALU.mult).then_inc(q_ready, 1)

            for u in range(1, ROUND + 1):
                lo(u % ROUND, B_QUERY + u, HALF)
                if u == 2:
                    dve.wait_ge(ss_mm, 2)
                    nc.vector.tensor_copy(SSC, ps[6][:, 0:2]).then_inc(ssc_ready, 1)
                if u == 3:
                    diagonals(2)
                if u == 5:
                    dve.wait_ge(rstdb_ready, 1)
                    q_evac(0, 0)
                    q_evac(0, 1)
                if u in (6, 8):
                    q_evac(0, u // 2 - 1)
            with dve.Fori(1, N_QUERY // ROUND) as i:
                for u in range(1, ROUND + 1):
                    lo(u % ROUND, i * ROUND + (B_QUERY + u), HALF)
                    if u % 2 == 0:
                        m = u // 2 - 1
                        if m == 0:
                            dve.wait_ge(sk_mm, i * 4)
                        q_evac(i, m)

            def u_evac(i, m):
                dve.wait_ge(pe_done, i * ROUND + (B_U + 2 * m + 2))
                dve.wait_ge(act_ready, i * 4 + (m + 1))
                nc.vector.tensor_tensor(TMP[:, m % 2, :], ps[m][:, 0:T], RSTDB[:, :], ALU.mult).then_inc(tmp_ready, 1)

            def top16(values, indices, src, spare):
                dve.drain()
                nc.vector.max(values[:, 0:8], src)
                dve.drain()
                nc.vector.max_index(indices[:, 0:8], values[:, 0:8], src)
                nc.vector.match_replace(spare, values[:, 0:8], src, TAKEN)
                dve.drain()
                nc.vector.max(values[:, 8:16], spare)
                dve.drain()
                nc.vector.max_index(indices[:, 8:16], values[:, 8:16], spare)
                dve.drain()

            def route(i, step):
                if step == 0:
                    own.mark(nc.vector.tensor_copy(SC.rearrange("p a b -> p (a b)"), big[:, bass.ds(i * 256 + 17408, 256)]))
                    top16(V16[:, 0, :], I16U[:, 0, :], SC[:, 0, :], SC2[:, 0, :])
                if step == 1:
                    top16(V16[:, 1, :], I16U[:, 1, :], SC[:, 1, :], SC2[:, 1, :])
                    own.seq(nc.vector.tensor_copy(I16F, I16U))
                if step == 2:
                    own.mark(nc.vector.tensor_tensor(CAND, V16[:, 0, :].unsqueeze(2).broadcast_to([P, PK, PK]),
                                                    V16[:, 1, :].unsqueeze(1).broadcast_to([P, PK, PK]), ALU.add))
                    top16(C16, CIU, CAND.rearrange("p a b -> p (a b)"), CAND2)
                if step == 3:
                    own.seq(nc.vector.tensor_scalar(IJU[:, 0, :], CIU, 4, None, ALU.logical_shift_right))
                    own.seq(nc.vector.tensor_scalar(IJU[:, 1, :], CIU, 15, None, ALU.bitwise_and))
                    own.seq(nc.vector.tensor_copy(IJF, IJU))
                    own.seq(nc.vector.tensor_scalar(big[:, bass.ds(i * PK + (23552 + 512), PK)], C16, C16[:, 0:1], None,
                                                    ALU.subtract))
                if step in (3, 4):
                    w = step - 3
                    own.seq(nc.vector.tensor_tensor(OH, IJF[:, w, :].unsqueeze(2).broadcast_to([P, PK, PK]),
                                                    IOTA16.unsqueeze(1).broadcast_to([P, PK, PK]), ALU.is_equal))
                    own.seq(nc.vector.tensor_tensor(OH, OH, I16F[:, w, :].unsqueeze(1).broadcast_to([P, PK, PK]), ALU.mult))
                    own.seq(nc.vector.tensor_reduce(big[:, bass.ds(i * PK + (23552 + 256 * w), PK)], OH, AX.X, ALU.add))

            ROUTE_STEPS = 13
            dve.nop().then_inc(tmp_ready, 4)
            for f in range(PK):
                own.mark(nc.vector.memset(IOTA16[:, f:f + 1], float(f)))
            dve.wait_ge(dve_own, own.total)
            dve.wait_ge(sall_ready, 2 * PH)
            with dve.Fori(0, 16) as i:
                own.enter(i, ROUTE_STEPS)
                for u in range(1, ROUND + 1):
                    lo(u % ROUND, i * ROUND + (B_U + u), HALF)
                    if u % 2 == 0:
                        u_evac(i, u // 2 - 1)
                    if u in (1, 3, 5, 7, 8):
                        route(i, (1, 3, 5, 7, 8).index(u))
                own.leave(16)
            dve.nop().then_inc(graw_ready, 1)
            dve.wait_ge(gexp_ready, 1)
            g3 = TOK[:, 2, :].rearrange("p (g k) -> p g k", k=PK)
            own.seq(nc.vector.tensor_reduce(GSUM, g3, AX.X, ALU.add))
            own.seq(nc.vector.reciprocal(GSUM, GSUM))
            nc.vector.tensor_tensor(g3, g3, GSUM.unsqueeze(2).broadcast_to([P, TT * PH, PK]), ALU.mult).then_inc(tok_ready, 1)
            with dve.Fori(16, 32) as i:
                for u in range(1, ROUND + 1):
                    lo(u % ROUND, i * ROUND + (B_U + u), HALF)
                    if u % 2 == 0:
                        u_evac(i, u // 2 - 1)

            def onehots(t0, slot0):
                for q in range(4):
                    nc.vector.tensor_scalar(OHB[:, slot0 + q, :], IOTA[:, :], E2T[:, bass.ds(t0 + q, 1)], None, ALU.is_equal)
                    ins = nc.vector.tensor_scalar(OHA[:, slot0 + q, :], IOTA[:, :], E1T[:, bass.ds(t0 + q, 1)],
                                                  GT[:, bass.ds(t0 + q, 1)], ALU.is_equal, ALU.mult)
                ins.then_inc(oh_ready, 1)

            def apply_gates(t0, bank, group):
                dve.wait_ge(g_mm, group + 1)
                c = big[:, :].rearrange("p (e t) -> p t e", t=T)[:, bass.ds(t0, 4), :]
                nc.vector.tensor_tensor(c, ps[bank][:, :].rearrange("p (q e) -> p q e", q=4), c, ALU.mult).then_inc(g_done, 1)

            dve.wait_ge(iota_ready, 1)
            dve.wait_ge(tokt_ready, 3)
            dve.wait_ge(act_ready, NE1 + 2)
            onehots(0, 0)
            with dve.Fori(0, 31) as i:
                onehots(i * 8 + 4, 4)
                apply_gates(i * 8, 0, i * 2)
                onehots(i * 8 + 8, 0)
                apply_gates(i * 8 + 4, 1, i * 2 + 1)
            onehots(31 * 8 + 4, 4)
            apply_gates(31 * 8, 0, 62)
            apply_gates(31 * 8 + 4, 1, 63)

            def c2(i, slot):
                dve.wait_ge(c1_ready, i + 1)
                nc.vector.tensor_tensor(X2[:, slot, :], at(i), X1[:, slot, :].bitcast(F32), ALU.subtract).then_inc(c2_ready, 1)

            c2(0, 0)
            with dve.Fori(0, N_V // ROUND - 1) as i:
                for u in range(1, ROUND + 1):
                    if u % 2 == 0:
                        c2(i * 4 + u // 2, (u // 2) % 4)
                    lo(u % ROUND, i * ROUND + (B_V + u), HALF)
            for u in range(1, ROUND + 1):
                if u % 2 == 0 and u < ROUND:
                    c2(NE1 - 4 + u // 2, u // 2)
                lo(u % ROUND, B_V + N_V - ROUND + u, HALF if u < ROUND else 512)

            dve.wait_ge(p1_ready, 1)
            nc.vector.tensor_tensor(X2[:, 4:6, :], PTIN, X1[:, 4:6, :].bitcast(F32), ALU.subtract).then_inc(p2_ready, 1)
            dve.wait_ge(ht_back, 16)
            dve.wait_ge(pe_done, B_PROJ)
            for k in range(KC):
                nc.vector.tensor_tensor(HT[:, k, :], ps[k // 2][:, (k % 2) * T:(k % 2 + 1) * T], HT[:, k, :],
                                        ALU.add).then_inc(h3_ready, 1)
            for u in range(1, ROUND + 1):
                lo(u % ROUND, B_PROJ + u, 512 if u < ROUND else HALF)
                for j in (2 * u - 2, 2 * u - 1):
                    x2_part(TAIL_ORDER[j], 2, 2 * KC + j + 1)
            dve.wait_ge(ss_mm, 3)
            nc.vector.tensor_copy(SSC, ps[6][:, 0:2]).then_inc(ssc_ready, 1)
            lo(1, B_GATE + 1, HALF)
            diagonals(3)
            for u in range(2, 6):
                lo(u, B_GATE + u, HALF)
            dve.wait_ge(rstdb_ready, 2)

            def gate_tmp(m):
                dve.wait_ge(pe_done, B_GATE + 2 * m + 2)
                nc.vector.tensor_tensor(TMP[:, m % 2, :], ps[m % 4][:, 0:T], RSTDB[:, :], ALU.mult).then_inc(gtmp_ready, 1)

            def gate_add(m):
                dve.wait_ge(sig_ready, m + 1)
                own.seq(nc.vector.tensor_tensor(TMP[:, m % 2, :], TMP[:, m % 2, :], PROJ[:, m, :], ALU.mult))
                own.seq(nc.vector.tensor_tensor(HT[:, m, :], HT[:, m, :], TMP[:, m % 2, :], ALU.add))
                dve.nop().then_inc(hout_ready, 1)

            gate_tmp(0)
            for u in range(6, N_GATE):
                lo(u % ROUND, B_GATE + u, HALF)
                if u % 2 == 0:
                    gate_tmp(u // 2 - 2)
                    gate_add(u // 2 - 3)
            for m in range(14, 16):
                gate_tmp(m)
                gate_add(m - 1)
            gate_add(15)

        @block.tensor
        def _(pe):
            mm = nc.tensor.matmul

            def x_half(s, n, width, kk0, banks, cols, chunk_waits=False):
                pe.wait_ge(hi_ready, n + 1)
                for part in (1, 2):
                    w = WH[:, s % HI, :] if part == 1 else WL[:, s % LO, :]
                    if part == 2:
                        pe.wait_ge(lo_ready, n + 1)
                    for kk in range(2):
                        k = kk0 + kk
                        if chunk_waits and part == 1:
                            pe.wait_ge(x2_ready, k + 1)
                        for tt in range(TT):
                            for xpart in ((X1, X2) if part == 1 else (X1,)):
                                ins = mm(ps[banks + tt][:, 0:cols], xpart[:, k, tt * P:(tt + 1) * P],
                                         w[:, kk * cols:(kk + 1) * cols],
                                         start=(k == 0 and part == 1 and xpart is X1),
                                         stop=(k == KC - 1 and part == 2))
                ins.then_inc(pe_done, 1)

            for j in range(8):
                x_half(j, j, 2 * SMALL, 2 * j, 2, SMALL, chunk_waits=True)
            pe.wait_ge(consts, 2)
            pe.wait_ge(sqsum_ready, 1)
            for tt in range(TT):
                ins = mm(ps[4][:, tt:tt + 1], SQ0[:, 0, tt * P:(tt + 1) * P], ONES[:, 0:1], start=True, stop=True)
            ins.then_inc(ss_mm, 1)

            def block_pair(i, base, first_block):
                for b in range(2):
                    if isinstance(i, int):
                        need = first_block + b - 1
                        if need > 0:
                            pe.wait_ge(xblk_evac, need)
                    else:
                        pe.wait_ge(xblk_evac, i * 2 + (first_block + b - 1))
                    for j in range(8):
                        x_half(j, i * 16 + (base + b * 8 + j), HALF, 2 * j, 2 * b, 512)

            block_pair(0, B_PLAIN, 1)
            with pe.Fori(1, 3) as i:
                block_pair(i, B_PLAIN, 1)
            with pe.Fori(0, 4) as i:
                block_pair(i, B_QK, 7)

            pe.wait_ge(qi_roped, 1)
            for tt in range(TT):
                ins = nc.tensor.transpose(ps[4][:, tt * P:(tt + 1) * P], KI[:, tt, 0:128], IDENT[:, :])
            ins.then_inc(it_mm, 1)

            def qi_transpose(pr):
                if pr == 1:
                    pe.wait_ge(it_ready, 1)
                if pr >= 2:
                    pe.wait_ge(it_ready, pr)
                for tt in range(TT):
                    ins = nc.tensor.transpose(ps[5 - pr % 2][:, tt * P:(tt + 1) * P],
                                              QI[:, tt, 2 * pr:2 * pr + 2, :].rearrange("p h d -> p (h d)"), IDENT[:, :])
                ins.then_inc(it_mm, 1)

            qi_transpose(0)
            for pr in range(IH // 2):
                if pr + 1 < IH // 2:
                    qi_transpose(pr + 1)
                pe.wait_ge(it_ready, pr + 2)
                for h in (2 * pr, 2 * pr + 1):
                    if h >= 2:
                        pe.wait_ge(relu_ready, h - 1)
                    r = slice(IDIM * (h % 2), IDIM * (h % 2) + IDIM)
                    mm(ps[6 + h % 2][:, 0:128], QIT[r, pr % 2, 0:128], KIT[r, 0:128], start=True, stop=True)
                    mm(ps[6 + h % 2][:, 128:384], QIT[r, pr % 2, 128:256], KIT[r, 0:256], start=True,
                       stop=True).then_inc(lg_mm, 1)

            pe.wait_ge(xblk_evac, 15)
            pe.wait_ge(qk_normed, 4)
            pe.wait_ge(relu_ready, IH)

            def transposes(j):
                if j >= 2:
                    pe.wait_ge(qkt_ready, j - 1)
                g0, hh = (2, j) if j < 8 else (0, j - 8)
                for g in range(2):
                    for tt in range(TT):
                        off = O_QK + 2048 * (g0 + g) + tt * 1024 + hh * HD
                        ins = nc.tensor.transpose(ps[4 * (j % 2)][:, (2 * g + tt) * P:(2 * g + tt + 1) * P],
                                                  big[:, off:off + HD], IDENT[:, :])
                ins.then_inc(qk_tr, 1)

            def score_products(j):
                s = j % 2
                pe.wait_ge(qkt_ready, j + 1)
                if j >= 2:
                    pe.wait_ge(s_ready, j - 1)
                mm(ps[4 * s + 1][:, 0:128], QKT[:, s, 0:128], QKT[:, s, 256:384], start=True, stop=True)
                mm(ps[4 * s + 1][:, 128:384], QKT[:, s, 128:256], QKT[:, s, 256:512], start=True,
                   stop=True).then_inc(s_mm, 1)

            transposes(0)
            score_products(0)
            transposes(1)
            score_products(1)
            for j in range(NH):
                s = j % 2
                v = V_[0] if j < 8 else V_[8]
                hh = j % 8
                pe.wait_ge(p_ready, j + 1)
                if j >= 2:
                    pe.wait_ge(pt_ready, j - 1)
                for c in range(3):
                    ins = nc.tensor.transpose(ps[4 * s + 2][:, c * P:(c + 1) * P], PR_[:, s, c * P:(c + 1) * P], IDENT[:, :])
                ins.then_inc(pt_tr, 1)
                if j + 2 < NH:
                    transposes(j + 2)
                pe.wait_ge(pt_ready, j + 1)
                if j >= 2:
                    pe.wait_ge(o2_ready, j - 1)
                mm(ps[4 * s + 3][:, 0:256], v[:, 0, hh * HD:(hh + 1) * HD], PT_[:, s, 0:256], start=True, stop=False)
                mm(ps[4 * s + 3][:, 128:256], v[:, 1, hh * HD:(hh + 1) * HD], PT_[:, s, 256:384], start=False,
                   stop=True).then_inc(o_mm, 1)
                if j + 2 < NH:
                    score_products(j + 2)

            def unit(i, base, m, bank, xa, xb, chunks=None):
                for hf in range(2):
                    s = 2 * m + hf
                    n = i * ROUND + (base + s)
                    pe.wait_ge(hi_ready, n + 1)
                    for kk in range(8):
                        if chunks is not None:
                            pe.wait_ge(x2_ready, chunks + 8 * hf + kk + 1)
                        for xpart in (xa, xb):
                            mm(ps[bank][:, 0:T], WH[:, s % HI, kk * P:(kk + 1) * P], xpart[:, 8 * hf + kk, :],
                               start=(hf == 0 and kk == 0 and xpart is xa), stop=False)
                    pe.wait_ge(lo_ready, n + 1)
                    for kk in range(8):
                        ins = mm(ps[bank][:, 0:T], WL[:, s % LO, kk * P:(kk + 1) * P], xa[:, 8 * hf + kk, :],
                                 start=False, stop=(hf == 1 and kk == 7))
                    ins.then_inc(pe_done, 1)

            pe.wait_ge(o2_ready, NH)
            for m in range(4):
                unit(0, B_OUT, m, m, X1, X2)
            with pe.Fori(1, N_OUT // ROUND) as i:
                for m in range(4):
                    pe.wait_ge(h_ready, i * 4 + (m - 3))
                    unit(i, B_OUT, m, m, X1, X2)

            def sum_squares(bank, src):
                for tt in range(TT):
                    ins = mm(ps[bank][:, tt:tt + 1], src[:, tt * P:(tt + 1) * P], ONES[:, 0:1], start=True, stop=True)
                ins.then_inc(ss_mm, 1)

            def spread(which):
                pe.wait_ge(diag_ready, which)
                mm(ps[7][:, 0:T], ONES[:, :], TMP[:, 0, :], start=True, stop=True).then_inc(bc_mm, 1)

            def subkey_products(i, m):
                pe.wait_ge(q_ready, i * 4 + (m + 1))
                for tt in range(TT):
                    ins = mm(ps[4 + m][:, tt * P:(tt + 1) * P], QT[:, m, tt * P:(tt + 1) * P], SUBK[:, m % 2, :],
                             start=True, stop=True)
                ins.then_inc(sk_mm, 1)

            for m in range(4):
                pe.wait_ge(h_ready, KC - 3 + m)
                unit(0, B_QUERY, m, m, X1, X2, chunks=KC if m == 0 else None)
                if m == 0:
                    pe.wait_ge(sq_done, 1)
                    sum_squares(6, SQACC)
                if m == 1:
                    spread(1)
            pe.wait_ge(subk_loaded, 16)
            pe.wait_ge(rstdb_ready, 1)
            for m in range(4):
                subkey_products(0, m)
            with pe.Fori(1, N_QUERY // ROUND) as i:
                for m in range(4):
                    pe.wait_ge(q_ready, i * 4 + (m - 3))
                    unit(i, B_QUERY, m, m, X1, X2)
                pe.wait_ge(sall_ready, i * 4)
                for m in range(4):
                    subkey_products(i, m)

            def u_units(i):
                for m in range(4):
                    pe.wait_ge(tmp_ready, i * 4 + (m + 1))
                    unit(i, B_U, m, m, X1, X2)

            with pe.Fori(0, 16) as i:
                u_units(i)
            pe.wait_ge(tok_ready, 1)
            pe.wait_ge(sall_ready, 16)
            for w in range(3):
                for tt in range(TT):
                    ins = nc.tensor.transpose(ps[4 + w][:, tt * P:(tt + 1) * P], TOK[:, w, tt * P:(tt + 1) * P], IDENT[:, :])
                ins.then_inc(tok_mm, 1)
            with pe.Fori(16, 32) as i:
                u_units(i)

            pe.wait_ge(tmp_ready, 4 + NE1)
            def gates(i, b):
                pe.wait_ge(oh_ready, i * 2 + (b + 1))
                for q in range(4):
                    ins = mm(ps[b][:, q * P:(q + 1) * P], OHB[:, 4 * b + q, :], OHA[:, 4 * b + q, :], start=True, stop=True)
                ins.then_inc(g_mm, 1)

            for b in range(2):
                gates(0, b)
            with pe.Fori(1, 32) as i:
                for b in range(2):
                    pe.wait_ge(g_done, i * 2 + (b - 1))
                    gates(i, b)

            def v_units(i, peeled):
                for m in range(4):
                    pe.wait_ge(c2_ready, i * 4 + (m + 1))
                    for hf in range(2):
                        s = 2 * m + hf
                        n = i * ROUND + (B_V + s)
                        pe.wait_ge(hi_ready, n + 1)
                        for j in range(8):
                            k = 8 * hf + j
                            dst = ps[k // 2][:, (k % 2) * T:(k % 2 + 1) * T]
                            mm(dst, WH[:, s % HI, j * P:(j + 1) * P], X1[:, m, :],
                               start=(peeled and m == 0 and k % 2 == 0), stop=False, skip_group_check=True)
                            mm(dst, WH[:, s % HI, j * P:(j + 1) * P], X2[:, m, :], start=False, stop=False,
                               skip_group_check=True)
                        pe.wait_ge(lo_ready, n + 1)
                        for j in range(8):
                            k = 8 * hf + j
                            ins = mm(ps[k // 2][:, (k % 2) * T:(k % 2 + 1) * T], WL[:, s % LO, j * P:(j + 1) * P], X1[:, m, :],
                                     start=False, stop=False, skip_group_check=True)
                        ins.then_inc(pe_done, 1)

            pe.wait_ge(g_done, 64)
            v_units(0, True)
            with pe.Fori(1, N_V // ROUND) as i:
                v_units(i, False)

            pe.wait_ge(p2_ready, 1)
            pe.wait_ge(h3_ready, 8)
            for u in range(ROUND):
                n = B_PROJ + u
                pe.wait_ge(lo_ready, n + 1)
                for q in range(2):
                    m = 2 * u + q
                    if m >= 4:
                        pe.wait_ge(proj_evac, m - 3)
                    c = [slice((2 * q + kk) * P, (2 * q + kk + 1) * P) for kk in range(2)]
                    parts = [t for kk in range(2) for t in ((WH[:, u % HI, c[kk]], X1[:, 4 + kk, :]),
                                                            (WH[:, u % HI, c[kk]], X2[:, 4 + kk, :]),
                                                            (WL[:, u % LO, c[kk]], X1[:, 4 + kk, :]))]
                    for j, (a, b) in enumerate(parts):
                        ins = mm(ps[m % 4][:, 0:T], a, b, start=(j == 0), stop=(j == len(parts) - 1))
                ins.then_inc(pe_done, 1)
            pe.wait_ge(h3_ready, KC)
            pe.wait_ge(sq4_ready, KC)
            for k in range(KC):
                for tt in range(TT):
                    ins = mm(ps[6][:, tt:tt + 1], SQ4[:, k, tt * P:(tt + 1) * P], ONES[:, 0:1],
                             start=(k == 0 and tt == 0), stop=(k == KC - 1), skip_group_check=True)
            ins.then_inc(ss_mm, 1)
            pe.wait_ge(x2_ready, 3 * KC)
            for m in range(16):
                if m < 4:
                    pe.wait_ge(proj_evac, 13 + m)
                else:
                    pe.wait_ge(gtmp_ready, m - 3)
                unit(m // 4, B_GATE, m % 4, m % 4, X1, X2)
                if m == 0:
                    spread(2)


def kernel(x, p, positions, norm_mix, w_in, qk_norm_a, qk_norm_b, rel_bias, w_out, norm_ffn, peer_query,
           peer_sub_keys, peer_u, peer_v, norm_ple, ple_gate, ple_proj):
    import concourse.bacc as bacc
    from concourse.bass_utils import run_bass_kernel_spmd as run

    c = np.ascontiguousarray
    x, p, positions, w_in, w_out = (np.asarray(a) for a in (x, p, positions, w_in, w_out))
    w = w_in[0]
    A = 1024
    qa, ka, va, qb, kb, vb = (w[:, j * A:(j + 1) * A] for j in range(6))
    qi, ki, wi = w[:, 6 * A:7 * A], w[:, 7 * A:7 * A + IDIM], w[:, 7 * A + IDIM:]

    def chunks(a):
        return c(a.reshape(-1, P, a.shape[1]).transpose(1, 0, 2))

    def blocks(parts):
        a = np.concatenate(parts, axis=1).reshape(8, 2, P, -1, 512)
        return c(a.transpose(3, 0, 2, 1, 4).reshape(-1, P, HALF))

    def units(a):
        a = np.asarray(a).reshape(2, 8, P, -1, P)
        return c(a.transpose(3, 0, 2, 1, 4).reshape(-1, P, HALF))

    small = np.concatenate([ki, ki, wi], axis=1).reshape(8, 2, P, SMALL).transpose(0, 2, 1, 3).reshape(8, P, 2 * SMALL)
    q = np.arange(P)[:, None]
    k0, k1 = np.arange(P)[None, :], np.arange(T)[None, :]
    dist = np.concatenate([np.clip(q - k0, -128, 128), np.clip(q + P - k1, -128, 128)], axis=1) + 128
    arrays = {
        "xT": chunks(x[0].T),
        "pT": chunks(p[0, 0].T),
        "pos": c(positions[0].reshape(TT, P).T),
        "norms": c(np.stack([np.asarray(g)[0].reshape(KC, P).T for g in (norm_mix, norm_ffn, norm_ple)], axis=1)),
        "head_gains": c(np.broadcast_to(np.concatenate([np.asarray(qk_norm_b)[0], np.asarray(qk_norm_a)[0]])[None],
                                        (P, 4, HD))),
        "bias_a": c(np.asarray(rel_bias)[0][:, dist].transpose(1, 0, 2)),
        "subkeys": c(np.asarray(peer_sub_keys)[0].transpose(2, 0, 1)),
        "w_small": c(small),
        "w_plain": blocks([qi, vb, va]),
        "w_qk": blocks([qb, kb, qa, ka]),
        "w_out": units(w_out[0]),
        "w_query": units(peer_query[0]),
        "w_u": c(np.asarray(peer_u)[0].reshape(NE1, P, 2, 8, P).transpose(0, 2, 4, 3, 1).reshape(2 * NE1, P, HALF)),
        "w_v": c(np.asarray(peer_v)[0].reshape(NE1, P, D)),
        "w_proj": c(np.asarray(ple_proj)[0].reshape(2, P, 8, 2, P).transpose(2, 1, 3, 0, 4).reshape(8, P, 512)),
        "w_gate": units(ple_gate[0]),
    }
    nc = bacc.Bacc("TRN2", target_bir_lowering=False, num_devices=1)
    args = [nc.dram_tensor(n, a.shape, mybir.dt.from_np(a.dtype), kind="ExternalInput").ap() for n, a in arrays.items()]
    out = nc.dram_tensor("out", (P, KC, T), F32, kind="ExternalOutput").ap()
    layer_kernel(nc, *args, out)
    r = run(nc, [arrays], core_ids=[0])
    return c(np.asarray(r.results[0]["out"]).transpose(1, 0, 2).reshape(D, T).T).reshape(1, T, D)
```

```python
from contextlib import ExitStack

import numpy as np

import concourse.bass as bass
from concourse import mybir

F32 = mybir.dt.float32
F32R = mybir.dt.float32r
U32 = mybir.dt.uint32
I32 = mybir.dt.int32
ALU = mybir.AluOpType
ACT = mybir.ActivationFunctionType
AX = mybir.AxisListType

P = 128
T = 256
TT = T // P
D = 2048
KC = D // P
HD = 128
HALF = 1024
ROUND = 8
RAW, HI, LO = 4, 4, 2
NH = 16
IH, IDIM = 16, 64
CH = 64
TOPK = 64
PH, PN, PK = 8, 128, 16
NE1 = 128
EPS = 1e-6
THETA = 500000.0
SCALE = float(HD) ** -0.5
NEG = -1.0e30
TAKEN = -3.0e38
SMALL = 144

N_SMALL, N_PLAIN, N_QK = 8, 48, 64
N_OUT, N_QUERY, N_U, N_V, N_PROJ, N_GATE = 32, 32, 256, 256, 8, 32
B_SMALL = 0
B_PLAIN = B_SMALL + N_SMALL
B_QK = B_PLAIN + N_PLAIN
B_OUT = B_QK + N_QK
B_QUERY = B_OUT + N_OUT
B_U = B_QUERY + N_QUERY
B_V = B_U + N_U
B_PROJ = B_V + N_V
B_GATE = B_PROJ + N_PROJ
N_ALL = B_GATE + N_GATE


AHEAD = HI - 1
R_GATE = 17
G_MUL = 4 * R_GATE
TAIL_ORDER = [0, 1, 2, 3] + list(range(6, 16)) + [4, 5]


class Tally:

    def __init__(self, eng, sem):
        self.eng, self.sem = eng, sem
        self.total, self.i, self.per, self.k = 0, None, 0, 0

    def enter(self, i, per):
        self.i, self.per, self.k = i, per, 0

    def leave(self, n):
        assert self.k == self.per, (self.k, self.per)
        self.total += n * self.per
        self.i = None

    def mark(self, ins):
        ins.then_inc(self.sem, 1)
        if self.i is None:
            self.total += 1
            return self.total
        self.k += 1
        return self.i * self.per + (self.total + self.k)

    def now(self):
        return self.total if self.i is None else self.i * self.per + (self.total + self.k)

    def seq(self, ins):
        self.eng.wait_ge(self.sem, self.mark(ins))


def layer_kernel(nc, xT, pT, pos, norms, head_gains, bias_a, subkeys,
                 w_small, w_plain, w_qk, w_out, w_query, w_u, w_v, w_proj, w_gate, out):
    ctx = ExitStack()
    with ctx:
        def sb(name, shape, dt=F32):
            return ctx.enter_context(nc.sbuf_tensor(name, shape, dt))

        def sem(name):
            return ctx.enter_context(nc.semaphore(name))

        big = sb("big", [P, NE1 * T])
        X1 = sb("x_hi", [P, KC, T], F32R)
        X2 = sb("x_lo", [P, KC, T], F32R)
        WR = sb("w_raw", [P, RAW, HALF])
        WL = sb("w_lo", [P, LO, HALF], F32R)
        IOTA = sb("iota_row", [P, P])
        WH = sb("w_hi", [P, HI, HALF], F32R)
        IDENT = sb("ident", [P, P])
        ONES = sb("ones", [P, P])
        RSTDB = sb("rstd_bcast", [P, T])
        TMP = sb("tmp", [P, 2, T])
        OHA = RSTDB[:, :].rearrange("p (s n) -> p s n", n=P)
        OHB = TMP[:, 1, :].rearrange("p (s n) -> p s n", n=P)
        TOKT = sb("tok_t", [P, 3, T])
        GAIN = sb("gain", [P, 3, KC])
        MISC = sb("misc", [P, 24])
        TOK2 = MISC[:, 22:24]
        RSTD1 = MISC[:, 0:2]
        SSC = MISC[:, 2:4]
        VAR = MISC[:, 4:6]
        RSC = MISC[:, 6:8]
        MHALF = MISC[:, 8:24]

        def view(off, *shape, dt=None):
            n = int(np.prod(shape))
            v = big[:, off:off + n]
            if dt is not None:
                v = v.bitcast(dt)
            if len(shape) == 2:
                v = v.rearrange("p (a b) -> p a b", b=shape[1])
            elif len(shape) == 3:
                v = v.rearrange("p (a b c) -> p a b c", b=shape[1], c=shape[2])
            return v

        XT = view(24576, KC, T)
        SQ0 = view(28672, 4, HALF)
        O_QI, O_VB, O_VA, O_QK, O_KI = 0, 2048, 4096, 6144, 14336
        QI = view(O_QI, TT, IH, IDIM)
        V_ = {8: view(O_VB, TT, HALF), 0: view(O_VA, TT, HALF)}
        KI = view(O_KI, TT, SMALL)
        POSI = view(14624, TT, dt=I32)
        POSF = view(14626, TT)
        ANG = view(14628, TT, 16)
        ANGK = view(14660, TT, 16)
        ANGA = view(14692, TT, 16)
        COS = view(14724, TT, 16)
        SIN = view(14756, TT, 16)
        COS8 = view(14788, TT, 8)
        SIN8 = view(14804, TT, 8)
        HG = view(15104, 4, HD)
        SS = view(15616, 4, TT, 8)
        RS = view(15680, 4, TT * 8)
        O_ROPE = 24576
        BIAS = view(15872, 8, 384)
        MASKB = view(18944, 384)
        SCORE = view(19328, 384)
        QIT = view(19712, 2, T)
        KIT = view(20224, T)
        RELU = view(20480, 2, 384)
        QKT = view(21248, 2, 512)
        S_ = view(22272, 2, 384)
        PR_ = view(23040, 2, 384)
        PT_ = view(23808, 2, 384)
        SMX = ctx.enter_context(nc.sbuf_tensor("softmax_small", [P, 2, 4], F32))
        T8 = ctx.enter_context(nc.sbuf_tensor("top8", [P, 8], F32))
        HT = view(0, KC, T)
        SQ = view(4096, T)
        SQACC = view(4352, T)
        QT = view(16384, 4, T)
        SALL = view(17408, TT, 2 * PH, PN)
        SUBK = view(21504, 2, PN)
        SC = view(21760, 2, PN)
        SC2 = view(22016, 2, PN)
        V16 = view(22272, 2, PK)
        I16U = view(22304, 2, PK, dt=U32)
        I16F = view(22336, 2, PK)
        IJU = view(22368, 2, PK, dt=U32)
        IJF = view(22400, 2, PK)
        C16 = view(22432, PK)
        CIU = view(22448, PK, dt=U32)
        CAND = view(22528, PK, PK)
        CAND2 = view(22784, PK * PK)
        OH = view(23040, PK, PK)
        TOK = view(23552, 3, TT * PH * PK)
        IOTA16 = view(24320, PK)
        GSUM = view(24336, TT * PH)
        SQ4 = view(10240, KC, T)
        PROJ = view(4608, KC, T)
        PTIN = view(9728, 2, T)

        ps = [ctx.enter_context(nc.psum_tensor(f"bank{b}", [P, 512], F32)) for b in range(8)]
        h_scratch = nc.dram_tensor("h_scratch", (P, KC, T), F32, kind="Internal").ap()

        raw_ready = [sem(f"raw_ready{s}") for s in range(RAW)]
        hi_ready = sem("hi_ready")
        lo_ready = sem("lo_ready")
        pe_done = sem("pe_done")
        x_loaded = [sem(f"x_loaded{q}") for q in range(4)]
        pos_loaded = sem("pos_loaded")
        norms_loaded = sem("norms_loaded")
        hg_loaded = sem("head_gains_loaded")
        bias_loaded = sem("bias_loaded")
        consts = sem("consts")
        x1_ready = sem("x1_ready")
        x2_ready = sem("x2_ready")
        sq_ready = sem("sq_ready")
        sqsum_ready = sem("sqsum_ready")
        ss_mm = sem("ss_mm")
        ssc_ready = sem("ssc_ready")
        rstd_ready = sem("rstd_ready")
        diag_ready = sem("diag_ready")
        bc_mm = sem("bc_mm")
        rstdb_ready = sem("rstdb_ready")
        xblk_evac = sem("xblk_evac")
        angles_ready = sem("angles_ready")
        trig_ready = sem("trig_ready")
        qi_roped = sem("qi_roped")
        qk_normed = sem("qk_normed")
        it_mm, it_ready = sem("it_mm"), sem("it_ready")
        lg_mm, relu_ready, acc_done = sem("lg_mm"), sem("relu_ready"), sem("acc_done")
        qk_tr, qkt_ready = sem("qk_tr"), sem("qkt_ready")
        s_mm, s_ready, exp_ready, p_ready = sem("s_mm"), sem("s_ready"), sem("exp_ready"), sem("p_ready")
        pt_tr, pt_ready, o_mm, o1_ready, o2_ready = (sem(n) for n in ("pt_tr", "pt_ready", "o_mm", "o1_ready", "o2_ready"))
        ht_loaded = sem("ht_loaded")
        h_ready = sem("h_ready")
        q_ready = sem("q_ready")
        sq_done = sem("sq_done")
        h_stored = sem("h_stored")
        subk_loaded = sem("subk_loaded")
        sk_mm, sall_ready = sem("sk_mm"), sem("sall_ready")
        hn_ready = sem("hn_ready")
        act_ready = sem("act_ready")
        mul_ready = sem("mul_ready")
        ones_ready = sem("ones_ready")
        graw_ready, gexp_ready, tok_ready = sem("graw_ready"), sem("gexp_ready"), sem("tok_ready")
        tok_mm, tokt_ready = sem("tok_mm"), sem("tokt_ready")
        iota_ready = sem("iota_ready")
        oha_ready, ohb_ready = sem("oha_ready"), sem("ohb_ready")
        g_mm, g_done = sem("g_mm"), sem("g_done")
        c1_ready, c2_ready = sem("c1_ready"), sem("c2_ready")
        ht_back = sem("ht_back")
        p_loaded = sem("p_loaded")
        p1_ready, p2_ready = sem("p1_ready"), sem("p2_ready")
        h3_ready = sem("h3_ready")
        sq4_ready = sem("sq4_ready")
        proj_evac = sem("proj_evac")
        gtmp_ready, sig_ready, hout_ready = sem("gtmp_ready"), sem("sig_ready"), sem("hout_ready")
        out_stored = sem("out_stored")
        act_own, dve_own, pool_own = sem("act_own"), sem("dve_own"), sem("pool_own")

        block = ctx.enter_context(nc.Block())

        def at(i):
            return big[:, bass.ds(i * T, T)]

        @block.sync
        def _(sp):
            def load(slot, src, width):
                sp.dma_start(WR[:, slot % RAW, 0:width], src).then_inc(raw_ready[slot % RAW], 16)

            def stream(base, w, n, first=0):
                def tile(i, s):
                    sp.wait_ge(lo_ready, i * ROUND + (base + s + 1 - RAW))
                    load(s, w[bass.ds(i * ROUND + s, 1), :, :].rearrange("a p n -> p (a n)"), HALF)

                for s in range(first, ROUND if first else 0):
                    tile(0, s)
                with sp.Fori(1 if first else 0, n // ROUND) as i:
                    for s in range(ROUND):
                        tile(i, s)

            sp.dma_start(GAIN[:, :, :], norms).then_inc(norms_loaded, 16)
            sp.dma_start(XT[:, 0:4, :], xT[:, 0:4, :]).then_inc(x_loaded[0], 16)
            for s in range(2):
                load(s, w_small[s], 2 * SMALL)
            for q in range(1, 4):
                sp.dma_start(XT[:, 4 * q:4 * q + 4, :], xT[:, 4 * q:4 * q + 4, :]).then_inc(x_loaded[q], 16)
            for s in range(2, ROUND):
                if s >= RAW:
                    sp.wait_ge(lo_ready, s + 1 - RAW)
                load(s, w_small[s], 2 * SMALL)
            sp.dma_start(POSI, pos).then_inc(pos_loaded, 16)
            sp.dma_start(HG, head_gains).then_inc(hg_loaded, 16)
            sp.dma_start(BIAS, bias_a).then_inc(bias_loaded, 16)
            stream(B_PLAIN, w_plain, N_PLAIN)
            stream(B_QK, w_qk, N_QK)
            for s in range(RAW):
                sp.wait_ge(lo_ready, B_OUT + s + 1 - RAW)
                load(s, w_out[s], HALF)
            sp.wait_ge(o_mm, NH)
            sp.dma_start(HT, xT).then_inc(ht_loaded, 16)
            sp.dma_start(SUBK, subkeys).then_inc(subk_loaded, 16)
            stream(B_OUT, w_out, N_OUT, RAW)
            for s in range(RAW):
                sp.wait_ge(lo_ready, B_QUERY + s + 1 - RAW)
                load(s, w_query[s], HALF)
            sp.wait_ge(h_ready, KC)
            sp.dma_start(h_scratch, HT).then_inc(h_stored, 16)
            stream(B_QUERY, w_query, N_QUERY, RAW)
            stream(B_U, w_u, N_U)
            with sp.Fori(0, N_V // ROUND) as i:
                for s in range(ROUND):
                    sp.wait_ge(lo_ready, i * ROUND + (B_V + s + 1 - RAW))
                    load(s, w_v[bass.ds(i * (ROUND // 2) + s // 2, 1), :, (s % 2) * HALF:(s % 2 + 1) * HALF]
                         .rearrange("a p n -> p (a n)"), HALF)
            sp.wait_ge(c2_ready, NE1)
            sp.wait_ge(h_stored, 16)
            sp.dma_start(HT, h_scratch).then_inc(ht_back, 16)
            sp.dma_start(PTIN, pT).then_inc(p_loaded, 16)
            for s in range(ROUND):
                sp.wait_ge(lo_ready, B_PROJ + s + 1 - RAW)
                load(s, w_proj[s], 512)
            stream(B_GATE, w_gate, N_GATE)
            for q in range(4):
                sp.wait_ge(hout_ready, 4 * (q + 1))
                sp.dma_start(out[:, 4 * q:4 * q + 4, :], HT[:, 4 * q:4 * q + 4, :]).then_inc(out_stored, 16)
            sp.wait_ge(out_stored, 64)

        @block.gpsimd
        def _(pool):
            own = Tally(pool, pool_own)
            nc.gpsimd.memset(ONES[:, :], 1.0).then_inc(consts, 1)
            own.seq(nc.gpsimd.memset(IDENT[:, :], 0.0))
            nc.gpsimd.affine_select(out=IDENT[:, :], in_=IDENT[:, :], compare_op=ALU.not_equal, fill=1.0, base=0,
                                    pattern=[[-1, P]], channel_multiplier=1).then_inc(consts, 1)
            nc.gpsimd.iota(IOTA[:, :], pattern=[[1, P]], base=0, channel_multiplier=0,
                           allow_small_or_imprecise_dtypes=True).then_inc(iota_ready, 1)
            own.seq(nc.gpsimd.memset(MHALF, -0.5))

            def inv_rms(which):
                pool.wait_ge(ssc_ready, which)
                own.seq(nc.gpsimd.tensor_scalar(VAR, SSC, 1.0 / D, EPS, ALU.mult, ALU.add))
                nc.gpsimd.tensor_tensor(RSTD1 if which == 1 else RSC, VAR, MHALF[:, 0:2], ALU.pow).then_inc(rstd_ready, 1)

            inv_rms(1)

            def rope(t, heads, half, cos, sin, last_inc):
                x1, x2 = t[:, :, :, 0:half], t[:, :, :, half:2 * half]

                def tmp(j):
                    return view(O_ROPE + 256 * j, TT, heads, half)

                def bc(c):
                    return c.unsqueeze(2).broadcast_to([P, TT, heads, half])

                a, b, c, d = (tmp(j) for j in range(4))
                nc.gpsimd.tensor_tensor(a, x1, bc(cos), ALU.mult)
                nc.gpsimd.tensor_tensor(b, x2, bc(sin), ALU.mult)
                nc.gpsimd.tensor_tensor(c, x2, bc(cos), ALU.mult)
                own.seq(nc.gpsimd.tensor_tensor(d, x1, bc(sin), ALU.mult))
                own.mark(nc.gpsimd.tensor_tensor(x1, a, b, ALU.subtract))
                own.seq(nc.gpsimd.tensor_tensor(x2, c, d, ALU.add))
                if last_inc is not None:
                    pool.nop().then_inc(last_inc, 1)

            pool.wait_ge(x2_ready, KC)
            pool.wait_ge(sqsum_ready, 1)
            pool.wait_ge(trig_ready, 3)
            pool.wait_ge(xblk_evac, 1)
            rope(KI[:, :, 0:2 * IDIM].rearrange("p t (h d) -> p t h d", d=IDIM), 2, 8, COS8, SIN8, None)
            pool.wait_ge(xblk_evac, 3)
            rope(QI, IH, 8, COS8, SIN8, qi_roped)
            pool.wait_ge(hg_loaded, 16)
            for g in range(4):
                pool.wait_ge(xblk_evac, 7 + 2 * (g + 1))
                own.seq(nc.gpsimd.tensor_scalar(RS[:, g, :], SS[:, g, :, :].rearrange("p a b -> p (a b)"),
                                                1.0 / HD, EPS, ALU.mult, ALU.add))
                own.seq(nc.gpsimd.tensor_tensor(RS[:, g, :], RS[:, g, :], MHALF, ALU.pow))
                q3 = big[:, O_QK + 2048 * g:O_QK + 2048 * (g + 1)].rearrange("p (h d) -> p h d", d=HD)
                own.seq(nc.gpsimd.tensor_tensor(q3, q3, RS[:, g, :].unsqueeze(2).broadcast_to([P, TT * 8, HD]), ALU.mult))
                ins = nc.gpsimd.tensor_tensor(q3, q3, HG[:, g, :].unsqueeze(1).broadcast_to([P, TT * 8, HD]), ALU.mult)
                if g < 2:
                    own.seq(ins)
                    rope(big[:, O_QK + 2048 * g:O_QK + 2048 * (g + 1)].rearrange("p (t h d) -> p t h d", t=TT, d=HD),
                         8, 16, COS, SIN, qk_normed)
                else:
                    ins.then_inc(qk_normed, 1)

            pool.wait_ge(o_mm, NH)
            own.seq(nc.gpsimd.memset(SQACC, 0.0))
            with pool.Fori(0, KC) as i:
                own.enter(i, 2)
                pool.wait_ge(h_ready, i + 1)
                h = at(i)
                own.seq(nc.gpsimd.tensor_tensor(SQ, h, h, ALU.mult))
                own.seq(nc.gpsimd.tensor_tensor(SQACC, SQACC, SQ, ALU.add))
                own.leave(KC)
            pool.nop().then_inc(sq_done, 1)
            inv_rms(2)
            pool.wait_ge(rstdb_ready, 1)
            pool.wait_ge(h_stored, 16)
            pool.wait_ge(x2_ready, 2 * KC)
            nc.gpsimd.tensor_tensor(HT, HT, RSTDB[:, :].unsqueeze(1).broadcast_to([P, KC, T]), ALU.mult).then_inc(hn_ready, 1)
            nc.gpsimd.memset(big[:, 24576:NE1 * T], 1.0).then_inc(ones_ready, 1)
            pool.wait_ge(tok_mm, 3)
            nc.gpsimd.memset(big[:, G_MUL * T:24576], 1.0).then_inc(ones_ready, 1)

            def onehots(pair):
                nc.gpsimd.tensor_copy(TOK2, TOKT[:, 1, bass.ds(pair * 2, 2)])
                pool.drain()
                for q in range(2):
                    ins = nc.gpsimd.tensor_scalar(OHB[:, q, :], IOTA[:, :], TOK2[:, q:q + 1], None, ALU.is_equal)
                ins.then_inc(ohb_ready, 1)

            pool.wait_ge(tokt_ready, 3)
            onehots(0)
            with pool.Fori(1, T // 2) as i:
                pool.wait_ge(g_mm, i)
                onehots(i)
            inv_rms(3)

        @block.scalar
        def _(act):
            own = Tally(act, act_own)

            def hi(s, n, width):
                act.wait_ge(raw_ready[s % RAW], wave(n, s % RAW))
                if not (isinstance(n, int) and n < HI):
                    act.wait_ge(pe_done, n + (1 - HI))
                nc.scalar.activation(WH[:, s % HI, 0:width], WR[:, s % RAW, 0:width], ACT.Copy).then_inc(hi_ready, 1)

            def wave(n, s):
                return 16 * (n // RAW + 1) if isinstance(n, int) else (n - s) * (16 // RAW) + 16

            act.wait_ge(norms_loaded, 16)
            for j in range(8):
                for k in (2 * j, 2 * j + 1):
                    if k % 4 == 0:
                        act.wait_ge(x_loaded[k // 4], 16)
                    nc.scalar.activation(X1[:, k, :], XT[:, k, :], ACT.Copy, scale=GAIN[:, 0, k:k + 1]).then_inc(x1_ready, 1)
                hi(j, j, 2 * SMALL)
            hi(0, B_PLAIN, HALF)
            hi(1, B_PLAIN + 1, HALF)
            for q in range(4):
                nc.scalar.activation(SQ0[:, q, :], XT[:, 4 * q:4 * q + 4, :].rearrange("p a b -> p (a b)"),
                                     ACT.Square).then_inc(sq_ready, 1)
            act.wait_ge(angles_ready, 1)
            own.mark(nc.scalar.activation(SIN, ANG, ACT.Sin))
            own.mark(nc.scalar.activation(COS, ANGA, ACT.Sin))
            act.wait_ge(act_own, own.total)
            nc.scalar.activation(COS8, COS[:, :, 0:16:2], ACT.Copy).then_inc(trig_ready, 1)
            nc.scalar.activation(SIN8, SIN[:, :, 0:16:2], ACT.Copy).then_inc(trig_ready, 1)
            act.nop().then_inc(trig_ready, 1)
            hi(2, B_PLAIN + 2, HALF)
            act.wait_ge(rstd_ready, 1)
            act.wait_ge(pe_done, B_PLAIN)
            for tt in range(TT):
                ins = nc.scalar.activation(KI[:, tt, :], ps[2 + tt][:, 0:SMALL], ACT.Copy, scale=RSTD1[:, tt:tt + 1])
            ins.then_inc(xblk_evac, 1)

            def evac_block(n_end, bank, dst, squares=None):
                act.wait_ge(pe_done, n_end)
                if squares is not None:
                    act.wait_ge(act_own, own.now())
                for tt in range(TT):
                    if squares is not None:
                        for hh in range(4):
                            own.mark(nc.scalar.activation(SQJ[:, 4 * tt + hh, :], ps[bank + tt][:, hh * HD:(hh + 1) * HD], ACT.Square,
                                                 scale=RSTD1[:, tt:tt + 1], accum_out=squares(tt, hh)))
                    ins = nc.scalar.activation(dst(tt), ps[bank + tt][:, :], ACT.Copy, scale=RSTD1[:, tt:tt + 1])
                ins.then_inc(xblk_evac, 1)

            SQJ = view(28672, 8, HD)
            with act.Fori(0, 3) as i:
                for u in range(AHEAD, 16 + AHEAD):
                    hi(u % ROUND, i * 16 + (B_PLAIN + u), HALF)
                    if u % 8 == AHEAD - 1:
                        b = u // 8 - 1
                        evac_block(i * 16 + (B_PLAIN + 8 * (b + 1)), 2 * b,
                                   lambda tt: big[:, bass.ds(i * 2048 + (tt * 1024 + b * 512), 512)])
            act.wait_ge(it_mm, 1)
            nc.scalar.activation(KIT, ps[4][:, 0:T], ACT.Copy).then_inc(it_ready, 1)

            def qi_evac(pr):
                act.wait_ge(it_mm, pr + 2)
                if pr >= 2:
                    act.wait_ge(lg_mm, 2 * (pr - 1))
                nc.scalar.activation(QIT[:, pr % 2, :], ps[5 - pr % 2][:, 0:T], ACT.Copy).then_inc(it_ready, 1)

            def index_relu(h):
                act.wait_ge(lg_mm, h + 1)
                if h >= 2:
                    act.wait_ge(acc_done, h - 1)
                nc.scalar.activation(RELU[:, h % 2, :], ps[6 + h % 2][:, 0:384], ACT.Relu,
                                     scale=float(IDIM) ** -0.5 * float(IH) ** -0.5).then_inc(relu_ready, 1)

            def qk_blocks(i, index=False):
                for u in range(AHEAD, 16 + AHEAD):
                    hi(u % ROUND, i * 16 + (B_QK + u), HALF)
                    if index and u > AHEAD:
                        h = u - AHEAD - 1
                        index_relu(h)
                        if h % 2 == 0 and h + 2 < IH:
                            qi_evac(h // 2 + 1)
                    if u % 8 == AHEAD - 1:
                        b = u // 8 - 1
                        evac_block(i * 16 + (B_QK + 8 * (b + 1)), 2 * b,
                                   lambda tt: big[:, bass.ds(i * 2048 + (O_QK + tt * 1024 + b * 512), 512)],
                                   lambda tt, hh: big[:, bass.ds(i * 16 + (15616 + tt * 8 + b * 4 + hh), 1)])
                if index:
                    index_relu(IH - 1)

            qi_evac(0)
            qk_blocks(0, index=True)
            with act.Fori(1, 4) as i:
                own.enter(i - 1, 16)
                qk_blocks(i)
                own.leave(3)

            for t in range(NH + 4):
                j = t - 2
                if 0 <= j < NH:
                    s = j % 2
                    act.wait_ge(s_ready, j + 1)
                    if j >= 2:
                        act.wait_ge(pt_tr, j - 1)
                    nc.scalar.activation(PR_[:, s, 0:128], S_[:, s, 0:128], ACT.Exp, bias=SMX[:, s, 0:1],
                                         accum_out=SMX[:, s, 2:3]).then_inc(exp_ready, 1)
                    nc.scalar.activation(PR_[:, s, 128:384], S_[:, s, 128:384], ACT.Exp, bias=SMX[:, s, 1:2],
                                         accum_out=SMX[:, s, 3:4]).then_inc(exp_ready, 1)
                if t < NH:
                    act.wait_ge(qk_tr, t + 1)
                    if t >= 2:
                        act.wait_ge(s_mm, t - 1)
                    nc.scalar.activation(QKT[:, t % 2, :], ps[4 * (t % 2)][:, :], ACT.Copy).then_inc(qkt_ready, 1)
                j = t - 3
                if 0 <= j < NH:
                    act.wait_ge(pt_tr, j + 1)
                    if j >= 2:
                        act.wait_ge(o_mm, j - 1)
                    nc.scalar.activation(PT_[:, j % 2, :], ps[4 * (j % 2) + 2][:, 0:384], ACT.Copy).then_inc(pt_ready, 1)
                j = t - 4
                if 0 <= j < NH:
                    act.wait_ge(o_mm, j + 1)
                    nc.scalar.activation(X1[:, j, :], ps[4 * (j % 2) + 3][:, 0:T], ACT.Copy).then_inc(o1_ready, 1)

            with act.Fori(0, N_OUT // ROUND) as i:
                for u in range(AHEAD, ROUND + AHEAD):
                    hi(u % ROUND, i * ROUND + (B_OUT + u), HALF)
            act.wait_ge(pe_done, B_QUERY)
            for k in range(KC):
                act.wait_ge(h_ready, k + 1)
                nc.scalar.activation(X1[:, k, :], HT[:, k, :], ACT.Copy, scale=GAIN[:, 1, k:k + 1]).then_inc(x1_ready, 1)

            def s_evac(i, m):
                act.wait_ge(sk_mm, i * 4 + (m + 1))
                nc.scalar.activation(
                    SALL[:, :, bass.ds(i * 4 + m, 1), :].rearrange("p t a n -> p t (a n)"),
                    ps[4 + m][:, 0:T].rearrange("p (t n) -> p t n", t=TT), ACT.Copy).then_inc(sall_ready, 1)

            for u in range(AHEAD, ROUND + AHEAD):
                hi(u % ROUND, B_QUERY + u, HALF)
                if u == 6:
                    act.wait_ge(bc_mm, 1)
                    nc.scalar.activation(RSTDB[:, :], ps[7][:, 0:T], ACT.Copy).then_inc(rstdb_ready, 1)
            for m in range(4):
                s_evac(0, m)
            with act.Fori(1, N_QUERY // ROUND) as i:
                for u in range(AHEAD, ROUND + AHEAD):
                    hi(u % ROUND, i * ROUND + (B_QUERY + u), HALF)
                for m in range(4):
                    s_evac(i, m)

            act.wait_ge(hn_ready, 1)
            act.wait_ge(pe_done, B_U)
            for k in range(KC):
                nc.scalar.activation(X1[:, k, :], HT[:, k, :], ACT.Copy, scale=GAIN[:, 1, k:k + 1]).then_inc(x1_ready, 1)

            def gelu(i, m):
                act.wait_ge(pe_done, i * ROUND + (B_U + 2 * m + 2))
                nc.scalar.activation(at(i * 4 + m), ps[m][:, 0:T], ACT.Gelu_apprx_tanh).then_inc(act_ready, 1)

            with act.Fori(0, R_GATE - 1) as i:
                for u in range(AHEAD, ROUND + AHEAD):
                    hi(u % ROUND, i * ROUND + (B_U + u), HALF)
                    if u % 2 == 0:
                        gelu(i, u // 2 - 2)
            i = R_GATE - 1
            act.wait_ge(graw_ready, 1)
            nc.scalar.activation(TOK[:, 2, :], TOK[:, 2, :], ACT.Exp).then_inc(gexp_ready, 1)
            for u in range(AHEAD, ROUND + AHEAD):
                hi(u % ROUND, i * ROUND + B_U + u, HALF)
                if u % 2 == 0:
                    gelu(i, u // 2 - 2)
                if u == 6:
                    for w in range(3):
                        act.wait_ge(tok_mm, w + 1)
                        nc.scalar.activation(TOKT[:, w, :], ps[4 + w][:, 0:T], ACT.Copy).then_inc(tokt_ready, 1)
            with act.Fori(R_GATE, N_U // ROUND) as i:
                for u in range(AHEAD, ROUND + AHEAD):
                    hi(u % ROUND, i * ROUND + (B_U + u), HALF)
                    if u % 2 == 0:
                        m = u // 2 - 2
                        act.wait_ge(pe_done, i * ROUND + (B_U + 2 * m + 2))
                        act.wait_ge(mul_ready, i * 4 + (m - G_MUL))
                        nc.scalar.activation(TMP[:, 0, :], ps[m][:, 0:T], ACT.Gelu_apprx_tanh).then_inc(act_ready, 1)

            def c1(i, slot):
                nc.scalar.activation(X1[:, slot, :], at(i), ACT.Copy).then_inc(c1_ready, 1)

            act.wait_ge(mul_ready, NE1 - G_MUL)
            act.wait_ge(g_done, T // 4)
            c1(0, 0)
            c1(1, 1)
            with act.Fori(0, N_V // ROUND - 1) as i:
                for u in range(AHEAD, ROUND + AHEAD):
                    if u % 2 == 0:
                        c1(i * 4 + u // 2, (u // 2) % 4)
                    hi(u % ROUND, i * ROUND + (B_V + u), HALF)
            for u in range(AHEAD, ROUND + AHEAD):
                if u % 2 == 0 and u < ROUND:
                    c1(NE1 - 4 + u // 2, u // 2)
                hi(u % ROUND, B_V + N_V - ROUND + u, HALF if u < ROUND else 512)

            act.wait_ge(p_loaded, 16)
            nc.scalar.activation(X1[:, 4:6, :], PTIN, ACT.Copy).then_inc(p1_ready, 1)
            for u in range(1, ROUND + 1):
                n = u + AHEAD - 1
                hi(n % ROUND, B_PROJ + n, 512 if n < ROUND else HALF)
                act.wait_ge(pe_done, B_PROJ + u)
                for m in (2 * u - 2, 2 * u - 1):
                    nc.scalar.activation(PROJ[:, m, :], ps[m % 4][:, 0:T], ACT.Copy).then_inc(proj_evac, 1)
                for k in TAIL_ORDER[2 * u - 2:2 * u]:
                    act.wait_ge(h3_ready, k + 1)
                    nc.scalar.activation(X1[:, k, :], HT[:, k, :], ACT.Copy, scale=GAIN[:, 2, k:k + 1]).then_inc(x1_ready, 1)
                    nc.scalar.activation(SQ4[:, k, :], HT[:, k, :], ACT.Square).then_inc(sq4_ready, 1)
            for u in range(AHEAD, 6):
                hi(u % ROUND, B_GATE + u, HALF)
            act.wait_ge(bc_mm, 2)
            nc.scalar.activation(RSTDB[:, :], ps[7][:, 0:T], ACT.Copy).then_inc(rstdb_ready, 1)

            def sig(m, s):
                act.wait_ge(gtmp_ready, m + 1)
                nc.scalar.activation(TMP[:, s, :], TMP[:, s, :], ACT.Sigmoid).then_inc(sig_ready, 1)

            for u in range(6, N_GATE):
                hi(u % ROUND, B_GATE + u, HALF)
                if u % 2 == 0:
                    sig(u // 2 - 3, (u // 2 - 3) % 2)
            for m in range(13, 16):
                sig(m, m % 2)

        @block.vector
        def _(dve):
            own = Tally(dve, dve_own)

            def lo(s, n, width):
                dve.wait_ge(hi_ready, n + 1)
                if not (isinstance(n, int) and n < LO):
                    dve.wait_ge(pe_done, n + (1 - LO))
                nc.vector.tensor_tensor(WL[:, s % LO, 0:width], WR[:, s % RAW, 0:width], WH[:, s % HI, 0:width].bitcast(F32),
                                        ALU.subtract).then_inc(lo_ready, 1)

            dve.wait_ge(norms_loaded, 16)
            for j in range(8):
                for k in (2 * j, 2 * j + 1):
                    dve.wait_ge(x1_ready, k + 1)
                    nc.vector.scalar_tensor_tensor(out=X2[:, k, :], in0=XT[:, k, :], scalar=GAIN[:, 0, k:k + 1],
                                                   in1=X1[:, k, :].bitcast(F32), op0=ALU.mult,
                                                   op1=ALU.subtract).then_inc(x2_ready, 1)
                lo(j, j, 2 * SMALL)
            lo(0, B_PLAIN, HALF)
            dve.wait_ge(sq_ready, 4)
            sq = SQ0.rearrange("p a b -> p (a b)")
            for w in (2048, 1024, 512):
                own.seq(nc.vector.tensor_tensor(sq[:, 0:w], sq[:, 0:w], sq[:, w:2 * w], ALU.add))
            nc.vector.tensor_tensor(sq[:, 0:256], sq[:, 0:256], sq[:, 256:512], ALU.add).then_inc(sqsum_ready, 1)

            dve.wait_ge(pos_loaded, 16)
            own.seq(nc.vector.tensor_copy(POSF, POSI))
            freq = np.float32(1.0) / np.power(np.float32(THETA), np.arange(16, dtype=np.float32) / np.float32(16))
            for f in range(16):
                ins = nc.vector.tensor_scalar(ANG[:, :, f], POSF, float(freq[f]), None, ALU.mult)
                own.mark(ins)
            dve.wait_ge(dve_own, own.total)
            MAGIC = float(1.5 * 2 ** 23)
            own.seq(nc.vector.tensor_scalar(ANGK, ANG, float(1 / (2 * np.pi)), MAGIC, ALU.mult, ALU.add))
            own.seq(nc.vector.tensor_scalar(ANGK, ANGK, -MAGIC, None, ALU.add))
            two_pi = 2 * np.pi
            c1 = 6.28125
            c2 = float(np.float32(int((two_pi - c1) * 2 ** 21) / 2 ** 21))
            c3 = float(np.float32(two_pi - c1 - c2))
            for c in (c1, c2, c3):
                own.seq(nc.vector.scalar_tensor_tensor(out=ANG, in0=ANGK, scalar=-c, in1=ANG, op0=ALU.mult, op1=ALU.add))
            lim = float(np.float32(3.1415925))
            own.seq(nc.vector.tensor_scalar(ANG, ANG, lim, -lim, ALU.min, ALU.max))
            own.seq(nc.vector.tensor_scalar(ANGK, ANG, -1.0, None, ALU.mult))
            own.seq(nc.vector.tensor_tensor(ANGA, ANG, ANGK, ALU.max))
            nc.vector.tensor_scalar(ANGA, ANGA, -1.0, float(np.pi / 2), ALU.mult, ALU.add).then_inc(angles_ready, 1)
            dve.wait_ge(ss_mm, 1)
            nc.vector.tensor_copy(SSC, ps[4][:, 0:2]).then_inc(ssc_ready, 1)

            with dve.Fori(0, N_PLAIN // ROUND) as i:
                for u in range(1, ROUND + 1):
                    lo(u % ROUND, i * ROUND + (B_PLAIN + u), HALF)

            dve.wait_ge(bias_loaded, 16)
            own.mark(nc.vector.memset(BIAS[0:CH, :, 64:128], NEG))
            own.mark(nc.vector.memset(BIAS[0:CH, :, 320:384], NEG))
            own.mark(nc.vector.memset(SCORE, 0.0))
            dve.wait_ge(dve_own, own.total)

            def index_add(h):
                dve.wait_ge(relu_ready, h + 1)
                own.mark(nc.vector.scalar_tensor_tensor(out=SCORE[:, 0:128], in0=RELU[:, h % 2, 0:128],
                                                        scalar=KI[:, 0, 128 + h:129 + h], in1=SCORE[:, 0:128],
                                                        op0=ALU.mult, op1=ALU.add))
                own.seq(nc.vector.scalar_tensor_tensor(out=SCORE[:, 128:384], in0=RELU[:, h % 2, 128:384],
                                                       scalar=KI[:, 1, 128 + h:129 + h], in1=SCORE[:, 128:384],
                                                       op0=ALU.mult, op1=ALU.add))
                dve.nop().then_inc(acc_done, 1)

            def topk_round(r):
                a, b = (0, 128) if r < TOPK // 8 else (128, 384)
                own.seq(nc.vector.max(T8[:, :], SCORE[:, a:b]))
                own.seq(nc.vector.match_replace(SCORE[:, a:b], T8[:, :], SCORE[:, a:b], TAKEN))

            for u in range(1, 33):
                lo(u % ROUND, B_QK + u, HALF)
                if 3 <= u < 3 + IH:
                    index_add(u - 3)
                if u == 2 + IH:
                    own.mark(nc.vector.memset(SCORE[0:CH, 64:128], NEG))
                    own.seq(nc.vector.memset(SCORE[0:CH, 320:384], NEG))
                if u > 2 + IH:
                    topk_round(u - 3 - IH)
            for r in (14, 15):
                topk_round(r)
            own.seq(nc.vector.tensor_scalar(MASKB, SCORE, 0.5 * TAKEN, NEG, ALU.is_gt, ALU.mult))
            with dve.Fori(4, N_QK // ROUND) as i:
                for u in range(1, ROUND + 1):
                    lo(u % ROUND, i * ROUND + (B_QK + u), HALF)

            for t in range(NH + 5):
                j = t - 2
                if 0 <= j < NH:
                    s = j % 2
                    dve.wait_ge(exp_ready, 2 * (j + 1))
                    own.seq(nc.vector.reciprocal(SMX[:, s, 2:4], SMX[:, s, 2:4]))
                    nc.vector.tensor_scalar(PR_[:, s, 0:128], PR_[:, s, 0:128], SMX[:, s, 2:3], None, ALU.mult)
                    nc.vector.tensor_scalar(PR_[:, s, 128:384], PR_[:, s, 128:384], SMX[:, s, 3:4], None,
                                            ALU.mult).then_inc(p_ready, 1)
                j = t - 1
                if 0 <= j < NH:
                    s = j % 2
                    dve.wait_ge(s_mm, j + 1)
                    if j >= 2:
                        dve.wait_ge(exp_ready, 2 * (j - 1))
                    extra = BIAS[:, j, :] if j < 8 else MASKB
                    own.seq(nc.vector.scalar_tensor_tensor(out=S_[:, s, :], in0=ps[4 * s + 1][:, 0:384], scalar=SCALE,
                                                           in1=extra, op0=ALU.mult, op1=ALU.add))
                    nc.vector.tensor_reduce(SMX[:, s, 0:1], S_[:, s, 0:128], AX.X, ALU.max, negate=True)
                    nc.vector.tensor_reduce(SMX[:, s, 1:2], S_[:, s, 128:384], AX.X, ALU.max, negate=True).then_inc(s_ready, 1)
                j = t - 5
                if 0 <= j < NH:
                    dve.wait_ge(o1_ready, j + 1)
                    nc.vector.tensor_tensor(X2[:, j, :], ps[4 * (j % 2) + 3][:, 0:T], X1[:, j, :].bitcast(F32),
                                            ALU.subtract).then_inc(o2_ready, 1)

            def x2_part(k, gain, ready):
                dve.wait_ge(x1_ready, ready)
                nc.vector.scalar_tensor_tensor(out=X2[:, k, :], in0=HT[:, k, :], scalar=GAIN[:, gain, k:k + 1],
                                               in1=X1[:, k, :].bitcast(F32), op0=ALU.mult,
                                               op1=ALU.subtract).then_inc(x2_ready, 1)

            dve.wait_ge(ht_loaded, 16)
            with dve.Fori(0, N_OUT // ROUND) as i:
                for u in range(1, ROUND + 1):
                    lo(u % ROUND, i * ROUND + (B_OUT + u), HALF)
                    if u % 2 == 0:
                        m = u // 2 - 1
                        dve.wait_ge(pe_done, i * ROUND + (B_OUT + u))
                        h = at(i * 4 + m)
                        nc.vector.tensor_tensor(h, ps[m][:, 0:T], h, ALU.add).then_inc(h_ready, 1)
            for k in range(KC):
                x2_part(k, 1, KC + k + 1)

            def diagonals(which):
                dve.wait_ge(rstd_ready, which)
                for tt in range(TT):
                    ins = nc.vector.tensor_scalar(TMP[:, 0, tt * P:(tt + 1) * P], IDENT[:, :], RSC[:, tt:tt + 1], None, ALU.mult)
                ins.then_inc(diag_ready, 1)

            def q_evac(i, m):
                dve.wait_ge(pe_done, i * ROUND + (B_QUERY + 2 * m + 2))
                nc.vector.tensor_tensor(QT[:, m, :], ps[m][:, 0:T], RSTDB[:, :], ALU.mult).then_inc(q_ready, 1)

            for u in range(1, ROUND + 1):
                lo(u % ROUND, B_QUERY + u, HALF)
                if u == 2:
                    dve.wait_ge(ss_mm, 2)
                    nc.vector.tensor_copy(SSC, ps[6][:, 0:2]).then_inc(ssc_ready, 1)
                if u == 3:
                    diagonals(2)
                if u == 5:
                    dve.wait_ge(rstdb_ready, 1)
                    q_evac(0, 0)
                    q_evac(0, 1)
                if u in (6, 8):
                    q_evac(0, u // 2 - 1)
            with dve.Fori(1, N_QUERY // ROUND) as i:
                for u in range(1, ROUND + 1):
                    lo(u % ROUND, i * ROUND + (B_QUERY + u), HALF)
                    if u % 2 == 0:
                        m = u // 2 - 1
                        if m == 0:
                            dve.wait_ge(sk_mm, i * 4)
                        q_evac(i, m)

            def top16(values, indices, src, spare):
                dve.drain()
                nc.vector.max(values[:, 0:8], src)
                dve.drain()
                nc.vector.max_index(indices[:, 0:8], values[:, 0:8], src)
                nc.vector.match_replace(spare, values[:, 0:8], src, TAKEN)
                dve.drain()
                nc.vector.max(values[:, 8:16], spare)
                dve.drain()
                nc.vector.max_index(indices[:, 8:16], values[:, 8:16], spare)
                dve.drain()

            def route(i, step):
                if step == 0:
                    own.mark(nc.vector.tensor_copy(SC.rearrange("p a b -> p (a b)"), big[:, bass.ds(i * 256 + 17408, 256)]))
                    top16(V16[:, 0, :], I16U[:, 0, :], SC[:, 0, :], SC2[:, 0, :])
                if step == 1:
                    top16(V16[:, 1, :], I16U[:, 1, :], SC[:, 1, :], SC2[:, 1, :])
                    own.seq(nc.vector.tensor_copy(I16F, I16U))
                if step == 2:
                    own.mark(nc.vector.tensor_tensor(CAND, V16[:, 0, :].unsqueeze(2).broadcast_to([P, PK, PK]),
                                                    V16[:, 1, :].unsqueeze(1).broadcast_to([P, PK, PK]), ALU.add))
                    top16(C16, CIU, CAND.rearrange("p a b -> p (a b)"), CAND2)
                if step == 3:
                    own.seq(nc.vector.tensor_scalar(IJU[:, 0, :], CIU, 4, None, ALU.logical_shift_right))
                    own.seq(nc.vector.tensor_scalar(IJU[:, 1, :], CIU, 15, None, ALU.bitwise_and))
                    own.seq(nc.vector.tensor_copy(IJF, IJU))
                    own.seq(nc.vector.tensor_scalar(big[:, bass.ds(i * PK + (23552 + 512), PK)], C16, C16[:, 0:1], None,
                                                    ALU.subtract))
                if step in (3, 4):
                    w = step - 3
                    own.seq(nc.vector.tensor_tensor(OH, IJF[:, w, :].unsqueeze(2).broadcast_to([P, PK, PK]),
                                                    IOTA16.unsqueeze(1).broadcast_to([P, PK, PK]), ALU.is_equal))
                    own.seq(nc.vector.tensor_tensor(OH, OH, I16F[:, w, :].unsqueeze(1).broadcast_to([P, PK, PK]), ALU.mult))
                    own.seq(nc.vector.tensor_reduce(big[:, bass.ds(i * PK + (23552 + 256 * w), PK)], OH, AX.X, ALU.add))

            ROUTE_STEPS = 13
            for k in range(KC):
                x2_part(k, 1, 2 * KC + k + 1)
            for f in range(PK):
                own.mark(nc.vector.memset(IOTA16[:, f:f + 1], float(f)))
            dve.wait_ge(dve_own, own.total)
            dve.wait_ge(sall_ready, 2 * PH)
            with dve.Fori(0, 16) as i:
                own.enter(i, ROUTE_STEPS)
                for u in range(1, ROUND + 1):
                    lo(u % ROUND, i * ROUND + (B_U + u), HALF)
                    if u in (1, 3, 5, 7, 8):
                        route(i, (1, 3, 5, 7, 8).index(u))
                own.leave(16)
            dve.nop().then_inc(graw_ready, 1)
            for u in range(1, ROUND + 1):
                lo(u % ROUND, 16 * ROUND + B_U + u, HALF)
                if u == 1:
                    dve.wait_ge(gexp_ready, 1)
                    g3 = TOK[:, 2, :].rearrange("p (g k) -> p g k", k=PK)
                    own.seq(nc.vector.tensor_reduce(GSUM, g3, AX.X, ALU.add))
                    own.seq(nc.vector.reciprocal(GSUM, GSUM))
                    nc.vector.tensor_tensor(g3, g3, GSUM.unsqueeze(2).broadcast_to([P, TT * PH, PK]), ALU.mult).then_inc(tok_ready, 1)


            def apply_gates(group):
                dve.wait_ge(g_mm, group * 2 + 2)
                c = big[:, :].rearrange("p (e t) -> p t e", t=T)[:, bass.ds(group * 4, 4), :]
                bank = 4 + (group % 4 if isinstance(group, int) else m)
                nc.vector.tensor_tensor(c, ps[bank][:, :].rearrange("p (q e) -> p q e", q=4), c, ALU.mult).then_inc(g_done, 1)

            def onehots(pair):
                if not isinstance(pair, int):
                    dve.wait_ge(g_mm, pair)
                for q in range(2):
                    ins = nc.vector.tensor_scalar(OHA[:, q, :], IOTA[:, :], TOKT[:, 0, bass.ds(pair * 2 + q, 1)],
                                                  TOKT[:, 2, bass.ds(pair * 2 + q, 1)], ALU.is_equal, ALU.mult)
                ins.then_inc(oha_ready, 1)

            dve.wait_ge(tokt_ready, 3)
            dve.wait_ge(ones_ready, 2)
            dve.wait_ge(act_ready, G_MUL)
            dve.wait_ge(iota_ready, 1)
            onehots(0)
            with dve.Fori(R_GATE, N_U // ROUND) as i:
                for u in range(1, ROUND + 1):
                    lo(u % ROUND, i * ROUND + (B_U + u), HALF)
                    onehots(i * ROUND + (u - ROUND * R_GATE))
                    if u % 2 == 0:
                        m = u // 2 - 1
                        dve.wait_ge(act_ready, i * 4 + (m + 1))
                        dve.wait_ge(g_done, i * 4 + (m - G_MUL))
                        c = at(i * 4 + m)
                        nc.vector.tensor_tensor(c, c, TMP[:, 0, :], ALU.mult).then_inc(mul_ready, 1)
                        dve.wait_ge(mul_ready, i * 4 + (m + 1 - G_MUL))
                        apply_gates(i * 4 + (m - G_MUL))
            for g in range(NE1 - G_MUL, T // 4):
                for pair in (2 * g + 1, 2 * g + 2):
                    if pair < T // 2:
                        dve.wait_ge(g_mm, pair)
                        onehots(pair)
                dve.wait_ge(g_done, g)
                apply_gates(g)

            def c2(i, slot):
                dve.wait_ge(c1_ready, i + 1)
                nc.vector.tensor_tensor(X2[:, slot, :], at(i), X1[:, slot, :].bitcast(F32), ALU.subtract).then_inc(c2_ready, 1)

            c2(0, 0)
            with dve.Fori(0, N_V // ROUND - 1) as i:
                for u in range(1, ROUND + 1):
                    if u % 2 == 0:
                        c2(i * 4 + u // 2, (u // 2) % 4)
                    lo(u % ROUND, i * ROUND + (B_V + u), HALF)
            for u in range(1, ROUND + 1):
                if u % 2 == 0 and u < ROUND:
                    c2(NE1 - 4 + u // 2, u // 2)
                lo(u % ROUND, B_V + N_V - ROUND + u, HALF if u < ROUND else 512)

            dve.wait_ge(p1_ready, 1)
            nc.vector.tensor_tensor(X2[:, 4:6, :], PTIN, X1[:, 4:6, :].bitcast(F32), ALU.subtract).then_inc(p2_ready, 1)
            dve.wait_ge(ht_back, 16)
            dve.wait_ge(pe_done, B_PROJ)
            for k in range(KC):
                nc.vector.tensor_tensor(HT[:, k, :], ps[k // 2][:, (k % 2) * T:(k % 2 + 1) * T], HT[:, k, :],
                                        ALU.add).then_inc(h3_ready, 1)
            for u in range(1, ROUND + 1):
                lo(u % ROUND, B_PROJ + u, 512 if u < ROUND else HALF)
                for j in (2 * u - 2, 2 * u - 1):
                    x2_part(TAIL_ORDER[j], 2, 3 * KC + j + 1)
            dve.wait_ge(ss_mm, 3)
            nc.vector.tensor_copy(SSC, ps[6][:, 0:2]).then_inc(ssc_ready, 1)
            lo(1, B_GATE + 1, HALF)
            diagonals(3)
            for u in range(2, 6):
                lo(u, B_GATE + u, HALF)
            dve.wait_ge(rstdb_ready, 2)

            def gate_tmp(m):
                dve.wait_ge(pe_done, B_GATE + 2 * m + 2)
                nc.vector.tensor_tensor(TMP[:, m % 2, :], ps[m % 4][:, 0:T], RSTDB[:, :], ALU.mult).then_inc(gtmp_ready, 1)

            def gate_add(m):
                dve.wait_ge(sig_ready, m + 1)
                own.seq(nc.vector.tensor_tensor(TMP[:, m % 2, :], TMP[:, m % 2, :], PROJ[:, m, :], ALU.mult))
                own.seq(nc.vector.tensor_tensor(HT[:, m, :], HT[:, m, :], TMP[:, m % 2, :], ALU.add))
                dve.nop().then_inc(hout_ready, 1)

            gate_tmp(0)
            for u in range(6, N_GATE):
                lo(u % ROUND, B_GATE + u, HALF)
                if u % 2 == 0:
                    gate_tmp(u // 2 - 2)
                    gate_add(u // 2 - 3)
            for m in range(14, 16):
                gate_tmp(m)
                gate_add(m - 1)
            gate_add(15)

        @block.tensor
        def _(pe):
            mm = nc.tensor.matmul

            def x_half(s, n, width, kk0, banks, cols, chunk_waits=False):
                pe.wait_ge(hi_ready, n + 1)
                for part in (1, 2):
                    w = WH[:, s % HI, :] if part == 1 else WL[:, s % LO, :]
                    if part == 2:
                        pe.wait_ge(lo_ready, n + 1)
                    for kk in range(2):
                        k = kk0 + kk
                        if chunk_waits and part == 1:
                            pe.wait_ge(x2_ready, k + 1)
                        for tt in range(TT):
                            for xpart in ((X1, X2) if part == 1 else (X1,)):
                                ins = mm(ps[banks + tt][:, 0:cols], xpart[:, k, tt * P:(tt + 1) * P],
                                         w[:, kk * cols:(kk + 1) * cols],
                                         start=(k == 0 and part == 1 and xpart is X1),
                                         stop=(k == KC - 1 and part == 2))
                ins.then_inc(pe_done, 1)

            for j in range(8):
                x_half(j, j, 2 * SMALL, 2 * j, 2, SMALL, chunk_waits=True)
            pe.wait_ge(consts, 2)
            pe.wait_ge(sqsum_ready, 1)
            for tt in range(TT):
                ins = mm(ps[4][:, tt:tt + 1], SQ0[:, 0, tt * P:(tt + 1) * P], ONES[:, 0:1], start=True, stop=True)
            ins.then_inc(ss_mm, 1)

            def block_pair(i, base, first_block, after=None):
                for b in range(2):
                    if isinstance(i, int):
                        need = first_block + b - 1
                        if need > 0:
                            pe.wait_ge(xblk_evac, need)
                    else:
                        pe.wait_ge(xblk_evac, i * 2 + (first_block + b - 1))
                    for j in range(8):
                        x_half(j, i * 16 + (base + b * 8 + j), HALF, 2 * j, 2 * b, 512)
                        if after is not None:
                            after(8 * b + j)

            block_pair(0, B_PLAIN, 1)
            with pe.Fori(1, 3) as i:
                block_pair(i, B_PLAIN, 1)

            pe.wait_ge(qi_roped, 1)
            for tt in range(TT):
                ins = nc.tensor.transpose(ps[4][:, tt * P:(tt + 1) * P], KI[:, tt, 0:128], IDENT[:, :])
            ins.then_inc(it_mm, 1)

            def qi_transpose(pr):
                if pr == 1:
                    pe.wait_ge(it_ready, 1)
                if pr >= 2:
                    pe.wait_ge(it_ready, pr)
                for tt in range(TT):
                    ins = nc.tensor.transpose(ps[5 - pr % 2][:, tt * P:(tt + 1) * P],
                                              QI[:, tt, 2 * pr:2 * pr + 2, :].rearrange("p h d -> p (h d)"), IDENT[:, :])
                ins.then_inc(it_mm, 1)

            def index_head(h):
                pr = h // 2
                pe.wait_ge(it_ready, pr + 2)
                if h >= 2:
                    pe.wait_ge(relu_ready, h - 1)
                r = slice(IDIM * (h % 2), IDIM * (h % 2) + IDIM)
                mm(ps[6 + h % 2][:, 0:128], QIT[r, pr % 2, 0:128], KIT[r, 0:128], start=True, stop=True)
                mm(ps[6 + h % 2][:, 128:384], QIT[r, pr % 2, 128:256], KIT[r, 0:256], start=True,
                   stop=True).then_inc(lg_mm, 1)
                if h % 2 == 0 and pr + 1 < IH // 2:
                    qi_transpose(pr + 1)

            qi_transpose(0)
            block_pair(0, B_QK, 7, after=index_head)
            with pe.Fori(1, 4) as i:
                block_pair(i, B_QK, 7)

            pe.wait_ge(xblk_evac, 15)
            pe.wait_ge(qk_normed, 4)
            pe.wait_ge(relu_ready, IH)
            for t in range(NH + 4):
                if t < NH:
                    if t >= 2:
                        pe.wait_ge(qkt_ready, t - 1)
                    g0, hh = (2, t) if t < 8 else (0, t - 8)
                    for g in range(2):
                        for tt in range(TT):
                            off = O_QK + 2048 * (g0 + g) + tt * 1024 + hh * HD
                            ins = nc.tensor.transpose(ps[4 * (t % 2)][:, (2 * g + tt) * P:(2 * g + tt + 1) * P],
                                                      big[:, off:off + HD], IDENT[:, :])
                    ins.then_inc(qk_tr, 1)
                j = t - 3
                if 0 <= j < NH:
                    s = j % 2
                    pe.wait_ge(p_ready, j + 1)
                    if j >= 2:
                        pe.wait_ge(pt_ready, j - 1)
                    for c in range(3):
                        ins = nc.tensor.transpose(ps[4 * s + 2][:, c * P:(c + 1) * P], PR_[:, s, c * P:(c + 1) * P], IDENT[:, :])
                    ins.then_inc(pt_tr, 1)
                j = t - 1
                if 0 <= j < NH:
                    s = j % 2
                    pe.wait_ge(qkt_ready, j + 1)
                    if j >= 2:
                        pe.wait_ge(s_ready, j - 1)
                    mm(ps[4 * s + 1][:, 0:128], QKT[:, s, 0:128], QKT[:, s, 256:384], start=True, stop=True)
                    mm(ps[4 * s + 1][:, 128:384], QKT[:, s, 128:256], QKT[:, s, 256:512], start=True,
                       stop=True).then_inc(s_mm, 1)
                j = t - 4
                if 0 <= j < NH:
                    s = j % 2
                    v = V_[0] if j < 8 else V_[8]
                    hh = j % 8
                    pe.wait_ge(pt_ready, j + 1)
                    if j >= 2:
                        pe.wait_ge(o2_ready, j - 1)
                    mm(ps[4 * s + 3][:, 0:256], v[:, 0, hh * HD:(hh + 1) * HD], PT_[:, s, 0:256], start=True, stop=False)
                    mm(ps[4 * s + 3][:, 128:256], v[:, 1, hh * HD:(hh + 1) * HD], PT_[:, s, 256:384], start=False,
                       stop=True).then_inc(o_mm, 1)

            def unit(i, base, m, bank, xa, xb, chunks=None, after=None):
                for hf in range(2):
                    s = 2 * m + hf
                    n = i * ROUND + (base + s)
                    pe.wait_ge(hi_ready, n + 1)
                    for kk in range(8):
                        if chunks is not None:
                            pe.wait_ge(x2_ready, chunks + 8 * hf + kk + 1)
                        for xpart in (xa, xb):
                            mm(ps[bank][:, 0:T], WH[:, s % HI, kk * P:(kk + 1) * P], xpart[:, 8 * hf + kk, :],
                               start=(hf == 0 and kk == 0 and xpart is xa), stop=False)
                    pe.wait_ge(lo_ready, n + 1)
                    for kk in range(8):
                        ins = mm(ps[bank][:, 0:T], WL[:, s % LO, kk * P:(kk + 1) * P], xa[:, 8 * hf + kk, :],
                                 start=False, stop=(hf == 1 and kk == 7))
                    ins.then_inc(pe_done, 1)
                    if after is not None:
                        after(hf)

            pe.wait_ge(o2_ready, NH)
            for m in range(4):
                unit(0, B_OUT, m, m, X1, X2)
            with pe.Fori(1, N_OUT // ROUND) as i:
                for m in range(4):
                    pe.wait_ge(h_ready, i * 4 + (m - 3))
                    unit(i, B_OUT, m, m, X1, X2)

            def sum_squares(bank, src):
                for tt in range(TT):
                    ins = mm(ps[bank][:, tt:tt + 1], src[:, tt * P:(tt + 1) * P], ONES[:, 0:1], start=True, stop=True)
                ins.then_inc(ss_mm, 1)

            def spread(which):
                pe.wait_ge(diag_ready, which)
                mm(ps[7][:, 0:T], ONES[:, :], TMP[:, 0, :], start=True, stop=True).then_inc(bc_mm, 1)

            def subkey_products(i, m):
                pe.wait_ge(q_ready, i * 4 + (m + 1))
                for tt in range(TT):
                    ins = mm(ps[4 + m][:, tt * P:(tt + 1) * P], QT[:, m, tt * P:(tt + 1) * P], SUBK[:, m % 2, :],
                             start=True, stop=True)
                ins.then_inc(sk_mm, 1)

            for m in range(4):
                pe.wait_ge(h_ready, KC - 3 + m)
                unit(0, B_QUERY, m, m, X1, X2, chunks=KC if m == 0 else None)
                if m == 0:
                    pe.wait_ge(sq_done, 1)
                    sum_squares(6, SQACC)
                if m == 1:
                    spread(1)
            pe.wait_ge(subk_loaded, 16)
            pe.wait_ge(rstdb_ready, 1)
            for m in range(4):
                subkey_products(0, m)
            with pe.Fori(1, N_QUERY // ROUND) as i:
                for m in range(4):
                    pe.wait_ge(q_ready, i * 4 + (m - 3))
                    unit(i, B_QUERY, m, m, X1, X2)
                pe.wait_ge(sall_ready, i * 4)
                for m in range(4):
                    subkey_products(i, m)

            def gates(group, m, hf):
                pe.wait_ge(oha_ready, group * 2 + (hf + 1))
                pe.wait_ge(ohb_ready, group * 2 + (hf + 1))
                for q in range(2):
                    o = (2 * hf + q) * P
                    ins = mm(ps[4 + m][:, o:o + P], OHB[:, q, :], OHA[:, q, :], start=True, stop=True)
                ins.then_inc(g_mm, 1)

            for m in range(4):
                unit(0, B_U, m, m, X1, X2, chunks=2 * KC if m == 0 else None)
            with pe.Fori(1, R_GATE - 1) as i:
                for m in range(4):
                    pe.wait_ge(act_ready, i * 4 + (m - 3))
                    unit(i, B_U, m, m, X1, X2)
            for m in range(4):
                pe.wait_ge(act_ready, G_MUL - 7 + m)
                unit(R_GATE - 1, B_U, m, m, X1, X2)
                if m == 1:
                    pe.wait_ge(tok_ready, 1)
                    for w in range(3):
                        for tt in range(TT):
                            ins = nc.tensor.transpose(ps[4 + w][:, tt * P:(tt + 1) * P], TOK[:, w, tt * P:(tt + 1) * P], IDENT[:, :])
                        ins.then_inc(tok_mm, 1)
            for m in range(4):
                pe.wait_ge(act_ready, G_MUL - 3 + m)
                unit(R_GATE, B_U, m, m, X1, X2, after=lambda hf: gates(m, m, hf))
            with pe.Fori(R_GATE + 1, N_U // ROUND) as i:
                for m in range(4):
                    pe.wait_ge(act_ready, i * 4 + (m - 3))
                    pe.wait_ge(g_done, i * 4 + (m - 3 - G_MUL))
                    unit(i, B_U, m, m, X1, X2, after=lambda hf: gates(i * 4 + (m - G_MUL), m, hf))
            for g in range(NE1 - G_MUL, T // 4):
                pe.wait_ge(g_done, g - 3)
                for hf in range(2):
                    gates(g, g % 4, hf)

            def v_units(i, peeled):
                for m in range(4):
                    pe.wait_ge(c2_ready, i * 4 + (m + 1))
                    for hf in range(2):
                        s = 2 * m + hf
                        n = i * ROUND + (B_V + s)
                        pe.wait_ge(hi_ready, n + 1)
                        for j in range(8):
                            k = 8 * hf + j
                            dst = ps[k // 2][:, (k % 2) * T:(k % 2 + 1) * T]
                            mm(dst, WH[:, s % HI, j * P:(j + 1) * P], X1[:, m, :],
                               start=(peeled and m == 0 and k % 2 == 0), stop=False, skip_group_check=True)
                            mm(dst, WH[:, s % HI, j * P:(j + 1) * P], X2[:, m, :], start=False, stop=False,
                               skip_group_check=True)
                        pe.wait_ge(lo_ready, n + 1)
                        for j in range(8):
                            k = 8 * hf + j
                            ins = mm(ps[k // 2][:, (k % 2) * T:(k % 2 + 1) * T], WL[:, s % LO, j * P:(j + 1) * P], X1[:, m, :],
                                     start=False, stop=False, skip_group_check=True)
                        ins.then_inc(pe_done, 1)

            pe.wait_ge(g_done, T // 4)
            v_units(0, True)
            with pe.Fori(1, N_V // ROUND) as i:
                v_units(i, False)

            pe.wait_ge(p2_ready, 1)
            pe.wait_ge(h3_ready, 8)
            for u in range(ROUND):
                n = B_PROJ + u
                pe.wait_ge(lo_ready, n + 1)
                for q in range(2):
                    m = 2 * u + q
                    if m >= 4:
                        pe.wait_ge(proj_evac, m - 3)
                    c = [slice((2 * q + kk) * P, (2 * q + kk + 1) * P) for kk in range(2)]
                    parts = [t for kk in range(2) for t in ((WH[:, u % HI, c[kk]], X1[:, 4 + kk, :]),
                                                            (WH[:, u % HI, c[kk]], X2[:, 4 + kk, :]),
                                                            (WL[:, u % LO, c[kk]], X1[:, 4 + kk, :]))]
                    for j, (a, b) in enumerate(parts):
                        ins = mm(ps[m % 4][:, 0:T], a, b, start=(j == 0), stop=(j == len(parts) - 1))
                ins.then_inc(pe_done, 1)
            pe.wait_ge(h3_ready, KC)
            pe.wait_ge(sq4_ready, KC)
            for k in range(KC):
                for tt in range(TT):
                    ins = mm(ps[6][:, tt:tt + 1], SQ4[:, k, tt * P:(tt + 1) * P], ONES[:, 0:1],
                             start=(k == 0 and tt == 0), stop=(k == KC - 1), skip_group_check=True)
            ins.then_inc(ss_mm, 1)
            pe.wait_ge(x2_ready, 4 * KC)
            for m in range(16):
                if m < 4:
                    pe.wait_ge(proj_evac, 13 + m)
                else:
                    pe.wait_ge(gtmp_ready, m - 3)
                unit(m // 4, B_GATE, m % 4, m % 4, X1, X2)
                if m == 0:
                    spread(2)


def kernel(x, p, positions, norm_mix, w_in, qk_norm_a, qk_norm_b, rel_bias, w_out, norm_ffn, peer_query,
           peer_sub_keys, peer_u, peer_v, norm_ple, ple_gate, ple_proj):
    import concourse.bacc as bacc
    from concourse.bass_utils import run_bass_kernel_spmd as run

    c = np.ascontiguousarray
    x, p, positions, w_in, w_out = (np.asarray(a) for a in (x, p, positions, w_in, w_out))
    w = w_in[0]
    A = 1024
    qa, ka, va, qb, kb, vb = (w[:, j * A:(j + 1) * A] for j in range(6))
    qi, ki, wi = w[:, 6 * A:7 * A], w[:, 7 * A:7 * A + IDIM], w[:, 7 * A + IDIM:]

    def chunks(a):
        return c(a.reshape(-1, P, a.shape[1]).transpose(1, 0, 2))

    def blocks(parts):
        a = np.concatenate(parts, axis=1).reshape(8, 2, P, -1, 512)
        return c(a.transpose(3, 0, 2, 1, 4).reshape(-1, P, HALF))

    def units(a):
        a = np.asarray(a).reshape(2, 8, P, -1, P)
        return c(a.transpose(3, 0, 2, 1, 4).reshape(-1, P, HALF))

    small = np.concatenate([ki, ki, wi], axis=1).reshape(8, 2, P, SMALL).transpose(0, 2, 1, 3).reshape(8, P, 2 * SMALL)
    q = np.arange(P)[:, None]
    k0, k1 = np.arange(P)[None, :], np.arange(T)[None, :]
    dist = np.concatenate([np.clip(q - k0, -128, 128), np.clip(q + P - k1, -128, 128)], axis=1) + 128
    arrays = {
        "xT": chunks(x[0].T),
        "pT": chunks(p[0, 0].T),
        "pos": c(positions[0].reshape(TT, P).T),
        "norms": c(np.stack([np.asarray(g)[0].reshape(KC, P).T for g in (norm_mix, norm_ffn, norm_ple)], axis=1)),
        "head_gains": c(np.broadcast_to(np.concatenate([np.asarray(qk_norm_b)[0], np.asarray(qk_norm_a)[0]])[None],
                                        (P, 4, HD))),
        "bias_a": c(np.asarray(rel_bias)[0][:, dist].transpose(1, 0, 2)),
        "subkeys": c(np.asarray(peer_sub_keys)[0].transpose(2, 0, 1)),
        "w_small": c(small),
        "w_plain": blocks([qi, vb, va]),
        "w_qk": blocks([qb, kb, qa, ka]),
        "w_out": units(w_out[0]),
        "w_query": units(peer_query[0]),
        "w_u": c(np.asarray(peer_u)[0].reshape(NE1, P, 2, 8, P).transpose(0, 2, 4, 3, 1).reshape(2 * NE1, P, HALF)),
        "w_v": c(np.asarray(peer_v)[0].reshape(NE1, P, D)),
        "w_proj": c(np.asarray(ple_proj)[0].reshape(2, P, 8, 2, P).transpose(2, 1, 3, 0, 4).reshape(8, P, 512)),
        "w_gate": units(ple_gate[0]),
    }
    nc = bacc.Bacc("TRN2", target_bir_lowering=False, num_devices=1)
    args = [nc.dram_tensor(n, a.shape, mybir.dt.from_np(a.dtype), kind="ExternalInput").ap() for n, a in arrays.items()]
    out = nc.dram_tensor("out", (P, KC, T), F32, kind="ExternalOutput").ap()
    layer_kernel(nc, *args, out)
    r = run(nc, [arrays], core_ids=[0])
    return c(np.asarray(r.results[0]["out"]).transpose(1, 0, 2).reshape(D, T).T).reshape(1, T, D)
```

```python
from contextlib import ExitStack

import numpy as np

import concourse.bass as bass
from concourse import mybir

F32 = mybir.dt.float32
F32R = mybir.dt.float32r
U32 = mybir.dt.uint32
I32 = mybir.dt.int32
ALU = mybir.AluOpType
ACT = mybir.ActivationFunctionType
AX = mybir.AxisListType

P = 128
T = 256
TT = T // P
D = 2048
KC = D // P
HD = 128
HALF = 1024
ROUND = 8
RAW, HI, LO = 4, 4, 2
NH = 16
IH, IDIM = 16, 64
CH = 64
TOPK = 64
PH, PN, PK = 8, 128, 16
NE1 = 128
EPS = 1e-6
THETA = 500000.0
SCALE = float(HD) ** -0.5
NEG = -1.0e30
TAKEN = -3.0e38
SMALL = 144

N_SMALL, N_PLAIN, N_QK = 8, 48, 64
N_OUT, N_QUERY, N_U, N_V, N_PROJ, N_GATE = 32, 32, 256, 256, 8, 32
B_SMALL = 0
B_PLAIN = B_SMALL + N_SMALL
B_QK = B_PLAIN + N_PLAIN
B_OUT = B_QK + N_QK
B_QUERY = B_OUT + N_OUT
B_U = B_QUERY + N_QUERY
B_V = B_U + N_U
B_PROJ = B_V + N_V
B_GATE = B_PROJ + N_PROJ
N_ALL = B_GATE + N_GATE


AHEAD = HI - 1
R_GATE = 17
G_AHEAD = 2
LAST_PAIRS = 2 * 4 * (N_U // ROUND - R_GATE) + 2 * G_AHEAD + 1
G_MUL = 4 * R_GATE
PLE = KC - 2


class Tally:

    def __init__(self, eng, sem):
        self.eng, self.sem = eng, sem
        self.total, self.i, self.per, self.k = 0, None, 0, 0

    def enter(self, i, per):
        self.i, self.per, self.k = i, per, 0

    def leave(self, n):
        assert self.k == self.per, (self.k, self.per)
        self.total += n * self.per
        self.i = None

    def mark(self, ins):
        ins.then_inc(self.sem, 1)
        if self.i is None:
            self.total += 1
            return self.total
        self.k += 1
        return self.i * self.per + (self.total + self.k)

    def now(self):
        return self.total if self.i is None else self.i * self.per + (self.total + self.k)

    def seq(self, ins):
        self.eng.wait_ge(self.sem, self.mark(ins))


def layer_kernel(nc, xT, pT, pos, norms, head_gains, bias_a, subkeys,
                 w_small, w_plain, w_qk, w_out, w_query, w_u, w_v, w_proj, w_gate, out):
    ctx = ExitStack()
    with ctx:
        def sb(name, shape, dt=F32):
            return ctx.enter_context(nc.sbuf_tensor(name, shape, dt))

        def sem(name):
            return ctx.enter_context(nc.semaphore(name))

        big = sb("big", [P, NE1 * T])
        X1 = sb("x_hi", [P, KC, T], F32R)
        X2 = sb("x_lo", [P, KC, T], F32R)
        WR = sb("w_raw", [P, RAW, HALF])
        WL = sb("w_lo", [P, LO, HALF], F32R)
        IOTA = sb("iota_row", [P, P])
        WH = sb("w_hi", [P, HI, HALF], F32R)
        IDENT = sb("ident", [P, P])
        ONES = sb("ones", [P, P])
        RSTDB = sb("rstd_bcast", [P, T])
        TMP = sb("tmp", [P, 2, T])
        OHA = RSTDB[:, :].rearrange("p (s n) -> p s n", n=P)
        OHB = TMP[:, 1, :].rearrange("p (s n) -> p s n", n=P)
        TOKT = sb("tok_t", [P, 3, T])
        GAIN = sb("gain", [P, 3, KC])
        MISC = sb("misc", [P, 24])
        TOK2 = MISC[:, 22:24]
        RSTD1 = MISC[:, 0:2]
        SSC = MISC[:, 2:4]
        VAR = MISC[:, 4:6]
        RSC = MISC[:, 6:8]
        MHALF = MISC[:, 8:24]

        def view(off, *shape, dt=None):
            n = int(np.prod(shape))
            v = big[:, off:off + n]
            if dt is not None:
                v = v.bitcast(dt)
            if len(shape) == 2:
                v = v.rearrange("p (a b) -> p a b", b=shape[1])
            elif len(shape) == 3:
                v = v.rearrange("p (a b c) -> p a b c", b=shape[1], c=shape[2])
            return v

        XT = view(24576, KC, T)
        SQ0 = view(28672, 4, HALF)
        O_QI, O_VB, O_VA, O_QK, O_KI = 0, 2048, 4096, 6144, 14336
        QI = view(O_QI, TT, IH, IDIM)
        V_ = {8: view(O_VB, TT, HALF), 0: view(O_VA, TT, HALF)}
        KI = view(O_KI, TT, SMALL)
        POSI = view(14624, TT, dt=I32)
        POSF = view(14626, TT)
        ANG = view(14628, TT, 16)
        ANGK = view(14660, TT, 16)
        ANGA = view(14692, TT, 16)
        COS = view(14724, TT, 16)
        SIN = view(14756, TT, 16)
        COS8 = view(14788, TT, 8)
        SIN8 = view(14804, TT, 8)
        HG = view(15104, 4, HD)
        SS = view(15616, 4, TT, 8)
        RS = view(15680, 4, TT * 8)
        O_ROPE = 24576
        BIAS = view(15872, 8, 384)
        MASKB = view(18944, 384)
        SCORE = view(19328, 384)
        QIT = view(19712, 2, T)
        KIT = view(20224, T)
        RELU = view(20480, 2, 384)
        QKT = view(21248, 2, 512)
        S_ = view(22272, 2, 384)
        PR_ = view(23040, 2, 384)
        PT_ = view(23808, 2, 384)
        SMX = ctx.enter_context(nc.sbuf_tensor("softmax_small", [P, 2, 4], F32))
        T8 = ctx.enter_context(nc.sbuf_tensor("top8", [P, 8], F32))
        HT = view(0, KC, T)
        SQ = view(4096, T)
        SQACC = view(4352, T)
        QT = view(16384, 4, T)
        SALL = view(17408, TT, 2 * PH, PN)
        SUBK = view(21504, 2, PN)
        SC = view(21760, 2, PN)
        SC2 = view(22016, 2, PN)
        V16 = view(22272, 2, PK)
        I16U = view(22304, 2, PK, dt=U32)
        I16F = view(22336, 2, PK)
        IJU = view(22368, 2, PK, dt=U32)
        IJF = view(22400, 2, PK)
        C16 = view(22432, PK)
        CIU = view(22448, PK, dt=U32)
        CAND = view(22528, PK, PK)
        CAND2 = view(22784, PK * PK)
        OH = view(23040, 2 * PK, PK)
        TOK = view(23552, 3, TT * PH * PK)
        IOTA16 = view(24320, PK)
        GSUM = view(24336, TT * PH)
        SQ4 = view(10240, 4, T)
        PROJ = view(4608, KC, T)
        PTIN = view(9728, 2, T)

        ps = [ctx.enter_context(nc.psum_tensor(f"bank{b}", [P, 512], F32)) for b in range(8)]
        h_scratch = nc.dram_tensor("h_scratch", (P, KC, T), F32, kind="Internal").ap()

        raw_ready = [sem(f"raw_ready{s}") for s in range(RAW)]
        hi_ready = sem("hi_ready")
        lo_ready = sem("lo_ready")
        pe_done = sem("pe_done")
        x_first_loaded = sem("x_first_loaded")
        x_loaded = [sem(f"x_loaded{q}") for q in range(4)]
        pos_loaded = sem("pos_loaded")
        norms_loaded = sem("norms_loaded")
        hg_loaded = sem("head_gains_loaded")
        bias_loaded = sem("bias_loaded")
        consts = sem("consts")
        x1_ready = sem("x1_ready")
        x2_ready = sem("x2_ready")
        sq_ready = sem("sq_ready")
        sqsum_ready = sem("sqsum_ready")
        ss_mm = sem("ss_mm")
        ssc_ready = sem("ssc_ready")
        rstd_ready = sem("rstd_ready")
        diag_ready = sem("diag_ready")
        bc_mm = sem("bc_mm")
        rstdb_ready = sem("rstdb_ready")
        xblk_evac = sem("xblk_evac")
        tile0_evac = sem("tile0_evac")
        angles_ready = sem("angles_ready")
        trig_ready = sem("trig_ready")
        qi_roped = sem("qi_roped")
        qk_normed = sem("qk_normed")
        it_mm, it_ready = sem("it_mm"), sem("it_ready")
        lg_mm, relu_ready, acc_done = sem("lg_mm"), sem("relu_ready"), sem("acc_done")
        qk_tr, qkt_ready = sem("qk_tr"), sem("qkt_ready")
        s_mm, s_ready, exp_ready, p_ready = sem("s_mm"), sem("s_ready"), sem("exp_ready"), sem("p_ready")
        pt_tr, pt_ready, o_mm, o1_ready, o2_ready = (sem(n) for n in ("pt_tr", "pt_ready", "o_mm", "o1_ready", "o2_ready"))
        ht_loaded = [sem(f"ht_loaded{q}") for q in range(2)]
        h_ready = sem("h_ready")
        q_ready = sem("q_ready")
        sq_done = sem("sq_done")
        h_stored = sem("h_stored")
        subk_loaded = sem("subk_loaded")
        sk_mm, sall_ready = sem("sk_mm"), sem("sall_ready")
        hn_ready = sem("hn_ready")
        act_ready = sem("act_ready")
        mul_ready = sem("mul_ready")
        ones_ready = sem("ones_ready")
        graw_ready, gexp_ready, tok_ready = sem("graw_ready"), sem("gexp_ready"), sem("tok_ready")
        tok_mm, tokt_ready = sem("tok_mm"), sem("tokt_ready")
        iota_ready = sem("iota_ready")
        sc_ready = sem("sc_ready")
        rank_ready, index_ready = sem("rank_ready"), sem("index_ready")
        oha_ready, ohb_ready = sem("oha_ready"), sem("ohb_ready")
        g_mm, g_done = sem("g_mm"), sem("g_done")
        c1_ready, c2_ready = sem("c1_ready"), sem("c2_ready")
        ht_back = sem("ht_back")
        p_loaded = sem("p_loaded")
        p1_ready, p2_ready = sem("p1_ready"), sem("p2_ready")
        h3_ready = sem("h3_ready")
        sq4_ready = sem("sq4_ready")
        proj_evac = sem("proj_evac")
        gtmp_ready, sig_ready, hout_ready = sem("gtmp_ready"), sem("sig_ready"), sem("hout_ready")
        out_stored = sem("out_stored")
        act_own, dve_own, pool_own = sem("act_own"), sem("dve_own"), sem("pool_own")

        block = ctx.enter_context(nc.Block())

        def at(i):
            return big[:, bass.ds(i * T, T)]

        @block.sync
        def _(sp):
            def load(slot, src, width):
                sp.dma_start(WR[:, slot % RAW, 0:width], src).then_inc(raw_ready[slot % RAW], 16)

            def stream(base, w, n, first=0):
                def tile(i, s):
                    sp.wait_ge(lo_ready, i * ROUND + (base + s + 1 - RAW))
                    load(s, w[bass.ds(i * ROUND + s, 1), :, :].rearrange("a p n -> p (a n)"), HALF)

                for s in range(first, ROUND if first else 0):
                    tile(0, s)
                with sp.Fori(1 if first else 0, n // ROUND) as i:
                    for s in range(ROUND):
                        tile(i, s)

            sp.dma_start(GAIN[:, :, :], norms).then_inc(norms_loaded, 16)
            sp.dma_start(XT[:, 0:1, :], xT[:, 0:1, :]).then_inc(x_first_loaded, 16)
            for q in range(4):
                k = slice(1 if q == 0 else 4 * q, 4 * q + 4)
                sp.dma_start(XT[:, k, :], xT[:, k, :]).then_inc(x_loaded[q], 16)
                for j in (2 * q, 2 * q + 1):
                    sp.dma_start(WR[:, q, (j % 2) * 2 * SMALL:(j % 2 + 1) * 2 * SMALL], w_small[j]).then_inc(raw_ready[q], 16)
            sp.dma_start(POSI, pos).then_inc(pos_loaded, 16)
            sp.dma_start(HG, head_gains).then_inc(hg_loaded, 16)
            sp.dma_start(BIAS, bias_a).then_inc(bias_loaded, 16)
            stream(B_PLAIN, w_plain, N_PLAIN)
            stream(B_QK, w_qk, N_QK)
            for s in range(6):
                sp.wait_ge(lo_ready, B_OUT + s + 1 - RAW)
                load(s, w_out[s], HALF)
                if s == RAW - 1:
                    sp.wait_ge(it_mm, 1 + IH // 2)
                    sp.dma_start(HT[:, 0:8, :], xT[:, 0:8, :]).then_inc(ht_loaded[0], 16)
            sp.wait_ge(o_mm, NH)
            sp.dma_start(HT[:, 8:16, :], xT[:, 8:16, :]).then_inc(ht_loaded[1], 16)
            sp.dma_start(SUBK, subkeys).then_inc(subk_loaded, 16)
            stream(B_OUT, w_out, N_OUT, 6)
            for s in range(ROUND):
                sp.wait_ge(lo_ready, B_QUERY + s + 1 - RAW)
                load(s, w_query[s], HALF)
                if s == 4:
                    sp.wait_ge(h_ready, KC)
                if s >= 4:
                    k = slice(4 * (s - 4), 4 * (s - 4) + 4)
                    sp.dma_start(h_scratch[:, k, :], HT[:, k, :]).then_inc(h_stored, 16)
            stream(B_QUERY, w_query, N_QUERY, ROUND)
            stream(B_U, w_u, N_U)
            def stream_v(first, end):
                with sp.Fori(first, end) as i:
                    for s in range(ROUND):
                        sp.wait_ge(lo_ready, i * ROUND + (B_V + s + 1 - RAW))
                        load(s, w_v[bass.ds(i * (ROUND // 2) + s // 2, 1), :, (s % 2) * HALF:(s % 2 + 1) * HALF]
                             .rearrange("a p n -> p (a n)"), HALF)

            stream_v(0, 16)
            sp.wait_ge(c2_ready, 40)
            sp.wait_ge(h_stored, 64)
            sp.dma_start(HT, h_scratch).then_inc(ht_back, 16)
            sp.dma_start(PTIN, pT).then_inc(p_loaded, 16)
            stream_v(16, N_V // ROUND)
            for s in range(ROUND):
                sp.wait_ge(lo_ready, B_PROJ + s + 1 - RAW)
                load(s, w_proj[s], 512)
            stream(B_GATE, w_gate, N_GATE)
            done = 0
            for k in (4, 8, 12, 14, 15, 16):
                sp.wait_ge(hout_ready, k)
                sp.dma_start(out[:, done:k, :], HT[:, done:k, :]).then_inc(out_stored, 16)
                done = k
            sp.wait_ge(out_stored, 6 * 16)

        @block.gpsimd
        def _(pool):
            own = Tally(pool, pool_own)
            nc.gpsimd.memset(ONES[:, :], 1.0).then_inc(consts, 1)
            own.seq(nc.gpsimd.memset(IDENT[:, :], 0.0))
            nc.gpsimd.affine_select(out=IDENT[:, :], in_=IDENT[:, :], compare_op=ALU.not_equal, fill=1.0, base=0,
                                    pattern=[[-1, P]], channel_multiplier=1).then_inc(consts, 1)
            nc.gpsimd.iota(IOTA[:, :], pattern=[[1, P]], base=0, channel_multiplier=0,
                           allow_small_or_imprecise_dtypes=True).then_inc(iota_ready, 1)
            own.seq(nc.gpsimd.memset(MHALF, -0.5))

            def inv_rms(which):
                pool.wait_ge(ssc_ready, which)
                own.seq(nc.gpsimd.tensor_scalar(VAR, SSC, 1.0 / D, EPS, ALU.mult, ALU.add))
                nc.gpsimd.tensor_tensor(RSTD1 if which == 1 else RSC, VAR, MHALF[:, 0:2], ALU.pow).then_inc(rstd_ready, 1)

            inv_rms(1)

            def rope(t, heads, half, cos, sin, last_inc):
                x1, x2 = t[:, :, :, 0:half], t[:, :, :, half:2 * half]

                def tmp(j):
                    return view(O_ROPE + 256 * j, TT, heads, half)

                def bc(c):
                    return c.unsqueeze(2).broadcast_to([P, TT, heads, half])

                a, b, c, d = (tmp(j) for j in range(4))
                nc.gpsimd.tensor_tensor(a, x1, bc(cos), ALU.mult)
                nc.gpsimd.tensor_tensor(b, x2, bc(sin), ALU.mult)
                nc.gpsimd.tensor_tensor(c, x2, bc(cos), ALU.mult)
                own.seq(nc.gpsimd.tensor_tensor(d, x1, bc(sin), ALU.mult))
                own.mark(nc.gpsimd.tensor_tensor(x1, a, b, ALU.subtract))
                own.seq(nc.gpsimd.tensor_tensor(x2, c, d, ALU.add))
                if last_inc is not None:
                    pool.nop().then_inc(last_inc, 1)

            pool.wait_ge(x2_ready, KC)
            pool.wait_ge(sqsum_ready, 1)
            pool.wait_ge(trig_ready, 3)
            pool.wait_ge(xblk_evac, 1)
            rope(KI[:, :, 0:2 * IDIM].rearrange("p t (h d) -> p t h d", d=IDIM), 2, 8, COS8, SIN8, None)
            pool.wait_ge(xblk_evac, 3)
            rope(QI, IH, 8, COS8, SIN8, qi_roped)
            pool.wait_ge(hg_loaded, 16)
            for g in range(4):
                for b in range(2):
                    pool.wait_ge(xblk_evac, 7 + 2 * g + b + 1)
                    rs = RS[:, g, :].rearrange("p (t h) -> p t h", t=TT)[:, :, 4 * b:4 * b + 4]
                    ex = MHALF[:, 0:8].rearrange("p (t h) -> p t h", t=TT)
                    own.seq(nc.gpsimd.tensor_scalar(rs, SS[:, g, :, 4 * b:4 * b + 4], 1.0 / HD, EPS, ALU.mult, ALU.add))
                    own.seq(nc.gpsimd.tensor_tensor(rs, rs, ex, ALU.pow))
                    q4 = big[:, O_QK + 2048 * g:O_QK + 2048 * (g + 1)].rearrange("p (t h d) -> p t h d", t=TT, d=HD)[:, :, 4 * b:4 * b + 4, :]
                    for tt in range(TT):
                        own.mark(nc.gpsimd.tensor_tensor(q4[:, tt, :, :], q4[:, tt, :, :],
                                                         rs[:, tt, :].unsqueeze(2).broadcast_to([P, 4, HD]), ALU.mult))
                    pool.wait_ge(pool_own, own.now())
                    for tt in range(TT):
                        own.mark(nc.gpsimd.tensor_tensor(q4[:, tt, :, :], q4[:, tt, :, :],
                                                         HG[:, g, :].unsqueeze(1).broadcast_to([P, 4, HD]), ALU.mult))
                    pool.wait_ge(pool_own, own.now())
                    if g >= 2:
                        rope(q4, 4, 16, COS, SIN, qk_normed)
                    else:
                        pool.nop().then_inc(qk_normed, 1)

            pool.wait_ge(o_mm, NH)
            own.seq(nc.gpsimd.memset(SQACC, 0.0))
            with pool.Fori(0, KC) as i:
                own.enter(i, 2)
                pool.wait_ge(h_ready, i + 1)
                h = at(i)
                own.seq(nc.gpsimd.tensor_tensor(SQ, h, h, ALU.mult))
                own.seq(nc.gpsimd.tensor_tensor(SQACC, SQACC, SQ, ALU.add))
                own.leave(KC)
            pool.nop().then_inc(sq_done, 1)
            inv_rms(2)
            pool.wait_ge(rstdb_ready, 1)
            pool.wait_ge(h_stored, 64)
            pool.wait_ge(x2_ready, 2 * KC)
            nc.gpsimd.tensor_tensor(HT, HT, RSTDB[:, :].unsqueeze(1).broadcast_to([P, KC, T]), ALU.mult).then_inc(hn_ready, 1)
            nc.gpsimd.memset(big[:, 24576:NE1 * T], 1.0).then_inc(ones_ready, 1)
            own.mark(nc.gpsimd.iota(IOTA16, pattern=[[1, PK]], base=0, channel_multiplier=0,
                                    allow_small_or_imprecise_dtypes=True))
            pool.wait_ge(pool_own, own.now())

            def fetch_scores(i):
                nc.gpsimd.tensor_copy(SC.rearrange("p a b -> p (a b)"), big[:, bass.ds(i * 256 + 17408, 256)]).then_inc(sc_ready, 1)

            def rank_products(i):
                pool.wait_ge(rank_ready, i + 1)
                oh = OH.rearrange("p (w r) n -> p w r n", w=2)
                for w in range(2):
                    ins = nc.gpsimd.tensor_tensor(oh[:, w, :, :], oh[:, w, :, :],
                                                  I16F[:, w, :].unsqueeze(1).broadcast_to([P, PK, PK]), ALU.mult)
                ins.then_inc(index_ready, 1)

            pool.wait_ge(sall_ready, 2 * PH)
            fetch_scores(0)
            with pool.Fori(0, 15) as i:
                rank_products(i)
                fetch_scores(i + 1)
            rank_products(15)

            def onehots(pair):
                nc.gpsimd.tensor_copy(TOK2, TOKT[:, 1, bass.ds(pair * 2, 2)])
                pool.drain()
                for q in range(2):
                    ins = nc.gpsimd.tensor_scalar(OHB[:, q, :], IOTA[:, :], TOK2[:, q:q + 1], None, ALU.is_equal)
                ins.then_inc(ohb_ready, 1)

            pool.wait_ge(tokt_ready, 3)
            part = (24576 - G_MUL * T) // 4
            for pair in range(4):
                if pair > 0:
                    pool.wait_ge(g_mm, pair)
                onehots(pair)
                o = G_MUL * T + part * pair
                nc.gpsimd.memset(big[:, o:o + part], 1.0).then_inc(ones_ready, 1)
            with pool.Fori(4, LAST_PAIRS) as i:
                pool.wait_ge(g_mm, i)
                onehots(i)
            for b in range(KC // 2):
                pool.wait_ge(h3_ready, b + 1)
                h = HT[:, 2 * b:2 * b + 2, :]
                if b == 0:
                    own.seq(nc.gpsimd.tensor_tensor(SQ4[:, 0:2, :], h, h, ALU.mult))
                else:
                    own.seq(nc.gpsimd.tensor_tensor(SQ4[:, 2:4, :], h, h, ALU.mult))
                    own.seq(nc.gpsimd.tensor_tensor(SQ4[:, 0:2, :], SQ4[:, 0:2, :], SQ4[:, 2:4, :], ALU.add))
            pool.nop().then_inc(sq4_ready, 1)
            inv_rms(3)

        @block.scalar
        def _(act):
            own = Tally(act, act_own)

            def hi(s, n, width):
                act.wait_ge(raw_ready[s % RAW], wave(n, s % RAW))
                if not (isinstance(n, int) and n < HI):
                    act.wait_ge(pe_done, n + (1 - HI))
                nc.scalar.activation(WH[:, s % HI, 0:width], WR[:, s % RAW, 0:width], ACT.Copy).then_inc(hi_ready, 1)

            def wave(n, s):
                return 16 * (n // RAW + 1) if isinstance(n, int) else (n - s) * (16 // RAW) + 16

            def small(j):
                return WR[:, j // 2, (j % 2) * 2 * SMALL:(j % 2 + 1) * 2 * SMALL]

            act.wait_ge(norms_loaded, 16)
            for j in range(8):
                for k in (2 * j, 2 * j + 1):
                    if k == 0:
                        act.wait_ge(x_first_loaded, 16)
                    elif k % 4 == 0 or k == 1:
                        act.wait_ge(x_loaded[k // 4], 16)
                    nc.scalar.activation(X1[:, k, :], XT[:, k, :], ACT.Copy, scale=GAIN[:, 0, k:k + 1]).then_inc(x1_ready, 1)
                act.wait_ge(raw_ready[j // 2], 32)
                if j >= HI:
                    act.wait_ge(pe_done, j + 1 - HI)
                nc.scalar.activation(WH[:, j % HI, 0:2 * SMALL], small(j), ACT.Copy).then_inc(hi_ready, 1)
                if j % 2 == 1:
                    q = j // 2
                    nc.scalar.activation(SQ0[:, q, :], XT[:, 4 * q:4 * q + 4, :].rearrange("p a b -> p (a b)"),
                                         ACT.Square).then_inc(sq_ready, 1)
            hi(0, B_PLAIN, HALF)
            hi(1, B_PLAIN + 1, HALF)
            hi(2, B_PLAIN + 2, HALF)
            def evac_block(n_end, bank, dst, squares=None, tiles=(0, 1)):
                act.wait_ge(pe_done, n_end)
                if squares is not None:
                    act.wait_ge(act_own, own.now())
                for tt in tiles:
                    if squares is not None:
                        for hh in range(4):
                            own.mark(nc.scalar.activation(SQJ[:, 4 * tt + hh, :], ps[bank + tt][:, hh * HD:(hh + 1) * HD], ACT.Square,
                                                 scale=RSTD1[:, tt:tt + 1], accum_out=squares(tt, hh)))
                    ins = nc.scalar.activation(dst(tt), ps[bank + tt][:, :], ACT.Copy, scale=RSTD1[:, tt:tt + 1])
                ins.then_inc(xblk_evac if tiles[-1] == TT - 1 else tile0_evac, 1)

            SQJ = view(28672, 8, HD)
            def plain_blocks(i, first=False):
                for u in range(AHEAD, 16 + AHEAD):
                    hi(u % ROUND, i * 16 + (B_PLAIN + u), HALF)
                    if first and u == 5:
                        act.wait_ge(rstd_ready, 1)
                        for tt in range(TT):
                            ins = nc.scalar.activation(KI[:, tt, :], ps[2 + tt][:, 0:SMALL], ACT.Copy, scale=RSTD1[:, tt:tt + 1])
                        ins.then_inc(xblk_evac, 1)
                    if first and u == 9:
                        act.wait_ge(angles_ready, 1)
                        own.mark(nc.scalar.activation(SIN, ANG, ACT.Sin))
                        own.mark(nc.scalar.activation(COS, ANGA, ACT.Sin))
                        act.wait_ge(act_own, own.total)
                        nc.scalar.activation(COS8, COS[:, :, 0:16:2], ACT.Copy).then_inc(trig_ready, 1)
                        nc.scalar.activation(SIN8, SIN[:, :, 0:16:2], ACT.Copy).then_inc(trig_ready, 1)
                        act.nop().then_inc(trig_ready, 1)
                    if u % 8 == AHEAD - 1:
                        b = u // 8 - 1
                        evac_block(i * 16 + (B_PLAIN + 8 * (b + 1)), 2 * b,
                                   lambda tt: big[:, bass.ds(i * 2048 + (tt * 1024 + b * 512), 512)])

            plain_blocks(0, first=True)
            with act.Fori(1, 3) as i:
                plain_blocks(i)

            act.wait_ge(it_mm, 1)
            nc.scalar.activation(KIT, ps[4][:, 0:T], ACT.Copy).then_inc(it_ready, 1)

            def qi_evac(pr):
                act.wait_ge(it_mm, pr + 2)
                if pr >= 2:
                    act.wait_ge(lg_mm, 2 * (pr - 1))
                nc.scalar.activation(QIT[:, pr % 2, :], ps[5 - pr % 2][:, 0:T], ACT.Copy).then_inc(it_ready, 1)

            def index_relu(h):
                act.wait_ge(lg_mm, h + 1)
                if h >= 2:
                    act.wait_ge(acc_done, h - 1)
                nc.scalar.activation(RELU[:, h % 2, :], ps[6 + h % 2][:, 0:384], ACT.Relu,
                                     scale=float(IDIM) ** -0.5 * float(IH) ** -0.5).then_inc(relu_ready, 1)

            def qk_evac(i, b, tiles=(0, 1)):
                evac_block(i * 16 + (B_QK + 8 * (b + 1)), 2 * b,
                           lambda tt: big[:, bass.ds(i * 2048 + (O_QK + tt * 1024 + b * 512), 512)],
                           lambda tt, hh: big[:, bass.ds(i * 16 + (15616 + tt * 8 + b * 4 + hh), 1)], tiles)

            def qk_blocks(i, index=False, last=False):
                for u in range(AHEAD, 16 + AHEAD):
                    hi(u % ROUND, i * 16 + (B_QK + u), HALF)
                    if index and u > AHEAD:
                        h = u - AHEAD - 1
                        index_relu(h)
                        if h % 2 == 0 and h + 2 < IH:
                            qi_evac(h // 2 + 1)
                    if u % 8 == AHEAD - 1 and not (last and u > ROUND + AHEAD):
                        qk_evac(i, u // 8 - 1)
                if index:
                    index_relu(IH - 1)

            qi_evac(0)
            qk_blocks(0, index=True)
            with act.Fori(1, 3) as i:
                own.enter(i - 1, 16)
                qk_blocks(i)
                own.leave(2)
            qk_blocks(3, last=True)
            hi(3, B_OUT + 3, HALF)

            for t in range(NH + 4):
                j = t - 2
                if 0 <= j < NH:
                    s = j % 2
                    act.wait_ge(s_ready, j + 1)
                    if j >= 2:
                        act.wait_ge(pt_tr, j - 1)
                    nc.scalar.activation(PR_[:, s, 0:128], S_[:, s, 0:128], ACT.Exp, bias=SMX[:, s, 0:1],
                                         accum_out=SMX[:, s, 2:3]).then_inc(exp_ready, 1)
                    nc.scalar.activation(PR_[:, s, 128:384], S_[:, s, 128:384], ACT.Exp, bias=SMX[:, s, 1:2],
                                         accum_out=SMX[:, s, 3:4]).then_inc(exp_ready, 1)
                if t < NH:
                    act.wait_ge(qk_tr, t + 1)
                    if t >= 2:
                        act.wait_ge(s_mm, t - 1)
                    nc.scalar.activation(QKT[:, t % 2, :], ps[4 * (t % 2)][:, :], ACT.Copy).then_inc(qkt_ready, 1)
                if t == 2:
                    qk_evac(3, 1, (0,))
                j = t - 3
                if 0 <= j < NH:
                    act.wait_ge(pt_tr, j + 1)
                    if j >= 2:
                        act.wait_ge(o_mm, j - 1)
                    nc.scalar.activation(PT_[:, j % 2, :], ps[4 * (j % 2) + 2][:, 0:384], ACT.Copy).then_inc(pt_ready, 1)
                if t == 3:
                    qk_evac(3, 1, (1,))
                j = t - 4
                if 0 <= j < NH:
                    act.wait_ge(o_mm, j + 1)
                    nc.scalar.activation(X1[:, j, :], ps[4 * (j % 2) + 3][:, 0:T], ACT.Copy).then_inc(o1_ready, 1)
                if t >= NH + 2:
                    hi(t - NH + 2, B_OUT + t - NH + 2, HALF)

            for u in range(6, ROUND + AHEAD):
                hi(u % ROUND, B_OUT + u, HALF)
            with act.Fori(1, N_OUT // ROUND - 1) as i:
                for u in range(AHEAD, ROUND + AHEAD):
                    hi(u % ROUND, i * ROUND + (B_OUT + u), HALF)

            def x1_part(k):
                act.wait_ge(h_ready, k + 1)
                nc.scalar.activation(X1[:, k, :], HT[:, k, :], ACT.Copy, scale=GAIN[:, 1, k:k + 1]).then_inc(x1_ready, 1)

            for u in range(AHEAD, ROUND + AHEAD):
                hi(u % ROUND, B_QUERY - ROUND + u, HALF)
                if u >= 7:
                    act.wait_ge(pe_done, B_QUERY - 4)
                    x1_part(2 * u - 14)
                    x1_part(2 * u - 13)

            def s_evac(i, m):
                act.wait_ge(sk_mm, i * 4 + (m + 1))
                nc.scalar.activation(
                    SALL[:, :, bass.ds(i * 4 + m, 1), :].rearrange("p t a n -> p t (a n)"),
                    ps[4 + m][:, 0:T].rearrange("p (t n) -> p t n", t=TT), ACT.Copy).then_inc(sall_ready, 1)

            act.wait_ge(pe_done, B_QUERY)
            for u in range(AHEAD, ROUND + AHEAD):
                hi(u % ROUND, B_QUERY + u, HALF)
                for k in {3: range(8, 12), 4: range(12, KC)}.get(u, ()):
                    x1_part(k)
                if u == 6:
                    act.wait_ge(bc_mm, 1)
                    nc.scalar.activation(RSTDB[:, :], ps[7][:, 0:T], ACT.Copy).then_inc(rstdb_ready, 1)
            for m in range(4):
                s_evac(0, m)
            with act.Fori(1, N_QUERY // ROUND - 1) as i:
                for u in range(AHEAD, ROUND + AHEAD):
                    hi(u % ROUND, i * ROUND + (B_QUERY + u), HALF)
                for m in range(4):
                    s_evac(i, m)
            act.wait_ge(hn_ready, 1)
            for u in range(AHEAD, ROUND + AHEAD):
                hi(u % ROUND, B_U - ROUND + u, HALF)
                if u >= 7:
                    act.wait_ge(pe_done, B_U - 4)
                    x1_part(2 * u - 14)
                    x1_part(2 * u - 13)
            act.wait_ge(pe_done, B_U)
            for m in range(4):
                s_evac(N_QUERY // ROUND - 1, m)

            def gelu(i, m, halves=None):
                act.wait_ge(pe_done, i * ROUND + (B_U + (halves or 2 * m + 2)))
                nc.scalar.activation(at(i * 4 + m), ps[m][:, 0:T], ACT.Gelu_apprx_tanh).then_inc(act_ready, 1)

            for u in range(AHEAD, ROUND + AHEAD):
                hi(u % ROUND, B_U + u, HALF)
                for k in {3: range(8, 12), 4: range(12, KC)}.get(u, ()):
                    x1_part(k)
                if u >= 7:
                    gelu(0, u - 7, halves=u - 2)
            with act.Fori(1, R_GATE - 1) as i:
                for u in range(AHEAD, ROUND + AHEAD):
                    hi(u % ROUND, i * ROUND + (B_U + u), HALF)
                    if u % 2 == 0:
                        gelu(i, u // 2 - 2)
            i = R_GATE - 1
            act.wait_ge(graw_ready, 1)
            nc.scalar.activation(TOK[:, 2, :], TOK[:, 2, :], ACT.Exp).then_inc(gexp_ready, 1)
            for u in range(AHEAD, ROUND + AHEAD):
                hi(u % ROUND, i * ROUND + B_U + u, HALF)
                if u % 2 == 0:
                    gelu(i, u // 2 - 2)
                if u == 4:
                    for w in range(3):
                        act.wait_ge(tok_mm, w + 1)
                        nc.scalar.activation(TOKT[:, w, :], ps[4 + w][:, 0:T], ACT.Copy).then_inc(tokt_ready, 1)
            with act.Fori(R_GATE, N_U // ROUND) as i:
                for u in range(AHEAD, ROUND + AHEAD):
                    hi(u % ROUND, i * ROUND + (B_U + u), HALF)
                    if u % 2 == 0:
                        m = u // 2 - 2
                        act.wait_ge(pe_done, i * ROUND + (B_U + 2 * m + 2))
                        act.wait_ge(mul_ready, i * 4 + (m - G_MUL))
                        nc.scalar.activation(TMP[:, 0, :], ps[m][:, 0:T], ACT.Gelu_apprx_tanh).then_inc(act_ready, 1)

            def c1(i, slot):
                nc.scalar.activation(X1[:, slot, :], at(i), ACT.Copy).then_inc(c1_ready, 1)

            act.wait_ge(mul_ready, NE1 - G_MUL)
            act.wait_ge(g_done, T // 4)
            c1(0, 0)
            c1(1, 1)
            with act.Fori(0, N_V // ROUND - 1) as i:
                for u in range(AHEAD, ROUND + AHEAD):
                    if u % 2 == 0:
                        c1(i * 4 + u // 2, (u // 2) % 4)
                    hi(u % ROUND, i * ROUND + (B_V + u), HALF)
            act.wait_ge(p_loaded, 16)
            nc.scalar.activation(X1[:, PLE:KC, :], PTIN, ACT.Copy).then_inc(p1_ready, 1)
            for u in range(AHEAD, ROUND + AHEAD):
                if u % 2 == 0 and u < ROUND:
                    c1(NE1 - 4 + u // 2, u // 2)
                hi(u % ROUND, B_V + N_V - ROUND + u, HALF if u < ROUND else 512)

            for u in range(1, ROUND + 1):
                n = u + AHEAD - 1
                hi(n % ROUND, B_PROJ + n, 512 if n < ROUND else HALF)
                act.wait_ge(pe_done, B_PROJ + u)
                nc.scalar.activation(PROJ[:, 2 * u - 2:2 * u, :].rearrange("p a t -> p (a t)"), ps[(u - 1) % 4][:, :],
                                     ACT.Copy).then_inc(proj_evac, 1)
                for k in (2 * u - 4, 2 * u - 3) if 2 <= u < ROUND else (12, 13, 14, 15) if u == ROUND else ():
                    act.wait_ge(h3_ready, k // 2 + 1)
                    nc.scalar.activation(X1[:, k, :], HT[:, k, :], ACT.Copy, scale=GAIN[:, 2, k:k + 1]).then_inc(x1_ready, 1)
            def sig(m, s):
                act.wait_ge(gtmp_ready, m + 1)
                nc.scalar.activation(TMP[:, s, :], TMP[:, s, :], ACT.Sigmoid).then_inc(sig_ready, 1)

            for u in range(AHEAD, N_GATE):
                hi(u % ROUND, B_GATE + u, HALF)
                if u == 9:
                    act.wait_ge(bc_mm, 2)
                    nc.scalar.activation(RSTDB[:, :], ps[7][:, 0:T], ACT.Copy).then_inc(rstdb_ready, 1)
                if 9 <= u < 13:
                    sig(u - 9, (u - 9) % 2)
                if u >= 14 and u % 2 == 0:
                    sig(u // 2 - 3, (u // 2 - 3) % 2)
            for m in range(13, 16):
                sig(m, m % 2)

        @block.vector
        def _(dve):
            own = Tally(dve, dve_own)

            def lo(s, n, width):
                dve.wait_ge(hi_ready, n + 1)
                if not (isinstance(n, int) and n < LO):
                    dve.wait_ge(pe_done, n + (1 - LO))
                nc.vector.tensor_tensor(WL[:, s % LO, 0:width], WR[:, s % RAW, 0:width], WH[:, s % HI, 0:width].bitcast(F32),
                                        ALU.subtract).then_inc(lo_ready, 1)

            dve.wait_ge(norms_loaded, 16)
            for j in range(8):
                for k in (2 * j, 2 * j + 1):
                    dve.wait_ge(x1_ready, k + 1)
                    nc.vector.scalar_tensor_tensor(out=X2[:, k, :], in0=XT[:, k, :], scalar=GAIN[:, 0, k:k + 1],
                                                   in1=X1[:, k, :].bitcast(F32), op0=ALU.mult,
                                                   op1=ALU.subtract).then_inc(x2_ready, 1)
                dve.wait_ge(hi_ready, j + 1)
                if j >= LO:
                    dve.wait_ge(pe_done, j + 1 - LO)
                nc.vector.tensor_tensor(WL[:, j % LO, 0:2 * SMALL], WR[:, j // 2, (j % 2) * 2 * SMALL:(j % 2 + 1) * 2 * SMALL],
                                        WH[:, j % HI, 0:2 * SMALL].bitcast(F32), ALU.subtract).then_inc(lo_ready, 1)
            sq = SQ0.rearrange("p a b -> p (a b)")
            dve.wait_ge(sq_ready, 4)
            lo(0, B_PLAIN, HALF)
            own.seq(nc.vector.tensor_tensor(sq[:, 0:2048], sq[:, 0:2048], sq[:, 2048:4096], ALU.add))
            lo(1, B_PLAIN + 1, HALF)
            for w in (1024, 512):
                own.seq(nc.vector.tensor_tensor(sq[:, 0:w], sq[:, 0:w], sq[:, w:2 * w], ALU.add))
            nc.vector.tensor_tensor(sq[:, 0:256], sq[:, 0:256], sq[:, 256:512], ALU.add).then_inc(sqsum_ready, 1)

            def angles(step):
                if step == 0:
                    dve.wait_ge(pos_loaded, 16)
                    own.seq(nc.vector.tensor_copy(POSF, POSI))
                    freq = np.float32(1.0) / np.power(np.float32(THETA), np.arange(16, dtype=np.float32) / np.float32(16))
                    for f in range(16):
                        own.mark(nc.vector.tensor_scalar(ANG[:, :, f], POSF, float(freq[f]), None, ALU.mult))
                    dve.wait_ge(dve_own, own.total)
                    MAGIC = float(1.5 * 2 ** 23)
                    own.seq(nc.vector.tensor_scalar(ANGK, ANG, float(1 / (2 * np.pi)), MAGIC, ALU.mult, ALU.add))
                    own.seq(nc.vector.tensor_scalar(ANGK, ANGK, -MAGIC, None, ALU.add))
                if step == 1:
                    two_pi = 2 * np.pi
                    c1 = 6.28125
                    c2 = float(np.float32(int((two_pi - c1) * 2 ** 21) / 2 ** 21))
                    c3 = float(np.float32(two_pi - c1 - c2))
                    for c in (c1, c2, c3):
                        own.seq(nc.vector.scalar_tensor_tensor(out=ANG, in0=ANGK, scalar=-c, in1=ANG, op0=ALU.mult, op1=ALU.add))
                    lim = float(np.float32(3.1415925))
                    own.seq(nc.vector.tensor_scalar(ANG, ANG, lim, -lim, ALU.min, ALU.max))
                    own.seq(nc.vector.tensor_scalar(ANGK, ANG, -1.0, None, ALU.mult))
                    own.seq(nc.vector.tensor_tensor(ANGA, ANG, ANGK, ALU.max))
                    nc.vector.tensor_scalar(ANGA, ANGA, -1.0, float(np.pi / 2), ALU.mult, ALU.add).then_inc(angles_ready, 1)

            for u in range(2, ROUND + 1):
                lo(u % ROUND, B_PLAIN + u, HALF)
                if u == 3:
                    dve.wait_ge(ss_mm, 1)
                    nc.vector.tensor_copy(SSC, ps[4][:, 0:2]).then_inc(ssc_ready, 1)
                if u in (4, 6):
                    angles(u // 2 - 2)
            with dve.Fori(1, N_PLAIN // ROUND) as i:
                for u in range(1, ROUND + 1):
                    lo(u % ROUND, i * ROUND + (B_PLAIN + u), HALF)

            dve.wait_ge(bias_loaded, 16)
            own.mark(nc.vector.memset(BIAS[0:CH, :, 64:128], NEG))
            own.mark(nc.vector.memset(BIAS[0:CH, :, 320:384], NEG))
            own.mark(nc.vector.memset(SCORE, 0.0))
            dve.wait_ge(dve_own, own.total)

            def index_add(h):
                dve.wait_ge(relu_ready, h + 1)
                own.mark(nc.vector.scalar_tensor_tensor(out=SCORE[:, 0:128], in0=RELU[:, h % 2, 0:128],
                                                        scalar=KI[:, 0, 128 + h:129 + h], in1=SCORE[:, 0:128],
                                                        op0=ALU.mult, op1=ALU.add))
                own.seq(nc.vector.scalar_tensor_tensor(out=SCORE[:, 128:384], in0=RELU[:, h % 2, 128:384],
                                                       scalar=KI[:, 1, 128 + h:129 + h], in1=SCORE[:, 128:384],
                                                       op0=ALU.mult, op1=ALU.add))
                dve.nop().then_inc(acc_done, 1)

            def topk_round(r):
                a, b = (0, 128) if r < TOPK // 8 else (128, 384)
                own.seq(nc.vector.max(T8[:, :], SCORE[:, a:b]))
                own.seq(nc.vector.match_replace(SCORE[:, a:b], T8[:, :], SCORE[:, a:b], TAKEN))

            for u in range(1, 33):
                lo(u % ROUND, B_QK + u, HALF)
                if 3 <= u < 3 + IH:
                    index_add(u - 3)
                if u == 2 + IH:
                    own.mark(nc.vector.memset(SCORE[0:CH, 64:128], NEG))
                    own.seq(nc.vector.memset(SCORE[0:CH, 320:384], NEG))
                if u > 2 + IH:
                    topk_round(u - 3 - IH)
            for r in (14, 15):
                topk_round(r)
            own.seq(nc.vector.tensor_scalar(MASKB, SCORE, 0.5 * TAKEN, NEG, ALU.is_gt, ALU.mult))
            with dve.Fori(4, N_QK // ROUND) as i:
                for u in range(1, ROUND + 1):
                    lo(u % ROUND, i * ROUND + (B_QK + u), HALF)

            lo(1, B_OUT + 1, HALF)

            for t in range(NH + 5):
                j = t - 1
                if 0 <= j < NH:
                    s = j % 2
                    dve.wait_ge(s_mm, j + 1)
                    if j >= 2:
                        dve.wait_ge(exp_ready, 2 * (j - 1))
                    extra = BIAS[:, j, :] if j < 8 else MASKB
                    own.seq(nc.vector.scalar_tensor_tensor(out=S_[:, s, :], in0=ps[4 * s + 1][:, 0:384], scalar=SCALE,
                                                           in1=extra, op0=ALU.mult, op1=ALU.add))
                    nc.vector.tensor_reduce(SMX[:, s, 0:1], S_[:, s, 0:128], AX.X, ALU.max, negate=True)
                    nc.vector.tensor_reduce(SMX[:, s, 1:2], S_[:, s, 128:384], AX.X, ALU.max, negate=True).then_inc(s_ready, 1)
                j = t - 2
                if 0 <= j < NH:
                    s = j % 2
                    dve.wait_ge(exp_ready, 2 * (j + 1))
                    own.seq(nc.vector.reciprocal(SMX[:, s, 2:4], SMX[:, s, 2:4]))
                    nc.vector.tensor_scalar(PR_[:, s, 0:128], PR_[:, s, 0:128], SMX[:, s, 2:3], None, ALU.mult)
                    nc.vector.tensor_scalar(PR_[:, s, 128:384], PR_[:, s, 128:384], SMX[:, s, 3:4], None,
                                            ALU.mult).then_inc(p_ready, 1)
                j = t - 5
                if 0 <= j < NH:
                    dve.wait_ge(o1_ready, j + 1)
                    nc.vector.tensor_tensor(X2[:, j, :], ps[4 * (j % 2) + 3][:, 0:T], X1[:, j, :].bitcast(F32),
                                            ALU.subtract).then_inc(o2_ready, 1)
                if t in (NH + 1, NH + 2):
                    lo(t - NH + 1, B_OUT + t - NH + 1, HALF)

            def x2_part(k, gain, ready):
                dve.wait_ge(x1_ready, ready)
                nc.vector.scalar_tensor_tensor(out=X2[:, k, :], in0=HT[:, k, :], scalar=GAIN[:, gain, k:k + 1],
                                               in1=X1[:, k, :].bitcast(F32), op0=ALU.mult,
                                               op1=ALU.subtract).then_inc(x2_ready, 1)

            def out_round(i, first, part=None):
                for u in range(first, ROUND + 1):
                    lo(u % ROUND, i * ROUND + (B_OUT + u), HALF)
                    if part is not None and u >= 5:
                        part(2 * u - 10)
                        part(2 * u - 9)
                    if u >= 5:
                        m = u - 5
                        dve.wait_ge(pe_done, i * ROUND + (B_OUT + u))
                        h = at(i * 4 + m)
                        nc.vector.tensor_tensor(h, ps[m][:, 0:T], h, ALU.add).then_inc(h_ready, 1)

            dve.wait_ge(ht_loaded[0], 16)
            out_round(0, 4)
            dve.wait_ge(ht_loaded[1], 16)
            with dve.Fori(1, N_OUT // ROUND - 1) as i:
                out_round(i, 1)
            out_round(N_OUT // ROUND - 1, 1, lambda k: x2_part(k, 1, KC + k + 1))

            def diagonals(which):
                dve.wait_ge(rstd_ready, which)
                for tt in range(TT):
                    ins = nc.vector.tensor_scalar(TMP[:, 0, tt * P:(tt + 1) * P], IDENT[:, :], RSC[:, tt:tt + 1], None, ALU.mult)
                ins.then_inc(diag_ready, 1)

            def q_evac(i, m, halves):
                dve.wait_ge(pe_done, i * ROUND + (B_QUERY + halves))
                nc.vector.tensor_tensor(QT[:, m, :], ps[m][:, 0:T], RSTDB[:, :], ALU.mult).then_inc(q_ready, 1)

            for u in range(1, ROUND + 1):
                lo(u % ROUND, B_QUERY + u, HALF)
                for k in {1: range(8, 12), 2: range(12, KC)}.get(u, ()):
                    x2_part(k, 1, KC + k + 1)
                if u == 2:
                    dve.wait_ge(ss_mm, 2)
                    nc.vector.tensor_copy(SSC, ps[6][:, 0:2]).then_inc(ssc_ready, 1)
                if u == 3:
                    diagonals(2)
                if u == 5:
                    dve.wait_ge(rstdb_ready, 1)
                if u >= 5:
                    q_evac(0, u - 5, halves=u)
            def query_round(i, part=None):
                for u in range(1, ROUND + 1):
                    lo(u % ROUND, i * ROUND + (B_QUERY + u), HALF)
                    if u == 5:
                        dve.wait_ge(sk_mm, i * 4)
                    if u >= 5:
                        if part is not None:
                            part(2 * u - 10)
                            part(2 * u - 9)
                        q_evac(i, u - 5, halves=u)

            with dve.Fori(1, N_QUERY // ROUND - 1) as i:
                query_round(i)
            query_round(N_QUERY // ROUND - 1, lambda k: x2_part(k, 1, 2 * KC + k + 1))

            def top8(values, indices, src, spare):
                dve.drain()
                nc.vector.max(values, src)
                dve.drain()
                nc.vector.max_index(indices, values, src)
                if spare is not None:
                    nc.vector.match_replace(spare, values, src, TAKEN)
                dve.drain()

            def route(i, step):
                if step in (0, 1):
                    w = step
                    if step == 1:
                        top8(V16[:, 0, 8:16], I16U[:, 0, 8:16], SC2[:, 0, :], None)
                    top8(V16[:, w, 0:8], I16U[:, w, 0:8], SC[:, w, :], SC2[:, w, :])
                if step == 2:
                    top8(V16[:, 1, 8:16], I16U[:, 1, 8:16], SC2[:, 1, :], None)
                    own.seq(nc.vector.tensor_copy(I16F, I16U))
                if step == 3:
                    own.mark(nc.vector.tensor_tensor(CAND, V16[:, 0, :].unsqueeze(2).broadcast_to([P, PK, PK]),
                                                    V16[:, 1, :].unsqueeze(1).broadcast_to([P, PK, PK]), ALU.add))
                    top8(C16[:, 0:8], CIU[:, 0:8], CAND.rearrange("p a b -> p (a b)"), CAND2)
                if step == 4:
                    top8(C16[:, 8:16], CIU[:, 8:16], CAND2, None)

                oh = OH.rearrange("p (w r) n -> p w r n", w=2)
                if step == 5:
                    own.seq(nc.vector.tensor_scalar(IJU[:, 0, :], CIU, 4, None, ALU.logical_shift_right))
                    own.seq(nc.vector.tensor_scalar(IJU[:, 1, :], CIU, 15, None, ALU.bitwise_and))
                    own.seq(nc.vector.tensor_copy(IJF, IJU))
                    own.seq(nc.vector.tensor_scalar(big[:, bass.ds(i * PK + (23552 + 512), PK)], C16, C16[:, 0:1], None,
                                                    ALU.subtract))
                    nc.vector.tensor_tensor(oh, IJF.unsqueeze(3).broadcast_to([P, 2, PK, PK]),
                                            IOTA16.unsqueeze(1).unsqueeze(1).broadcast_to([P, 2, PK, PK]),
                                            ALU.is_equal).then_inc(rank_ready, 1)
                if step == 7:
                    dve.wait_ge(index_ready, i + 1)
                    own.seq(nc.vector.tensor_reduce(TOK[:, 0:2, bass.ds(i * PK, PK)], oh, AX.X, ALU.add))

            ROUTE_STEPS = 7
            dve.wait_ge(sc_ready, 1)
            for u in range(1, ROUND + 1):
                lo(u % ROUND, B_U + u, HALF)
                for k in {2: range(8, 12), 3: range(12, KC)}.get(u, ()):
                    x2_part(k, 1, 2 * KC + k + 1)
                route(0, u - 1)
            with dve.Fori(1, 16) as i:
                own.enter(i - 1, ROUTE_STEPS)
                for u in range(1, ROUND + 1):
                    if u == 1:
                        dve.wait_ge(sc_ready, i + 1)
                    lo(u % ROUND, i * ROUND + (B_U + u), HALF)
                    route(i, u - 1)
                own.leave(15)
            def onehots(pair):
                if not (isinstance(pair, int) and pair == 0):
                    dve.wait_ge(g_mm, pair)
                if isinstance(pair, int) and pair >= LAST_PAIRS:
                    for q in range(2):
                        ins = nc.vector.tensor_scalar(OHB[:, q, :], IOTA[:, :], TOKT[:, 1, pair * 2 + q:pair * 2 + q + 1],
                                                      None, ALU.is_equal)
                    ins.then_inc(ohb_ready, 1)
                for q in range(2):
                    ins = nc.vector.tensor_scalar(OHA[:, q, :], IOTA[:, :], TOKT[:, 0, bass.ds(pair * 2 + q, 1)],
                                                  TOKT[:, 2, bass.ds(pair * 2 + q, 1)], ALU.is_equal, ALU.mult)
                ins.then_inc(oha_ready, 1)

            dve.nop().then_inc(graw_ready, 1)
            for u in range(1, ROUND + 1):
                lo(u % ROUND, 16 * ROUND + B_U + u, HALF)
                if u == 1:
                    dve.wait_ge(gexp_ready, 1)
                    g3 = TOK[:, 2, :].rearrange("p (g k) -> p g k", k=PK)
                    own.seq(nc.vector.tensor_reduce(GSUM, g3, AX.X, ALU.add))
                    own.seq(nc.vector.reciprocal(GSUM, GSUM))
                    nc.vector.tensor_tensor(g3, g3, GSUM.unsqueeze(2).broadcast_to([P, TT * PH, PK]), ALU.mult).then_inc(tok_ready, 1)
                if u == 4:
                    dve.wait_ge(tokt_ready, 3)
                    dve.wait_ge(iota_ready, 1)
                if u >= 4:
                    onehots(u - 4)

            def apply_gates(group, bank):
                dve.wait_ge(g_mm, group * 2 + 2)
                c = big[:, :].rearrange("p (e t) -> p t e", t=T)[:, bass.ds(group * 4, 4), :]
                nc.vector.tensor_tensor(c, ps[bank][:, :].rearrange("p (q e) -> p q e", q=4), c, ALU.mult).then_inc(g_done, 1)

            dve.wait_ge(ones_ready, 5)
            dve.wait_ge(act_ready, G_MUL)
            for g in range(G_AHEAD):
                if g > 0:
                    dve.wait_ge(g_done, g)
                apply_gates(g, 6 + g)
            with dve.Fori(R_GATE, N_U // ROUND) as i:
                for u in range(1, ROUND + 1):
                    lo(u % ROUND, i * ROUND + (B_U + u), HALF)
                    onehots(i * ROUND + (u + 2 * G_AHEAD - ROUND * R_GATE))
                    if u % 2 == 0:
                        m = u // 2 - 1
                        group = i * 4 + (m + G_AHEAD - G_MUL)
                        dve.wait_ge(act_ready, i * 4 + (m + 1))
                        dve.wait_ge(g_done, group)
                        c = at(i * 4 + m)
                        nc.vector.tensor_tensor(c, c, TMP[:, 0, :], ALU.mult).then_inc(mul_ready, 1)
                        dve.wait_ge(mul_ready, i * 4 + (m + 1 - G_MUL))
                        apply_gates(group, 4 + m)
            for g in range(NE1 - G_MUL + G_AHEAD, T // 4):
                for pair in (2 * g + 1, 2 * g + 2):
                    if pair < T // 2:
                        onehots(pair)
                dve.wait_ge(g_done, g)
                apply_gates(g, 4 + (g - G_AHEAD) % 4)

            def c2(i, slot):
                dve.wait_ge(c1_ready, i + 1)
                nc.vector.tensor_tensor(X2[:, slot, :], at(i), X1[:, slot, :].bitcast(F32), ALU.subtract).then_inc(c2_ready, 1)

            c2(0, 0)
            with dve.Fori(0, N_V // ROUND - 1) as i:
                for u in range(1, ROUND + 1):
                    if u % 2 == 0:
                        c2(i * 4 + u // 2, (u // 2) % 4)
                    lo(u % ROUND, i * ROUND + (B_V + u), HALF)
            dve.wait_ge(p1_ready, 1)
            nc.vector.tensor_tensor(X2[:, PLE:KC, :], PTIN, X1[:, PLE:KC, :].bitcast(F32), ALU.subtract).then_inc(p2_ready, 1)
            for u in range(1, ROUND + 1):
                if u % 2 == 0 and u < ROUND:
                    c2(NE1 - 4 + u // 2, u // 2)
                lo(u % ROUND, B_V + N_V - ROUND + u, HALF if u < ROUND else 512)

            dve.wait_ge(ht_back, 16)
            dve.wait_ge(pe_done, B_PROJ)

            def h3(b):
                h = HT[:, 2 * b:2 * b + 2, :].rearrange("p a t -> p (a t)")
                nc.vector.tensor_tensor(h, ps[b][:, :], h, ALU.add).then_inc(h3_ready, 1)

            for b in range(4):
                h3(b)
            for u in range(1, ROUND + 1):
                lo(u % ROUND, B_PROJ + u, 512 if u < ROUND else HALF)
                if u <= 4:
                    h3(3 + u)
                for k in (2 * u - 4, 2 * u - 3) if 2 <= u < ROUND else (12, 13, 14, 15) if u == ROUND else ():
                    x2_part(k, 2, 3 * KC + k + 1)
            def gate_tmp(m):
                dve.wait_ge(pe_done, B_GATE + (m + 5 if m < 4 else 2 * m + 2))
                nc.vector.tensor_tensor(TMP[:, m % 2, :], ps[m % 4][:, 0:T], RSTDB[:, :], ALU.mult).then_inc(gtmp_ready, 1)

            def gate_add(m):
                dve.wait_ge(sig_ready, m + 1)
                own.seq(nc.vector.tensor_tensor(TMP[:, m % 2, :], TMP[:, m % 2, :], PROJ[:, m, :], ALU.mult))
                own.seq(nc.vector.tensor_tensor(HT[:, m, :], HT[:, m, :], TMP[:, m % 2, :], ALU.add))
                dve.nop().then_inc(hout_ready, 1)

            for u in range(1, N_GATE):
                lo(u % ROUND, B_GATE + u, HALF)
                if u == 4:
                    dve.wait_ge(ss_mm, 3)
                    nc.vector.tensor_copy(SSC, ps[6][:, 0:2]).then_inc(ssc_ready, 1)
                if u == 5:
                    diagonals(3)
                if u == 7:
                    dve.wait_ge(rstdb_ready, 2)
                if 7 <= u < 11:
                    gate_tmp(u - 7)
                if 8 <= u < 12:
                    gate_add(u - 8)
                if u >= 12 and u % 2 == 0:
                    gate_tmp(u // 2 - 2)
                    if u >= 14:
                        gate_add(u // 2 - 3)
            for m in range(14, 16):
                gate_tmp(m)
                gate_add(m - 1)
            gate_add(15)

        @block.tensor
        def _(pe):
            mm = nc.tensor.matmul

            def x_half(s, n, width, kk0, banks, cols, chunk_waits=False):
                pe.wait_ge(hi_ready, n + 1)
                for part in (1, 2):
                    w = WH[:, s % HI, :] if part == 1 else WL[:, s % LO, :]
                    if part == 2:
                        pe.wait_ge(lo_ready, n + 1)
                    for kk in range(2):
                        k = kk0 + kk
                        if chunk_waits and part == 1:
                            pe.wait_ge(x2_ready, k + 1)
                        for tt in range(TT):
                            dst, rhs = ps[banks + tt][:, 0:cols], w[:, kk * cols:(kk + 1) * cols]
                            if cols < T:
                                dst = ps[banks + tt][:, 0:2 * cols].rearrange("p (r c) -> p r c", r=2)
                                rhs = rhs.unsqueeze(1).broadcast_to([P, 2, cols])
                            for xpart in ((X1, X2) if part == 1 else (X1,)):
                                ins = mm(dst, xpart[:, k, tt * P:(tt + 1) * P], rhs,
                                         start=(k == 0 and part == 1 and xpart is X1),
                                         stop=(k == KC - 1 and part == 2))
                ins.then_inc(pe_done, 1)

            for j in range(8):
                x_half(j, j, 2 * SMALL, 2 * j, 2, SMALL, chunk_waits=True)

            def input_squares(e):
                if e == 2:
                    pe.wait_ge(consts, 2)
                    pe.wait_ge(sqsum_ready, 1)
                    for tt in range(TT):
                        ins = mm(ps[4][:, tt:tt + 1], SQ0[:, 0, tt * P:(tt + 1) * P], ONES[:, 0:1], start=True, stop=True)
                    ins.then_inc(ss_mm, 1)

            def block_pair(i, base, first_block, after=None):
                for b in range(2):
                    if isinstance(i, int):
                        need = first_block + b - 1
                        if need > 0:
                            pe.wait_ge(xblk_evac, need)
                    else:
                        pe.wait_ge(xblk_evac, i * 2 + (first_block + b - 1))
                    for j in range(8):
                        x_half(j, i * 16 + (base + b * 8 + j), HALF, 2 * j, 2 * b, 512)
                        if after is not None:
                            after(8 * b + j)

            block_pair(0, B_PLAIN, 1, after=input_squares)
            with pe.Fori(1, 3) as i:
                block_pair(i, B_PLAIN, 1)

            pe.wait_ge(qi_roped, 1)
            for tt in range(TT):
                ins = nc.tensor.transpose(ps[4][:, tt * P:(tt + 1) * P], KI[:, tt, 0:128], IDENT[:, :])
            ins.then_inc(it_mm, 1)

            def qi_transpose(pr):
                if pr == 1:
                    pe.wait_ge(it_ready, 1)
                if pr >= 2:
                    pe.wait_ge(it_ready, pr)
                for tt in range(TT):
                    ins = nc.tensor.transpose(ps[5 - pr % 2][:, tt * P:(tt + 1) * P],
                                              QI[:, tt, 2 * pr:2 * pr + 2, :].rearrange("p h d -> p (h d)"), IDENT[:, :])
                ins.then_inc(it_mm, 1)

            def index_head(h):
                pr = h // 2
                pe.wait_ge(it_ready, pr + 2)
                if h >= 2:
                    pe.wait_ge(relu_ready, h - 1)
                r = slice(IDIM * (h % 2), IDIM * (h % 2) + IDIM)
                mm(ps[6 + h % 2][:, 0:128], QIT[r, pr % 2, 0:128], KIT[r, 0:128], start=True, stop=True)
                mm(ps[6 + h % 2][:, 128:384], QIT[r, pr % 2, 128:256], KIT[r, 0:256], start=True,
                   stop=True).then_inc(lg_mm, 1)
                if h % 2 == 0 and pr + 1 < IH // 2:
                    qi_transpose(pr + 1)

            qi_transpose(0)
            block_pair(0, B_QK, 7, after=index_head)
            with pe.Fori(1, 4) as i:
                block_pair(i, B_QK, 7)

            def half(n, s, bank, hf, xa, xb, chunks=None):
                pe.wait_ge(hi_ready, n + 1)
                for kk in range(8):
                    if chunks is not None:
                        pe.wait_ge(x2_ready, chunks + 8 * hf + kk + 1)
                    for xpart in (xa, xb):
                        mm(ps[bank][:, 0:T], WH[:, s % HI, kk * P:(kk + 1) * P], xpart[:, 8 * hf + kk, :],
                           start=(hf == 0 and kk == 0 and xpart is xa), stop=False)
                pe.wait_ge(lo_ready, n + 1)
                for kk in range(8):
                    ins = mm(ps[bank][:, 0:T], WL[:, s % LO, kk * P:(kk + 1) * P], xa[:, 8 * hf + kk, :],
                             start=False, stop=(hf == 1 and kk == 7))
                ins.then_inc(pe_done, 1)

            def unit(i, base, m, bank, xa, xb, after=None):
                for hf in range(2):
                    s = 2 * m + hf
                    half(i * ROUND + (base + s), s, bank, hf, xa, xb)
                    if after is not None:
                        after(hf)

            pe.wait_ge(xblk_evac, 14)
            pe.wait_ge(relu_ready, IH)
            for t in range(NH + 4):
                j = t - 1
                if 0 <= j < NH:
                    s = j % 2
                    pe.wait_ge(qkt_ready, j + 1)
                    if j >= 2:
                        pe.wait_ge(s_ready, j - 1)
                    mm(ps[4 * s + 1][:, 0:128], QKT[:, s, 0:128], QKT[:, s, 256:384], start=True, stop=True)
                    mm(ps[4 * s + 1][:, 128:384], QKT[:, s, 128:256], QKT[:, s, 256:512], start=True,
                       stop=True).then_inc(s_mm, 1)
                if t < NH:
                    if t % 4 == 0:
                        pe.wait_ge(qk_normed, (3, 4, 7, 8)[t // 4])
                    if t >= 2:
                        pe.wait_ge(qkt_ready, t - 1)
                    g0, hh = (0, t) if t < 8 else (2, t - 8)
                    for g in range(2):
                        for tt in range(TT):
                            off = O_QK + 2048 * (g0 + g) + tt * 1024 + hh * HD
                            ins = nc.tensor.transpose(ps[4 * (t % 2)][:, (2 * g + tt) * P:(2 * g + tt + 1) * P],
                                                      big[:, off:off + HD], IDENT[:, :])
                    ins.then_inc(qk_tr, 1)
                j = t - 3
                if j == 0:
                    pe.wait_ge(tile0_evac, 1)
                if 0 <= j < NH:
                    s = j % 2
                    pe.wait_ge(p_ready, j + 1)
                    if j >= 2:
                        pe.wait_ge(pt_ready, j - 1)
                    for c in range(3):
                        ins = nc.tensor.transpose(ps[4 * s + 2][:, c * P:(c + 1) * P], PR_[:, s, c * P:(c + 1) * P], IDENT[:, :])
                    ins.then_inc(pt_tr, 1)
                j = t - 4
                if 0 <= j < NH:
                    s = j % 2
                    v = V_[0] if j < 8 else V_[8]
                    hh = j % 8
                    pe.wait_ge(pt_ready, j + 1)
                    if j == 0:
                        pe.wait_ge(xblk_evac, 15)
                    if j >= 2:
                        pe.wait_ge(o2_ready, j - 1)
                    mm(ps[4 * s + 3][:, 0:256], v[:, 0, hh * HD:(hh + 1) * HD], PT_[:, s, 0:256], start=True, stop=False)
                    mm(ps[4 * s + 3][:, 128:256], v[:, 1, hh * HD:(hh + 1) * HD], PT_[:, s, 256:384], start=False,
                       stop=True).then_inc(o_mm, 1)
                if t >= NH:
                    m = t - NH
                    pe.wait_ge((qkt_ready, s_ready, pt_ready, o2_ready)[m], NH - 1)
                    pe.wait_ge(o2_ready, 8)
                    half(B_OUT + m, m, m, 0, X1, X2)

            pe.wait_ge(o2_ready, NH)
            for m in range(4):
                half(B_OUT + 4 + m, 4 + m, m, 1, X1, X2)
            with pe.Fori(1, N_OUT // ROUND) as i:
                for m in range(4):
                    pe.wait_ge(h_ready, i * 4 + (m - 3))
                    half(i * ROUND + (B_OUT + m), m, m, 0, X1, X2)
                for m in range(4):
                    half(i * ROUND + (B_OUT + 4 + m), 4 + m, m, 1, X1, X2)

            def first_round_half(base, n, chunks, bank_free):
                if n < 4:
                    bank_free(n)
                half(base + n, n, n % 4, n // 4, X1, X2, chunks if n % 4 == 0 else None)

            def sum_squares(bank, src):
                for tt in range(TT):
                    ins = mm(ps[bank][:, tt:tt + 1], src[:, tt * P:(tt + 1) * P], ONES[:, 0:1], start=True, stop=True)
                ins.then_inc(ss_mm, 1)

            def spread(which):
                pe.wait_ge(diag_ready, which)
                mm(ps[7][:, 0:T], ONES[:, :], TMP[:, 0, :], start=True, stop=True).then_inc(bc_mm, 1)

            def subkey_products(i, m):
                pe.wait_ge(q_ready, i * 4 + (m + 1))
                for tt in range(TT):
                    ins = mm(ps[4 + m][:, tt * P:(tt + 1) * P], QT[:, m, tt * P:(tt + 1) * P], SUBK[:, m % 2, :],
                             start=True, stop=True)
                ins.then_inc(sk_mm, 1)

            for n in range(ROUND):
                first_round_half(B_QUERY, n, KC, lambda m: pe.wait_ge(h_ready, KC - 3 + m))
                if n == 1:
                    pe.wait_ge(sq_done, 1)
                    sum_squares(6, SQACC)
                if n == 3:
                    spread(1)
            pe.wait_ge(subk_loaded, 16)
            pe.wait_ge(rstdb_ready, 1)
            for m in range(4):
                subkey_products(0, m)
            with pe.Fori(1, N_QUERY // ROUND) as i:
                for m in range(4):
                    pe.wait_ge(q_ready, i * 4 + (m - 3))
                    half(i * ROUND + (B_QUERY + m), m, m, 0, X1, X2)
                for m in range(4):
                    half(i * ROUND + (B_QUERY + 4 + m), 4 + m, m, 1, X1, X2)
                pe.wait_ge(sall_ready, i * 4)
                for m in range(4):
                    subkey_products(i, m)

            def gates(group, bank, hf):
                pe.wait_ge(oha_ready, group * 2 + (hf + 1))
                pe.wait_ge(ohb_ready, group * 2 + (hf + 1))
                for q in range(2):
                    o = (2 * hf + q) * P
                    ins = mm(ps[bank][:, o:o + P], OHB[:, q, :], OHA[:, q, :], start=True, stop=True)
                ins.then_inc(g_mm, 1)

            for n in range(ROUND):
                first_round_half(B_U, n, 2 * KC, lambda m: pe.wait_ge(q_ready, KC))
            with pe.Fori(1, R_GATE - 1) as i:
                for m in range(4):
                    pe.wait_ge(act_ready, i * 4 + (m - 3))
                    unit(i, B_U, m, m, X1, X2)
            for m in range(4):
                pe.wait_ge(act_ready, G_MUL - 7 + m)
                unit(R_GATE - 1, B_U, m, m, X1, X2, after=(lambda hf: gates(m - 2, 4 + m, hf)) if m >= 2 else None)
                if m == 0:
                    pe.wait_ge(tok_ready, 1)
                    for w in range(3):
                        for tt in range(TT):
                            ins = nc.tensor.transpose(ps[4 + w][:, tt * P:(tt + 1) * P], TOK[:, w, tt * P:(tt + 1) * P], IDENT[:, :])
                        ins.then_inc(tok_mm, 1)
            for m in range(4):
                pe.wait_ge(act_ready, G_MUL - 3 + m)
                if m >= 2:
                    pe.wait_ge(g_done, m - 1)
                unit(R_GATE, B_U, m, m, X1, X2, after=lambda hf: gates(m + G_AHEAD, 4 + m, hf))
            with pe.Fori(R_GATE + 1, N_U // ROUND) as i:
                for m in range(4):
                    group = i * 4 + (m + G_AHEAD - G_MUL)
                    pe.wait_ge(act_ready, i * 4 + (m - 3))
                    pe.wait_ge(g_done, group - 3)
                    unit(i, B_U, m, m, X1, X2, after=lambda hf: gates(group, 4 + m, hf))
            for g in range(NE1 - G_MUL + G_AHEAD, T // 4):
                pe.wait_ge(g_done, g - 3)
                for hf in range(2):
                    gates(g, 4 + (g - G_AHEAD) % 4, hf)

            def v_units(i, peeled):
                for m in range(4):
                    pe.wait_ge(c2_ready, i * 4 + (m + 1))
                    for hf in range(2):
                        s = 2 * m + hf
                        n = i * ROUND + (B_V + s)
                        pe.wait_ge(hi_ready, n + 1)
                        for j in range(8):
                            k = 8 * hf + j
                            dst = ps[k // 2][:, (k % 2) * T:(k % 2 + 1) * T]
                            mm(dst, WH[:, s % HI, j * P:(j + 1) * P], X1[:, m, :],
                               start=(peeled and m == 0 and k % 2 == 0), stop=False, skip_group_check=True)
                            mm(dst, WH[:, s % HI, j * P:(j + 1) * P], X2[:, m, :], start=False, stop=False,
                               skip_group_check=True)
                        pe.wait_ge(lo_ready, n + 1)
                        for j in range(8):
                            k = 8 * hf + j
                            ins = mm(ps[k // 2][:, (k % 2) * T:(k % 2 + 1) * T], WL[:, s % LO, j * P:(j + 1) * P], X1[:, m, :],
                                     start=False, stop=False, skip_group_check=True)
                        ins.then_inc(pe_done, 1)

            pe.wait_ge(g_done, T // 4)
            v_units(0, True)
            with pe.Fori(1, N_V // ROUND) as i:
                v_units(i, False)

            pe.wait_ge(p2_ready, 1)
            for u in range(ROUND):
                n = B_PROJ + u
                if u < 4:
                    pe.wait_ge(h3_ready, u + 1)
                else:
                    pe.wait_ge(proj_evac, u - 3)
                pe.wait_ge(lo_ready, n + 1)
                for q in range(2):
                    c = [slice((2 * q + kk) * P, (2 * q + kk + 1) * P) for kk in range(2)]
                    parts = [t for kk in range(2) for t in ((WH[:, u % HI, c[kk]], X1[:, PLE + kk, :]),
                                                            (WH[:, u % HI, c[kk]], X2[:, PLE + kk, :]),
                                                            (WL[:, u % LO, c[kk]], X1[:, PLE + kk, :]))]
                    for j, (a, b) in enumerate(parts):
                        ins = mm(ps[u % 4][:, q * T:(q + 1) * T], a, b, start=(j == 0), stop=(j == len(parts) - 1))
                ins.then_inc(pe_done, 1)
            for n in range(ROUND):
                first_round_half(B_GATE, n, 3 * KC, lambda m: pe.wait_ge(proj_evac, 5 + m))
                if n == 3:
                    pe.wait_ge(h3_ready, KC // 2)
                    pe.wait_ge(sq4_ready, 1)
                    for tt in range(TT):
                        for k in range(2):
                            ins = mm(ps[6][:, tt:tt + 1], SQ4[:, k, tt * P:(tt + 1) * P], ONES[:, 0:1],
                                     start=(k == 0), stop=(k == 1))
                    ins.then_inc(ss_mm, 1)
                if n == 5:
                    spread(2)
            for m in range(4, 16):
                pe.wait_ge(gtmp_ready, m - 3)
                unit(m // 4, B_GATE, m % 4, m % 4, X1, X2)


def kernel(x, p, positions, norm_mix, w_in, qk_norm_a, qk_norm_b, rel_bias, w_out, norm_ffn, peer_query,
           peer_sub_keys, peer_u, peer_v, norm_ple, ple_gate, ple_proj):
    import concourse.bacc as bacc
    from concourse.bass_utils import run_bass_kernel_spmd as run

    c = np.ascontiguousarray
    x, p, positions, w_in, w_out = (np.asarray(a) for a in (x, p, positions, w_in, w_out))
    w = w_in[0]
    A = 1024
    qa, ka, va, qb, kb, vb = (w[:, j * A:(j + 1) * A] for j in range(6))
    qi, ki, wi = w[:, 6 * A:7 * A], w[:, 7 * A:7 * A + IDIM], w[:, 7 * A + IDIM:]

    def chunks(a):
        return c(a.reshape(-1, P, a.shape[1]).transpose(1, 0, 2))

    def blocks(parts):
        a = np.concatenate(parts, axis=1).reshape(8, 2, P, -1, 512)
        return c(a.transpose(3, 0, 2, 1, 4).reshape(-1, P, HALF))

    def units(a):
        a = np.asarray(a).reshape(2, 8, P, -1, P)
        return c(a.transpose(3, 0, 2, 1, 4).reshape(-1, P, HALF))

    def halves_first(a):
        return c(units(a[0]).reshape(4, 4, 2, P, HALF).transpose(0, 2, 1, 3, 4).reshape(-1, P, HALF))

    def first_round(a):
        return np.concatenate([a[[0, 2, 4, 6, 1, 3, 5, 7]], a[8:]])

    small = np.concatenate([ki, ki, wi], axis=1).reshape(8, 2, P, SMALL).transpose(0, 2, 1, 3).reshape(8, P, 2 * SMALL)
    q = np.arange(P)[:, None]
    k0, k1 = np.arange(P)[None, :], np.arange(T)[None, :]
    dist = np.concatenate([np.clip(q - k0, -128, 128), np.clip(q + P - k1, -128, 128)], axis=1) + 128
    arrays = {
        "xT": chunks(x[0].T),
        "pT": chunks(p[0, 0].T),
        "pos": c(positions[0].reshape(TT, P).T),
        "norms": c(np.stack([np.asarray(g)[0].reshape(KC, P).T for g in (norm_mix, norm_ffn, norm_ple)], axis=1)),
        "head_gains": c(np.broadcast_to(np.concatenate([np.asarray(qk_norm_a)[0], np.asarray(qk_norm_b)[0]])[None],
                                        (P, 4, HD))),
        "bias_a": c(np.asarray(rel_bias)[0][:, dist].transpose(1, 0, 2)),
        "subkeys": c(np.asarray(peer_sub_keys)[0].transpose(2, 0, 1)),
        "w_small": c(small),
        "w_plain": blocks([qi, vb, va]),
        "w_qk": blocks([qa, ka, qb, kb]),
        "w_out": halves_first(w_out),
        "w_query": halves_first(peer_query),
        "w_u": first_round(np.asarray(peer_u)[0].reshape(NE1, P, 2, 8, P).transpose(0, 2, 4, 3, 1).reshape(2 * NE1, P, HALF)),
        "w_v": c(np.asarray(peer_v)[0].reshape(NE1, P, D)),
        "w_proj": c(np.asarray(ple_proj)[0].reshape(2, P, 8, 2, P).transpose(2, 1, 3, 0, 4).reshape(8, P, 512)),
        "w_gate": first_round(units(ple_gate[0])),
    }
    nc = bacc.Bacc("TRN2", target_bir_lowering=False, num_devices=1)
    args = [nc.dram_tensor(n, a.shape, mybir.dt.from_np(a.dtype), kind="ExternalInput").ap() for n, a in arrays.items()]
    out = nc.dram_tensor("out", (P, KC, T), F32, kind="ExternalOutput").ap()
    layer_kernel(nc, *args, out)
    r = run(nc, [arrays], core_ids=[0])
    return c(np.asarray(r.results[0]["out"]).transpose(1, 0, 2).reshape(D, T).T).reshape(1, T, D)
```
